# Optimizing a Trainium2 kernel written in Bass

```python
import math
import jax, jax.numpy as jnp
from jax import lax
import numpy as np

D_MODEL = 1024
BATCH = 1
SEQ = 1024
DEPTH = 2

MEM_LEN = 256
Q_BLOCK = 128
NSA_Q_BLOCK = 64
NEG_INF = -1e30
EPS = 1e-6
SEL_FORCE = 1e9

NUM_BUCKETS = 32
REL_MAX_DIST = 128
BIAS_HEADS = 8

MLA_HEADS = 8
MLA_Q_RANK = 256
MLA_KV_RANK = 128
MLA_NOPE = 64
MLA_ROPE = 32
MLA_V = 64
ROPE_BASE = 10000.0

SWA_HEADS = 8
SWA_KV_HEADS = 2
SWA_HEAD_DIM = 64
SWA_WINDOW = 128

NSA_HEADS = 8
NSA_KV_HEADS = 2
NSA_HEAD_DIM = 64
CMP_LEN = 32
CMP_STRIDE = 16
CMP_HIDDEN = 256
SEL_LEN = 64
SEL_TOP_N = 16
NSA_WINDOW = 512

MEM_HEADS = 4
MEM_HEAD_DIM = 128

MLA_W = MLA_HEADS * MLA_V
SWA_W = SWA_HEADS * SWA_HEAD_DIM
SWA_KV_W = SWA_KV_HEADS * SWA_HEAD_DIM
NSA_W = NSA_HEADS * NSA_HEAD_DIM
NSA_KV_W = NSA_KV_HEADS * NSA_HEAD_DIM
MEM_W = MEM_HEADS * MEM_HEAD_DIM

EVEN_SPLITS = (MLA_Q_RANK, MLA_KV_RANK, MLA_ROPE, MLA_W,
               SWA_W, SWA_KV_W, SWA_KV_W, SWA_W,
               MEM_W, MEM_W)
ODD_SPLITS = (NSA_W,
              NSA_KV_W, NSA_KV_W,
              NSA_KV_W, NSA_KV_W,
              NSA_KV_W, NSA_KV_W,
              NSA_HEADS * 3,
              NSA_W,
              MEM_W, MEM_W)
EVEN_IN = sum(EVEN_SPLITS)
ODD_IN = sum(ODD_SPLITS)
EVEN_OUT = MLA_W + SWA_W + MEM_W
ODD_OUT = NSA_W + MEM_W
N_EVEN = (DEPTH + 1) // 2
N_ODD = DEPTH // 2

kernel_name = "hybrid_mla_swa_nsa_memory_trunk"

def split_cols(x, sizes):
    cuts = [int(c) for c in np.cumsum(sizes)[:-1]]
    return jnp.split(x, cuts, axis=-1)

def rms_norm(x, g):
    xf = x.astype(jnp.float32)
    y = xf * lax.rsqrt(jnp.mean(jnp.square(xf), axis=-1, keepdims=True) + EPS)
    return (y * g.astype(jnp.float32)).astype(x.dtype)

def rope(x, pos):
    half = x.shape[-1] // 2
    inv = ROPE_BASE ** (-jnp.arange(half, dtype=jnp.float32) / half)
    ang = pos.astype(jnp.float32)[:, None] * inv[None, :]
    cos = jnp.cos(ang)[None, :, None, :]
    sin = jnp.sin(ang)[None, :, None, :]
    x1 = x[..., :half].astype(jnp.float32)
    x2 = x[..., half:].astype(jnp.float32)
    return jnp.concatenate([x1 * cos - x2 * sin, x2 * cos + x1 * sin], axis=-1).astype(x.dtype)

def t5_bucket(dist):
    max_exact = NUM_BUCKETS // 2
    d = jnp.maximum(dist, 0)
    log_ratio = jnp.log(jnp.maximum(d, 1).astype(jnp.float32) / max_exact) / math.log(REL_MAX_DIST / max_exact)
    large = max_exact + (log_ratio * (NUM_BUCKETS - max_exact)).astype(jnp.int32)
    return jnp.where(d < max_exact, d, jnp.minimum(large, NUM_BUCKETS - 1))

def rel_bias(table, dist, n_groups):
    b = table.astype(jnp.float32)[t5_bucket(dist)]
    q, k, h = b.shape
    return jnp.transpose(b, (2, 0, 1)).reshape(n_groups, h // n_groups, q, k)

def masked_softmax(logits, mask, sink=None):
    logits = jnp.where(mask, logits, NEG_INF)
    m = jnp.max(logits, axis=-1, keepdims=True)
    if sink is not None:
        m = jnp.maximum(m, sink)
    p = jnp.where(mask, jnp.exp(logits - m), 0.0)
    denom = jnp.sum(p, axis=-1, keepdims=True)
    if sink is not None:
        denom = denom + jnp.exp(sink - m)
    return p / jnp.maximum(denom, 1e-30)

def sweep(fn, n_blocks):
    out = lax.map(fn, jnp.arange(n_blocks))
    out = jnp.moveaxis(out, 0, 1)
    return out.reshape(out.shape[0], -1, *out.shape[3:])

def mla_attention(c_q, c_kv, k_rope, pos, q_norm, kv_norm, w_uq, w_ukv):
    B, S, _ = c_q.shape
    q = (rms_norm(c_q, q_norm) @ w_uq).reshape(B, S, MLA_HEADS, MLA_NOPE + MLA_ROPE)
    q_nope = q[..., :MLA_NOPE]
    q_pe = rope(q[..., MLA_NOPE:], pos)
    kv = (rms_norm(c_kv, kv_norm) @ w_ukv).reshape(B, S, MLA_HEADS, MLA_NOPE + MLA_V)
    k_nope, v = kv[..., :MLA_NOPE], kv[..., MLA_NOPE:]
    k_pe = rope(k_rope[:, :, None, :], pos)[:, :, 0, :]
    scale = (MLA_NOPE + MLA_ROPE) ** -0.5
    k_idx = jnp.arange(S)

    def block(i):
        s0 = i * Q_BLOCK
        qn = lax.dynamic_slice_in_dim(q_nope, s0, Q_BLOCK, axis=1)
        qp = lax.dynamic_slice_in_dim(q_pe, s0, Q_BLOCK, axis=1)
        logits = (jnp.einsum('bqhd,bkhd->bhqk', qn, k_nope)
                  + jnp.einsum('bqhd,bkd->bhqk', qp, k_pe)).astype(jnp.float32) * scale
        mask = (s0 + jnp.arange(Q_BLOCK))[:, None] >= k_idx[None, :]
        p = masked_softmax(logits, mask)
        return jnp.einsum('bhqk,bkhd->bqhd', p.astype(v.dtype), v).reshape(B, Q_BLOCK, MLA_W)

    return sweep(block, S // Q_BLOCK)

def banded_attention(q, k, v, pos, table, window, sinks=None):
    B, S, H, d = q.shape
    G = k.shape[2]
    R = H // G
    pad = -(-(window - 1) // Q_BLOCK) * Q_BLOCK
    kl = pad + Q_BLOCK
    kp = jnp.pad(k, ((0, 0), (pad, 0), (0, 0), (0, 0)))
    vp = jnp.pad(v, ((0, 0), (pad, 0), (0, 0), (0, 0)))
    posp = jnp.pad(pos, (pad, 0))
    scale = d ** -0.5
    sink = None if sinks is None else sinks.astype(jnp.float32).reshape(G, R)[None, :, :, None, None]

    def block(i):
        s0 = i * Q_BLOCK
        qb = lax.dynamic_slice_in_dim(q, s0, Q_BLOCK, axis=1).reshape(B, Q_BLOCK, G, R, d)
        kb = lax.dynamic_slice_in_dim(kp, s0, kl, axis=1)
        vb = lax.dynamic_slice_in_dim(vp, s0, kl, axis=1)
        q_idx = s0 + jnp.arange(Q_BLOCK)
        k_idx = s0 - pad + jnp.arange(kl)
        delta = q_idx[:, None] - k_idx[None, :]
        mask = (k_idx[None, :] >= 0) & (delta >= 0) & (delta < window)
        dist = (lax.dynamic_slice_in_dim(pos, s0, Q_BLOCK)[:, None]
                - lax.dynamic_slice_in_dim(posp, s0, kl)[None, :])
        logits = (jnp.einsum('bqgrd,bkgd->bgrqk', qb, kb).astype(jnp.float32) * scale
                  + rel_bias(table, dist, G))
        p = masked_softmax(logits, mask, sink)
        return jnp.einsum('bgrqk,bkgd->bqgrd', p.astype(v.dtype), vb).reshape(B, Q_BLOCK, H * d)

    return sweep(block, S // Q_BLOCK)

def memory_attention(q, mem_n, w_mem_kv):
    B, S, _ = q.shape
    M = mem_n.shape[1]
    kv = mem_n @ w_mem_kv
    k = kv[..., :MEM_W].reshape(B, M, MEM_HEADS, MEM_HEAD_DIM)
    v = kv[..., MEM_W:].reshape(B, M, MEM_HEADS, MEM_HEAD_DIM)
    qh = q.reshape(B, S, MEM_HEADS, MEM_HEAD_DIM)
    logits = jnp.einsum('bshd,bmhd->bhsm', qh, k).astype(jnp.float32) * MEM_HEAD_DIM ** -0.5
    p = jax.nn.softmax(logits, axis=-1)
    return jnp.einsum('bhsm,bmhd->bshd', p.astype(v.dtype), v).reshape(B, S, MEM_W)

def compress_blocks(x, pos_emb, w1, w2):
    B, S, G, d = x.shape
    nc = (S - CMP_LEN) // CMP_STRIDE + 1
    idx = jnp.arange(nc)[:, None] * CMP_STRIDE + jnp.arange(CMP_LEN)[None, :]
    blk = x[:, idx] + pos_emb[None, None, :, None, :]
    flat = jnp.transpose(blk, (0, 1, 3, 2, 4)).reshape(B, nc, G, CMP_LEN * d)
    return jax.nn.silu(flat @ w1) @ w2

def nsa_compressed_selected(q, k_cmp, v_cmp, k_slc, v_slc, pos, table,
                            cmp_pos_k, cmp_pos_v, w1k, w2k, w1v, w2v):
    B, S, H, d = q.shape
    G = k_slc.shape[2]
    R = H // G
    scale = d ** -0.5
    kc = compress_blocks(k_cmp, cmp_pos_k, w1k, w2k)
    vc = compress_blocks(v_cmp, cmp_pos_v, w1v, w2v)
    nc = kc.shape[1]
    c_start = jnp.arange(nc) * CMP_STRIDE
    c_end = c_start + CMP_LEN - 1
    c_pos = pos[c_end]
    ns = S // SEL_LEN
    top_n = min(SEL_TOP_N, ns)
    s_start = jnp.arange(ns) * SEL_LEN
    overlap = jnp.maximum(jnp.minimum(c_start[:, None] + CMP_LEN, s_start[None, :] + SEL_LEN)
                          - jnp.maximum(c_start[:, None], s_start[None, :]), 0)
    cmp_to_sel = overlap.astype(jnp.float32) / CMP_LEN
    ks = k_slc.reshape(B, ns, SEL_LEN, G, d).transpose(0, 3, 1, 2, 4)
    vs = v_slc.reshape(B, ns, SEL_LEN, G, d).transpose(0, 3, 1, 2, 4)
    gather = jax.vmap(jax.vmap(lambda blocks, ids: blocks[ids]))
    tbl_g = table.astype(jnp.float32).reshape(NUM_BUCKETS, G, R).transpose(1, 0, 2)
    QB = NSA_Q_BLOCK
    KS = top_n * SEL_LEN

    def block(i):
        s0 = i * QB
        qb = lax.dynamic_slice_in_dim(q, s0, QB, axis=1).reshape(B, QB, G, R, d)
        q_idx = s0 + jnp.arange(QB)
        q_pos = lax.dynamic_slice_in_dim(pos, s0, QB)
        logits = (jnp.einsum('bqgrd,bcgd->bgrqc', qb, kc).astype(jnp.float32) * scale
                  + rel_bias(table, q_pos[:, None] - c_pos[None, :], G))
        p_cmp = masked_softmax(logits, c_end[None, :] <= q_idx[:, None])
        o_cmp = jnp.einsum('bgrqc,bcgd->bqgrd', p_cmp.astype(vc.dtype), vc).reshape(B, QB, H * d)
        imp = jnp.einsum('bgqc,cj->bgqj', jnp.sum(p_cmp, axis=2), cmp_to_sel)
        j = jnp.arange(ns)[None, :]
        cur = (q_idx // SEL_LEN)[:, None]
        forced = (j == 0) | (j == cur) | (j == cur - 1)
        causal = j * SEL_LEN <= q_idx[:, None]
        score = jnp.where(forced, SEL_FORCE, jnp.where(causal, imp, -SEL_FORCE))
        _, sel = lax.top_k(score, top_n)
        kg = gather(ks, sel)
        vg = gather(vs, sel).reshape(B, G, QB, KS, d)
        tok = sel[..., None] * SEL_LEN + jnp.arange(SEL_LEN)
        tmask = (tok <= q_idx[None, None, :, None, None]).reshape(B, G, 1, QB, KS)
        bucket = t5_bucket(q_pos[None, None, :, None, None] - pos[tok])
        bias = tbl_g[jnp.arange(G)[None, :, None, None, None], bucket]
        bias = jnp.moveaxis(bias, -1, 2).reshape(B, G, R, QB, KS)
        logits = (jnp.einsum('bqgrd,bgqnld->bgrqnl', qb, kg).reshape(B, G, R, QB, KS).astype(jnp.float32)
                  * scale + bias)
        p_slc = masked_softmax(logits, tmask)
        o_slc = jnp.einsum('bgrqk,bgqkd->bqgrd', p_slc.astype(vg.dtype), vg).reshape(B, QB, H * d)
        return jnp.concatenate([o_cmp, o_slc], axis=-1)

    out = sweep(block, S // QB)
    return out[..., :H * d], out[..., H * d:]

def even_layer(h, mem_n, pos, table, w_in, q_norm, kv_norm, w_uq, w_ukv, sinks, w_mem_kv, w_out):
    B, S, _ = h.shape
    (c_q, c_kv, k_rope, g_mla, q_swa, k_swa, v_swa, g_swa,
     q_mem, g_mem) = split_cols(h @ w_in, EVEN_SPLITS)
    o_mla = mla_attention(c_q, c_kv, k_rope, pos, q_norm, kv_norm, w_uq, w_ukv) * jax.nn.silu(g_mla)
    o_swa = banded_attention(q_swa.reshape(B, S, SWA_HEADS, SWA_HEAD_DIM),
                             k_swa.reshape(B, S, SWA_KV_HEADS, SWA_HEAD_DIM),
                             v_swa.reshape(B, S, SWA_KV_HEADS, SWA_HEAD_DIM),
                             pos, table, SWA_WINDOW, sinks) * jax.nn.silu(g_swa)
    o_mem = memory_attention(q_mem, mem_n, w_mem_kv) * jax.nn.silu(g_mem)
    return jnp.concatenate([o_mla, o_swa, o_mem], axis=-1) @ w_out

def odd_layer(h, mem_n, pos, table, w_in, cmp_pos_k, cmp_pos_v, w1k, w2k, w1v, w2v, w_mem_kv, w_out):
    B, S, _ = h.shape
    (q, k_cmp, v_cmp, k_slc, v_slc, k_win, v_win, g_logit, g_nsa,
     q_mem, g_mem) = split_cols(h @ w_in, ODD_SPLITS)
    qh = q.reshape(B, S, NSA_HEADS, NSA_HEAD_DIM)
    kvh = lambda t: t.reshape(B, S, NSA_KV_HEADS, NSA_HEAD_DIM)
    o_cmp, o_slc = nsa_compressed_selected(qh, kvh(k_cmp), kvh(v_cmp), kvh(k_slc), kvh(v_slc), pos, table,
                                           cmp_pos_k, cmp_pos_v, w1k, w2k, w1v, w2v)
    o_win = banded_attention(qh, kvh(k_win), kvh(v_win), pos, table, NSA_WINDOW)
    g = jax.nn.sigmoid(g_logit.astype(jnp.float32)).reshape(B, S, NSA_HEADS, 3, 1).astype(h.dtype)
    per_head = lambda o: o.reshape(B, S, NSA_HEADS, NSA_HEAD_DIM)
    o_nsa = (g[..., 0, :] * per_head(o_cmp) + g[..., 1, :] * per_head(o_slc)
             + g[..., 2, :] * per_head(o_win)).reshape(B, S, NSA_W) * jax.nn.silu(g_nsa)
    o_mem = memory_attention(q_mem, mem_n, w_mem_kv) * jax.nn.silu(g_mem)
    return jnp.concatenate([o_nsa, o_mem], axis=-1) @ w_out

def setup_inputs(seed: int = 0) -> dict:
    key = jax.random.key(seed)
    ks = jax.random.split(key, 24)
    f32 = jnp.float32

    def nrm(k, shape, scale):
        return jax.random.normal(k, shape, f32) * scale

    def gain(k, shape):
        return 1.0 + 0.1 * jax.random.normal(k, shape, f32)

    offset = jax.random.randint(ks[2], (), 0, 1024, dtype=jnp.int32)
    d = NSA_HEAD_DIM
    return {
        "x": nrm(ks[0], (BATCH, SEQ, D_MODEL), 1.0),
        "mem": nrm(ks[1], (BATCH, MEM_LEN, D_MODEL), 1.0),
        "positions": offset + jnp.arange(SEQ, dtype=jnp.int32),
        "rel_bias_table": nrm(ks[3], (NUM_BUCKETS, BIAS_HEADS), 0.5),
        "norm_pre": gain(ks[4], (DEPTH, D_MODEL)),
        "norm_post": gain(ks[5], (DEPTH, D_MODEL)),
        "mem_norm": gain(ks[6], (DEPTH, D_MODEL)),
        "w_mem_kv": nrm(ks[7], (DEPTH, D_MODEL, 2 * MEM_W), D_MODEL ** -0.5),
        "w_in_even": nrm(ks[8], (N_EVEN, D_MODEL, EVEN_IN), D_MODEL ** -0.5),
        "mla_q_norm": gain(ks[9], (N_EVEN, MLA_Q_RANK)),
        "mla_kv_norm": gain(ks[10], (N_EVEN, MLA_KV_RANK)),
        "mla_w_uq": nrm(ks[11], (N_EVEN, MLA_Q_RANK, MLA_HEADS * (MLA_NOPE + MLA_ROPE)), MLA_Q_RANK ** -0.5),
        "mla_w_ukv": nrm(ks[12], (N_EVEN, MLA_KV_RANK, MLA_HEADS * (MLA_NOPE + MLA_V)), MLA_KV_RANK ** -0.5),
        "swa_sinks": nrm(ks[13], (N_EVEN, SWA_HEADS), 1.0),
        "w_out_even": nrm(ks[14], (N_EVEN, EVEN_OUT, D_MODEL), EVEN_OUT ** -0.5),
        "w_in_odd": nrm(ks[15], (N_ODD, D_MODEL, ODD_IN), D_MODEL ** -0.5),
        "cmp_pos_k": nrm(ks[16], (N_ODD, CMP_LEN, d), 0.1),
        "cmp_pos_v": nrm(ks[17], (N_ODD, CMP_LEN, d), 0.1),
        "cmp_w1_k": nrm(ks[18], (N_ODD, CMP_LEN * d, CMP_HIDDEN), (CMP_LEN * d) ** -0.5),
        "cmp_w2_k": nrm(ks[19], (N_ODD, CMP_HIDDEN, d), CMP_HIDDEN ** -0.5),
        "cmp_w1_v": nrm(ks[20], (N_ODD, CMP_LEN * d, CMP_HIDDEN), (CMP_LEN * d) ** -0.5),
        "cmp_w2_v": nrm(ks[21], (N_ODD, CMP_HIDDEN, d), CMP_HIDDEN ** -0.5),
        "w_out_odd": nrm(ks[22], (N_ODD, ODD_OUT, D_MODEL), ODD_OUT ** -0.5),
    }

def reference(x, mem, positions, rel_bias_table, norm_pre, norm_post, mem_norm, w_mem_kv,
              w_in_even, mla_q_norm, mla_kv_norm, mla_w_uq, mla_w_ukv, swa_sinks, w_out_even,
              w_in_odd, cmp_pos_k, cmp_pos_v, cmp_w1_k, cmp_w2_k, cmp_w1_v, cmp_w2_v, w_out_odd):
    for l in range(DEPTH):
        h = rms_norm(x, norm_pre[l])
        mem_n = rms_norm(mem, mem_norm[l])
        if l % 2 == 0:
            e = l // 2
            y = even_layer(h, mem_n, positions, rel_bias_table, w_in_even[e], mla_q_norm[e],
                           mla_kv_norm[e], mla_w_uq[e], mla_w_ukv[e], swa_sinks[e], w_mem_kv[l],
                           w_out_even[e])
        else:
            o = l // 2
            y = odd_layer(h, mem_n, positions, rel_bias_table, w_in_odd[o], cmp_pos_k[o], cmp_pos_v[o],
                          cmp_w1_k[o], cmp_w2_k[o], cmp_w1_v[o], cmp_w2_v[o], w_mem_kv[l], w_out_odd[o])
        x = x + rms_norm(y, norm_post[l])
    return x


_drawn_inputs = setup_inputs


def setup_inputs(seed=0):
    import zlib

    import numpy as np

    out = dict(_drawn_inputs(seed))
    spreads = {}
    factors = {'swa_sinks': 6.649, 'cmp_pos_k': 8.0}
    for name, (base, spread) in spreads.items():
        noise = np.random.default_rng([zlib.crc32(name.encode()), seed]).standard_normal(out[name].shape)
        drawn = base * np.exp(spread * noise) if base else spread * noise
        out[name] = __import__('jax').numpy.asarray(drawn.astype(out[name].dtype))
    for name, factor in factors.items():
        out[name] = (out[name] * factor).astype(out[name].dtype)
    return out
```

```python
import math
from contextlib import ExitStack

import numpy as np

import concourse.bass as bass
import concourse.mybir as mybir

F32 = mybir.dt.float32
I32 = mybir.dt.int32
ALU = mybir.AluOpType
ACT = mybir.ActivationFunctionType
AX = mybir.AxisListType

P = 128
SEQ = 1024
D = 1024
MEM = 256
KT = D // P
QB = SEQ // P
HALF = 512
HD = 64
HEADS = 8
PAIRS = HEADS // 2
NB = 32
BIG = 1e30
EPS = 1e-6

C_ID = 0
C_CAUSAL = 128
C_WIN = 256
C_ONES = 384
C_INV = 512
C_SIGN = 513
C_NTHR = 514
C_BKT = C_NTHR + NB
C_EPS = C_BKT + NB
N_CONST = C_EPS + 1

E_CQ, E_CKV, E_KR, E_GMLA, E_QSWA, E_KSWA, E_VSWA, E_GSWA, E_QMEM, E_GMEM = (
    0, 256, 384, 416, 928, 1440, 1568, 1696, 2208, 2720)
(O_Q, O_KCMP, O_VCMP, O_KSLC, O_VSLC, O_KWIN, O_VWIN, O_GL, O_GNSA, O_QMEM, O_GMEM) = (
    0, 512, 640, 768, 896, 1024, 1152, 1280, 1304, 1816, 2328)
NOPE, ROPE = 64, 32
CMP_L, CMP_S = 32, 16
NC = (SEQ - CMP_L) // CMP_S + 1
LOOK = 2


def make_constants():
    c = np.zeros((P, N_CONST), np.float32)
    q, k = np.arange(P)[:, None], np.arange(P)[None, :]
    c[:, C_ID:C_ID + P] = np.eye(P)
    c[:, C_CAUSAL:C_CAUSAL + P] = np.where(k <= q, 0, BIG)
    c[:, C_WIN:C_WIN + P] = np.where(k > q, 0, BIG)
    c[:, C_ONES:C_ONES + P] = 1
    half = ROPE // 2
    inv = np.float32(10000.0) ** (-np.arange(half, dtype=np.float32) / np.float32(half))
    c[:, C_INV] = inv[np.arange(P) % half]
    c[:, C_SIGN] = np.where(np.arange(P) % ROPE < half, -1, 1)
    d = np.arange(1, 256, dtype=np.float32)
    ratio = np.log(d / np.float32(16)).astype(np.float32) / np.float32(math.log(8))
    bucket = np.where(d < 16, d, np.minimum(16 + (ratio * 16).astype(np.int32), NB - 1)).astype(int)
    for b in range(1, NB):
        c[:, C_NTHR + b] = -d[np.argmax(bucket >= b)]
    c[:, C_BKT:C_BKT + NB] = np.arange(NB)
    c[:, C_EPS] = EPS
    return c


def trunk(nc, a):
    ctx = ExitStack()

    def sb(name, width, dt=F32):
        return ctx.enter_context(nc.sbuf_tensor(name, [P, width], dt))

    layer_sems = []

    def sem(name):
        layer_sems.append(nc.alloc_semaphore(name))
        return layer_sems[-1]

    consts = sb("consts", N_CONST)
    ident = consts[:, C_ID:C_ID + P]
    causal = consts[:, C_CAUSAL:C_CAUSAL + P]
    winmask = consts[:, C_WIN:C_WIN + P]
    ones = consts[:, C_ONES:C_ONES + P]
    table = sb("table", NB * HEADS)
    hT_t = sb("hT", KT * SEQ)
    hT = hT_t[:, :].rearrange("p (k t) -> p k t", k=KT)
    oT_t = sb("oT", 12 * SEQ)
    oT = oT_t[:, :].rearrange("p (k t) -> p k t", k=12)
    wsl_t = sb("w_slots", 4 * KT * P)
    wsl = wsl_t[:, :].rearrange("p (s k n) -> p s k n", s=4, k=KT)
    gains = sb("gains", 64)
    band = sb("band", HEADS * 256)
    small = sb("small", 256)
    gen_f = small[:, 250:251]
    wait_marks = small[0:1, 60:160]
    gen_i = sb("gen_i", 1, I32)
    work = sb("work", 24500)
    PS = ctx.enter_context(nc.psum_tensor("PS", [P, 8, HALF], F32))

    def carve(*widths):
        at, out = 0, []
        for w in widths:
            out.append(work[:, at:at + w])
            at += w
        assert at <= 24500, at
        return out

    x1_dram = nc.dram_tensor("x1_scratch", (SEQ, D), F32, kind="Internal").ap()
    memT1_dram = nc.dram_tensor("memT1_scratch", (P, KT * MEM), F32, kind="Internal").ap()

    eng_pe, eng_act, eng_dve = nc.tensor, nc.scalar, nc.vector

    def norm_stage():
        NT = QB + MEM // P
        xs, sq, memT_w, memT1_w = carve(NT * D, D, KT * MEM, KT * MEM)
        xs = xs.rearrange("p (t d) -> p t d", t=NT)
        memT = memT_w.rearrange("p (k t) -> p k t", k=KT)
        memT1 = memT1_w.rearrange("p (k t) -> p k t", k=KT)
        stat, rstd = small[:, 0:NT], small[:, 16:16 + NT]
        names = ("x", "const", "gain", "sq", "var", "rt", "xn", "tr", "ev_act", "ev_dve", "m1", "m1_out")
        (x_in, const_in, gain_in, sq_done, var_done, rt_done, xn_done, tr_done, ev_act, ev_dve, m1_done, m1_out) = (sem("n_" + n) for n in names)
        x_in = [sem(f"n_x{t}") for t in range(NT)]
        with nc.Block() as block:
            @block.sync
            def _(sp):
                for t in range(NT):
                    src = a["x"][t * P:(t + 1) * P, :] if t < QB else a["mem"][(t - QB) * P:(t - QB + 1) * P, :]
                    sp.dma_start(xs[:, t, :], src).then_inc(x_in[t], 16)
                    if t == 0:
                        sp.dma_start(consts[:, :], a["const_tables"]).then_inc(const_in, 16)
                with nc.allow_non_contiguous_dma(reason="gains, one per partition"):
                    for g, src in ((0, a["norm_pre"][0]), (8, a["mem_norm"][0]), (24, a["mem_norm"][1]), (32, a["norm_pre"][1])):
                        sp.dma_start(gains[:, g:g + KT], src.rearrange("(k p) -> p k", p=P)).then_inc(gain_in, 16)
                sp.dma_start(table[:, :], a["rel_bias_table"].rearrange("b h -> (b h)").partition_broadcast(P)).then_inc(const_in, 16)
                sp.wait_ge(const_in, 32)
                sp.wait_ge(m1_done, 1)
                sp.dma_start(memT1_dram, memT1_w).then_inc(m1_out, 16)
                sp.wait_ge(m1_out, 16)

            @block.scalar
            def _(act):
                def root(t):
                    act.wait_ge(var_done, t + 1)
                    nc.scalar.activation(rstd[:, t:t + 1], stat[:, t:t + 1], ACT.Sqrt).then_inc(rt_done, 1)

                def copy(t):
                    act.wait_ge(tr_done, 2 * t + 1)
                    b = 2 * (t % 4)
                    for k in range(4):
                        ins = nc.scalar.activation(hT[:, k, t * P:(t + 1) * P], PS[:, b, k * P:(k + 1) * P], ACT.Copy, scale=gains[:, k:k + 1])
                    ins.then_inc(ev_act, 1)

                for t in range(NT):
                    act.wait_ge(x_in[t], 16)
                    if t:
                        act.wait_ge(sq_done, t)
                    nc.scalar.activation(sq, xs[:, t, :], ACT.Square, accum_out=stat[:, t:t + 1]).then_inc(sq_done, 1)
                    if t >= 1:
                        root(t - 1)
                    if t == 3:
                        act.wait_ge(gain_in, 64)
                    if t >= 3:
                        copy(t - 3)
                root(NT - 1)
                for t in range(NT - 3, QB):
                    copy(t)

            @block.vector
            def _(dve):
                def scale(t):
                    dve.wait_ge(rt_done, t + 1)
                    nc.vector.tensor_scalar(xs[:, t, :], xs[:, t, :], rstd[:, t:t + 1], None, ALU.mult).then_inc(xn_done, 1)

                def copy(t):
                    wide = lambda g: gains[:, g + 4:g + 8].unsqueeze(2).to_broadcast([P, 4, P])
                    if t < QB:
                        dve.wait_ge(tr_done, 2 * t + 2)
                        nc.vector.tensor_tensor(hT[:, 4:8, t * P:(t + 1) * P], PS[:, 2 * (t % 4) + 1, :].rearrange("p (k n) -> p k n", k=4),
                                                wide(0), ALU.mult).then_inc(ev_dve, 1)
                        return
                    cs = slice((t - QB) * P, (t - QB + 1) * P)
                    for h in range(2):
                        dve.wait_ge(tr_done, 2 * t + h + 1)
                        src = PS[:, 2 * (t % 4) + h, :].rearrange("p (k n) -> p k n", k=4)
                        for dst, g in ((memT, 8), (memT1, 24)):
                            ins = nc.vector.tensor_tensor(dst[:, 4 * h:4 * h + 4, cs], src,
                                                          gains[:, g + 4 * h:g + 4 * h + 4].unsqueeze(2).to_broadcast([P, 4, P]), ALU.mult)
                    ins.then_inc(ev_dve, 1)

                for t in range(NT):
                    st = stat[:, t:t + 1]
                    dve.wait_ge(sq_done, t + 1)
                    nc.vector.tensor_scalar(st, st, 1.0 / D, EPS, ALU.mult, ALU.add)
                    dve.drain()
                    nc.vector.reciprocal(st, st).then_inc(var_done, 1)
                    if t >= 1:
                        scale(t - 1)
                    if t == 3:
                        dve.wait_ge(gain_in, 64)
                    if t >= 3:
                        copy(t - 3)
                scale(NT - 1)
                for t in range(NT - 3, NT):
                    copy(t)
                dve.drain().then_inc(m1_done, 1)

            @block.tensor
            def _(pe):
                pe.wait_ge(const_in, 16)
                for t in range(NT):
                    pe.wait_ge(xn_done, t + 1)
                    if t >= 4:
                        pe.wait_ge(ev_act, t - 3)
                        pe.wait_ge(ev_dve, t - 3)
                    for k in range(KT):
                        ins = nc.tensor.transpose(PS[:, 2 * (t % 4) + k // 4, (k % 4) * P:(k % 4 + 1) * P],
                                                  xs[:, t, k * P:(k + 1) * P], ident)
                        if k % 4 == 3:
                            ins.then_inc(tr_done, 1)
        return memT

    def project_stage(tag, jobs, memT, dve_side, sp_side, mem_in=None, pool_side=None):
        w_in = [sem(f"{tag}w_in{s}") for s in range(4)]
        pe_done, ev_done = sem(tag + "pe"), sem(tag + "ev")
        slot_of, used, where = [], [], {}
        for n, (loads, _, _) in enumerate(jobs):
            slot_of.append(len(used) % 4 if loads else None)
            if loads:
                used.append(n)
        with nc.Block() as block:
            @block.sync
            def _(sp):
                sp_side(sp)
                for m, n in enumerate(used):
                    if m >= 4:
                        sp.wait_ge(pe_done, used[m - 4] + 1)
                    for dst, src in jobs[n][0](wsl[:, m % 4]):
                        sp.dma_start(dst, src).then_inc(w_in[m % 4], 16)

            @block.tensor
            def _(pe):
                loaded = [0] * 4
                for n, (loads, kind, _) in enumerate(jobs):
                    if n >= 2:
                        pe.wait_ge(ev_done, n - 1)
                    b = 2 * (n % 2)
                    if loads:
                        m = slot_of[n]
                        w = wsl[:, m]
                        loaded[m] += 16 * len(loads(w))
                        pe.wait_ge(w_in[m], loaded[m])
                    if mem_in is not None and not callable(kind) and kind[:3] == "mem" and not any(
                            not callable(j[1]) and j[1][:3] == "mem" for j in jobs[:n]):
                        pe.wait_ge(mem_in, 16)
                    if callable(kind):
                        ins = kind(pe, b)
                    elif kind == "feat":
                        for c in range(2):
                            for k in range(KT):
                                ins = nc.tensor.matmul(PS[:, b + c, :], w[:, k, :], hT[:, k, c * HALF:(c + 1) * HALF],
                                                       start=k == 0, stop=k == KT - 1)
                    elif kind.startswith("tok"):
                        width = int(kind[3:] or P)
                        for t in range(QB):
                            for k in range(KT):
                                ins = nc.tensor.matmul(PS[:, b + t // 4, (t % 4) * P:(t % 4) * P + width],
                                                       hT[:, k, t * P:(t + 1) * P], w[:, k, 0:width],
                                                       start=k == 0, stop=k == KT - 1)
                    elif kind == "memk":
                        for k in range(KT):
                            ins = nc.tensor.matmul(PS[:, b, 0:MEM], w[:, k, :], memT[:, k, :],
                                                   start=k == 0, stop=k == KT - 1)
                    else:
                        for t in range(MEM // P):
                            for k in range(KT):
                                ins = nc.tensor.matmul(PS[:, b, t * P:(t + 1) * P], memT[:, k, t * P:(t + 1) * P],
                                                       w[:, k, :], start=k == 0, stop=k == KT - 1)
                    ins.then_inc(pe_done, 1)

            @block.scalar
            def _(act):
                for n, (_, kind, evac) in enumerate(jobs):
                    act.wait_ge(pe_done, n + 1)
                    evac(act, PS[:, 2 * (n % 2):2 * (n % 2) + 2, :]).then_inc(ev_done, 1)

            @block.vector
            def _(dve):
                dve_side(dve)

            if pool_side:
                @block.gpsimd
                def _(pool):
                    pool_side(pool)

    def cols(w, *runs):
        v = w.rearrange("(k p) n -> p k n", p=P)
        return lambda slot: [(slot[:, :, s:s + n], v[:, :, c:c + n]) for s, c, n in runs]

    def copy_out(dst):
        return lambda act, ps: nc.scalar.activation(dst, ps, ACT.Copy)

    def flat2(view):
        return view.rearrange("p (c n) -> p c n", c=2)

    def position_rows(dve, pos_row, pos_col, row_hi, row_lo, col_hi, col_lo, tmp):
        for src, hi, lo, t in ((pos_row, row_hi, row_lo, tmp), (pos_col, col_hi, col_lo, tmp[:, 0:QB])):
            nc.vector.tensor_scalar(t, src, 16, None, ALU.arith_shift_right)
            dve.drain()
            nc.vector.tensor_copy(hi, t)
            dve.drain()
            nc.vector.tensor_scalar(t, src, 65535, None, ALU.bitwise_and)
            dve.drain()
            nc.vector.tensor_copy(lo, t)
            dve.drain()

    def bias_block(dve, rows, qb, k0, width, dsts, heads, scratch, loop):
        row_hi, row_lo, col_hi, col_lo = rows
        diff, bkt, hot = (s[:, 0:width] for s in scratch)
        ks = slice(k0, k0 + width)
        nc.vector.tensor_scalar(diff, row_hi[:, ks], col_hi[:, qb:qb + 1], 65536.0, ALU.subtract, ALU.mult)
        nc.vector.memset(bkt, 0.0)
        dve.drain()
        nc.vector.scalar_tensor_tensor(out=diff, in0=row_lo[:, ks], scalar=col_lo[:, qb:qb + 1], in1=diff,
                                       op0=ALU.subtract, op1=ALU.add)
        dve.drain()

        def raise_bucket(thr):
            nc.vector.scalar_tensor_tensor(out=bkt, in0=diff, scalar=thr, in1=bkt, op0=ALU.is_le, op1=ALU.add)
            dve.drain()

        def pick(col, entry):
            nc.vector.tensor_scalar(hot, bkt, col, -1.0, ALU.is_equal, ALU.mult)
            dve.drain()
            for d, e in zip(dsts, entry):
                nc.vector.scalar_tensor_tensor(out=d, in0=hot, scalar=e, in1=d, op0=ALU.mult, op1=ALU.add)
            dve.drain()

        for d in dsts:
            nc.vector.memset(d, 0.0)
        dve.drain()
        if loop:
            with dve.Fori(1, NB) as b:
                raise_bucket(consts[:, bass.ds(b + C_NTHR, 1)])
            with dve.Fori(0, NB) as b:
                pick(consts[:, bass.ds(b + C_BKT, 1)], [table[:, bass.ds(b * HEADS + h, 1)] for h in heads])
        else:
            for b in range(1, NB):
                raise_bucket(consts[:, C_NTHR + b:C_NTHR + b + 1])
            for b in range(NB):
                pick(consts[:, C_BKT + b:C_BKT + b + 1], [table[:, b * HEADS + h:b * HEADS + h + 1] for h in heads])

    def add_to(dst, mask):
        nc.vector.tensor_tensor(dst, dst, mask, ALU.add)

    LOG, TP, OB, FILL, FILL_GAP = 0, 4, 5, 7, 1

    def attention_stage(tag, tracks, loads, proj_jobs=(), setup_dve=None, head_dve=None, stage_pool=None):
        units, at, owner, fins, col = [], 0, [None] * 4, 0, 0
        for qb in range(QB):
            for tr in tracks:
                for hf in range(tr["halves"]):
                    ulist = tr["parts"](qb)
                    f_cols = {}
                    for kind in tr["kinds"]:
                        f_cols[kind] = col
                        col += 1
                    for un, plist in enumerate(ulist):
                        total = sum(n for _, n in plist)
                        banks = 2 if total > HALF else 1
                        if "bank_of" in tr:
                            at = tr["bank_of"](qb, hf)
                        if banks == 2 and at % 2:
                            at = (at + 1) % 4
                        prev = max((owner[b] for b in range(at, at + banks) if owner[b] is not None), default=None)
                        for b in range(at, at + banks):
                            owner[b] = len(units)
                        parts, off = [], 0
                        for kind, n in plist:
                            parts.append(dict(kind=kind, n=n, off=off, qb=qb, hf=hf, col=f_cols[kind],
                                              slot=tr["kinds"].index(kind)))
                            off += n
                        units.append(dict(tr=tr, qb=qb, hf=hf, parts=parts, bank=at, banks=banks, prev=prev, total=total,
                                          fin=fins if un == len(ulist) - 1 else None, f=fins, c0=col - len(tr["kinds"])))
                        at = (at + banks) % 4
                    fins += 1
        NU, NF, NCOL = len(units), fins, col
        g = 0
        for u in units:
            tiles = []
            for p in u["parts"]:
                for t in range(-(-p["n"] // P)):
                    tiles.append((p["off"] + t * P, min(P, p["n"] - t * P), p, t))
            u["tiles"] = tiles
            u["g0"], g = g, g - (-len(tiles) // 4)
            u["g1"] = g
        fin_unit = {u["fin"]: n for n, u in enumerate(units) if u["fin"] is not None}
        steps_n = NU + LOOK + 6
        outs_at = {}
        for qb in range(QB):
            for k, tr in enumerate(tracks):
                last = max(n for n, u in enumerate(units) if u["qb"] == qb and u["tr"] is tr)
                outs_at.setdefault(last + LOOK + 3, []).append((qb, k))
        order = []
        for s in range(steps_n):
            if 0 <= s - LOOK < NU:
                u = units[s - LOOK]
                order += [("p", s - LOOK, n) for n in range(u["g1"] - u["g0"])]
            order += [("o", qb, k) for qb, k in outs_at.get(s, [])]
        NE = len(order)
        index = {e: n for n, e in enumerate(order)}
        last_t = {v: index[("p", v, units[v]["g1"] - units[v]["g0"] - 1)] for v in range(NU)}
        last_of = [max(n for n, u in enumerate(units) if u["qb"] == qb and u["tr"]["bias"]) if any(t["bias"] for t in tracks) else 0
                   for qb in range(QB)]
        gate_jobs = [(tr["gate_w"], c, k, "gate") for c in range(2) for k, tr in enumerate(tracks)]
        next_jobs = [(tr["next_w"], c, k, "next") for c in range(2) for k, tr in enumerate(tracks) if tr.get("next_w") is not None]
        NJF = len(gate_jobs) + len(next_jobs)
        NG = len(gate_jobs)

        bufs_w = sum([3 * 1032, 4 * HALF, 2 * len(tracks) * P, 192, NCOL, NCOL, NCOL, 2 * len(tracks) * HALF])
        region = tracks[0]["bufs"]
        assert bufs_w <= region.shape[1], (tag, bufs_w, region.shape)
        cut, views = 0, []
        for w in (3 * 1032, 4 * HALF, 2 * len(tracks) * P, 192, NCOL, NCOL, NCOL, 2 * len(tracks) * HALF):
            views.append(region[:, cut:cut + w])
            cut += w
        p_sb, pt_sb, o_sb, pv_scr, negmax, rowsum, coef, sil = views
        p_sb = p_sb.rearrange("p (s n) -> p s n", s=3)
        pt_sb = pt_sb.rearrange("p (s n) -> p s n", s=4)
        o_sb = o_sb.rearrange("p (k s n) -> p k s n", k=len(tracks), s=2)
        sil = sil.rearrange("p (j n) -> p j n", j=NG)

        names = ("w", "proj", "proj_act", "proj_dve", "qk", "max", "exp", "tr", "ev", "pv", "fin", "fill", "fill_exp", "fill_ev",
                 "setup", "bias", "sink")
        (w_in, proj_done, proj_act, proj_dve, qk_done, max_done, exp_done, tr_done, ev_done, pv_done, fin_done,
         fill_done, fill_exp, fill_ev, setup_done, bias_done, sink_set) = (sem(tag + n) for n in names)
        gw_in = [sem(f"{tag}gw{k}") for k in range(len(tracks))]
        nw_in = [sem(f"{tag}nw{k}") for k in range(len(tracks))]
        n_loads = len(loads(0)) if proj_jobs else 0
        NJ = len(proj_jobs)
        act_jobs = [j for j in range(NJ) if proj_jobs[j][1]]
        dve_jobs = [j for j in range(NJ) if proj_jobs[j][2]]
        NA, ND = len(act_jobs), len(dve_jobs)
        sinks = next((tr["sink"] for tr in tracks if tr.get("sink")), None)
        SINK = 2 * P
        STEPS = 4

        def part_logits(u, p):
            n, b = p["n"], u["bank"]
            if u["tr"].get("sink"):
                return PS[:, b, SINK - n:SINK + 1]
            if u["banks"] == 2:
                return PS[:, b:b + 2, :].rearrange("p b n -> p (b n)")[:, p["off"]:p["off"] + n]
            return PS[:, b, p["off"]:p["off"] + n]

        sink_banks = {u["bank"]: u["hf"] for u in units if u["tr"].get("sink")}
        for u in units:
            assert not u["tr"].get("sink") or sink_banks[u["bank"]] == u["hf"]

        def body_jobs(last):
            return gate_jobs + ([] if last else next_jobs)

        def uses_in(s):
            return (units[s - LOOK]["g1"] - units[s - LOOK]["g0"] if 0 <= s - LOOK < NU else 0) + len(outs_at.get(s, []))

        def fill_plan(last):
            jobs = body_jobs(last)
            first_at = {}
            e = 0
            for s in range(steps_n):
                first_at[s] = e
                e += uses_in(s)
            step_of = [n for n in range(steps_n) for _ in range(uses_in(n))]
            total = len(jobs) * KT
            plan_, at_e = [[] for _ in range(NE)], 0
            for x in range(total):
                job, m = divmod(x, KT)
                w, c, k, what = jobs[job]
                at_e = max(at_e, x * NE // total)
                if m == 0 and job:
                    at_e = max(at_e, first_at[step_of[at_last] + FILL_GAP])
                if m == KT - 1 and what == "next":
                    lastq = max(n for n, u in enumerate(units) if u["tr"] is tracks[k] and u["qb"] < 4 * (c + 1))
                    at_e = max(at_e, first_at[lastq])
                plan_[at_e].append((job, m))
                at_last = at_e
            return plan_

        def fill_end_step(last):
            plan_, at_step, e = fill_plan(last), {}, 0
            for s in range(steps_n):
                for _ in range(uses_in(s)):
                    for job, m in plan_[e]:
                        if m == KT - 1:
                            at_step.setdefault(s, []).append(job)
                    e += 1
            return at_step

        def each_step(engine, body):
            with engine.Fori(0, STEPS - 1) as i:
                body(i, False)
            body(STEPS - 1, True)

        with nc.Block() as block:
            @block.sync
            def _(sp):
                def send(what, done):
                    for dst, src in what:
                        sp.dma_start(dst, src).then_inc(done, 16)

                def gates(i):
                    for k, tr in enumerate(tracks):
                        send(tr["gate_loads"](i), gw_in[k])

                def queries(i):
                    for k, tr in enumerate(tracks):
                        if tr.get("next_w") is not None:
                            send(tr["next_loads"](i), nw_in[k])

                def again(i, with_queries):
                    if proj_jobs:
                        sp.wait_ge(proj_done, i * NJ + NJ)
                        send(loads(i + 1), w_in)
                    sp.wait_ge(fill_done, i * NJF + NG)
                    gates(i + 1)
                    if with_queries and next_jobs:
                        sp.wait_ge(fill_done, i * NJF + NJF)
                        queries(i + 2)
                if proj_jobs:
                    send(loads(0), w_in)
                gates(0)
                queries(1)
                with sp.Fori(0, STEPS - 2) as i:
                    again(i, True)
                again(STEPS - 2, False)

            @block.tensor
            def _(pe):
                def step(i, last):
                    plan_ = fill_plan(last)
                    jobs = body_jobs(last)

                    def fill(e):
                        for job, m in plan_[e]:
                            w, c, k, what = jobs[job]
                            if m == 0:
                                tr = tracks[k]
                                if c == 0:
                                    nl = 16 * len(tr[what + "_loads"](0))
                                    pe.wait_ge((gw_in if what == "gate" else nw_in)[k], i * nl + nl)
                                if job:
                                    pe.wait_ge(fill_ev, i * NJF + job)
                            ins = nc.tensor.matmul(PS[:, FILL, :], w[:, m, :], hT[:, m, c * HALF:(c + 1) * HALF], start=m == 0, stop=m == KT - 1)
                            if m == KT - 1:
                                ins.then_inc(fill_done, 1)

                    if proj_jobs:
                        pe.wait_ge(w_in, i * (16 * n_loads) + 16 * n_loads)
                        for j, (emit, _, _) in enumerate(proj_jobs):
                            if j >= 8:
                                pe.wait_ge(proj_act, i * NA + sum(x <= j - 8 for x in act_jobs))
                                if any(x <= j - 8 for x in dve_jobs):
                                    pe.wait_ge(proj_dve, i * ND + sum(x <= j - 8 for x in dve_jobs))
                            emit(j % 8, i).then_inc(proj_done, 1)
                        pe.wait_ge(proj_act, i * NA + NA)
                        if ND:
                            pe.wait_ge(proj_dve, i * ND + ND)
                    if sinks:
                        pe.wait_ge(sink_set, i + 1)
                    e = 0
                    for s in range(steps_n):
                        if s < NU:
                            u = units[s]
                            if u["prev"] is not None:
                                pe.wait_ge(exp_done, i * NU + (u["prev"] + 1))
                            for p in u["parts"]:
                                start = SINK - p["n"] if u["tr"].get("sink") else p["off"]
                                c = 0
                                while c < p["n"]:
                                    b, o = divmod(start + c, HALF)
                                    w = min(HALF - o, p["n"] - c)
                                    ins = nc.tensor.matmul(PS[:, u["bank"] + b, o:o + w], u["tr"]["q_ap"](u["qb"], u["hf"]),
                                                           u["tr"]["k_ap"](p, i, c, w), start=True, stop=True)
                                    c += w
                            ins.then_inc(qk_done, 1)
                        v = s - LOOK - 1
                        if 0 <= v < NU:
                            u = units[v]
                            pe.wait_ge(ev_done, i * NE + (last_t[v] + 1))
                            if u["f"] >= 2:
                                pe.wait_ge(fin_done, i * NF + (u["f"] - 1))
                            hw = u["tr"]["head_w"]
                            for n, (c, w, p, t) in enumerate(u["tiles"]):
                                o = PS[:, OB + u["f"] % 2, p["slot"] * hw:(p["slot"] + 1) * hw]
                                ins = nc.tensor.matmul(o, pt_sb[0:w, (u["g0"] + n // 4) % 4, (n % 4) * P:(n % 4 + 1) * P],
                                                       u["tr"]["v_ap"](p, t, i, w), start=t == 0, stop=(t + 1) * P >= p["n"])
                            ins.then_inc(pv_done, 1)
                        v = s - LOOK
                        if 0 <= v < NU:
                            u = units[v]
                            pe.wait_ge(exp_done, i * NU + (v + 1))
                            for gg in range(u["g1"] - u["g0"]):
                                if e >= 1:
                                    pe.wait_ge(ev_done, i * NE + e)
                                for n, (c, w, p, t) in enumerate(u["tiles"][4 * gg:4 * gg + 4]):
                                    ins = nc.tensor.transpose(PS[:, TP, n * P:(n + 1) * P], p_sb[:, v % 3, c:c + P], ident)
                                ins.then_inc(tr_done, 1)
                                fill(e)
                                e += 1
                        for qb, k in outs_at.get(s, []):
                            f = max(u["f"] for u in units if u["qb"] == qb and u["tr"] is tracks[k])
                            pe.wait_ge(fin_done, i * NF + (f + 1))
                            pe.wait_ge(ev_done, i * NE + e)
                            nc.tensor.transpose(PS[:, TP, 0:P], o_sb[:, k, qb % 2, :], ident).then_inc(tr_done, 1)
                            fill(e)
                            e += 1
                    pe.wait_ge(ev_done, i * NE + NE)
                    pe.wait_ge(fill_ev, i * NJF + len(jobs))
                each_step(pe, step)

            @block.scalar
            def _(act):
                def step(i, last):
                    jobs, ended = body_jobs(last), fill_end_step(last)
                    for j in act_jobs:
                        act.wait_ge(proj_done, i * NJ + (j + 1))
                        proj_jobs[j][1](j % 8).then_inc(proj_act, 1)
                    e = 0
                    for s in range(steps_n):
                        if s < NU:
                            u = units[s]
                            act.wait_ge(max_done, i * NU + (s + 1))
                            if s >= 3:
                                act.wait_ge(tr_done, i * NE + (last_t[s - 3] + 1))
                            for p in u["parts"]:
                                w = p["n"] + (1 if u["tr"].get("sink") else 0)
                                ins = nc.scalar.activation(p_sb[:, s % 3, p["off"]:p["off"] + w], part_logits(u, p), ACT.Exp,
                                                           bias=negmax[:, p["col"]:p["col"] + 1], scale=-1.0,
                                                           accum_out=rowsum[:, p["col"]:p["col"] + 1])
                            ins.then_inc(exp_done, 1)
                        v = s - LOOK
                        if 0 <= v < NU:
                            u = units[v]
                            for gg in range(u["g1"] - u["g0"]):
                                act.wait_ge(tr_done, i * NE + (e + 1))
                                G = u["g0"] + gg
                                if G >= 4:
                                    old = next(n for n, x in enumerate(units) if x["g0"] <= G - 4 < x["g1"])
                                    act.wait_ge(pv_done, i * NU + (old + 1))
                                tiles = u["tiles"][4 * gg:4 * gg + 4]
                                nc.scalar.activation(pt_sb[:, G % 4, 0:len(tiles) * P], PS[:, TP, 0:len(tiles) * P],
                                                     ACT.Copy).then_inc(ev_done, 1)
                                e += 1
                        for qb, k in outs_at.get(s, []):
                            act.wait_ge(tr_done, i * NE + (e + 1))
                            nc.scalar.activation(oT[:, bass.ds(i + tracks[k]["o_tile"], 1), qb * P:(qb + 1) * P].rearrange("p a n -> p (a n)"),
                                                 PS[:, TP, 0:P], ACT.Copy).then_inc(ev_done, 1)
                            e += 1
                        for job in ended.get(s, []):
                            w, c, k, what = jobs[job]
                            act.wait_ge(fill_done, i * NJF + (job + 1))
                            if what == "gate":
                                nc.scalar.activation(sil[:, job, :], PS[:, FILL, :], ACT.Exp, scale=-1.0).then_inc(fill_exp, 1)
                            else:
                                tracks[k]["next_out"](PS[:, FILL, :], c).then_inc(fill_ev, 1)
                each_step(act, step)

            if stage_pool:
                @block.gpsimd
                def _(pool):
                    if setup_dve:
                        pool.wait_ge(setup_done, 1)
                    gen = pool.value_load(gen_i[0:1, 0:1], min_val=0, max_val=1)

                    def stage(qb, i):
                        with pool.If(gen == 0):
                            stage_pool(qb, i)
                        with pool.Else():
                            pool.nop()
                        pool.drain().then_inc(bias_done, 1)

                    for qb in range(QB):
                        stage(qb, 0)
                    with pool.Fori(0, STEPS - 1) as i:
                        for qb in range(QB):
                            pool.wait_ge(max_done, i * NU + (last_of[qb] + 1))
                            nc.gpsimd.tensor_tensor(wait_marks[:, 99 - qb:100 - qb], ident[0:1, 0:1], ident[0:1, 0:1], ALU.add)
                            stage(qb, i + 1)

            @block.vector
            def _(dve):
                if any("cmp" in tr["kinds"] for tr in tracks):
                    nc.vector.memset(p_sb[:, :, :], 0.0)
                    dve.drain()
                if setup_dve:
                    setup_dve(dve).then_inc(setup_done, 1)
                gen = dve.value_load(gen_i[0:1, 0:1], min_val=0, max_val=1) if head_dve else None

                def step(i, last):
                    ended = fill_end_step(last)
                    if head_dve:
                        head_dve(dve, gen, i)
                    for j in dve_jobs:
                        dve.wait_ge(proj_done, i * NJ + (j + 1))
                        proj_jobs[j][2](dve, j % 8).then_inc(proj_dve, 1)
                    if sinks:
                        pair = sinks(i)
                        for b, hf in sink_banks.items():
                            ins = nc.vector.tensor_copy(PS[:, b, SINK:SINK + 1], pair[:, hf:hf + 1])
                        ins.then_inc(sink_set, 1)
                    marks = 0
                    for s in range(steps_n):
                        if s < NU:
                            u = units[s]
                            dve.wait_ge(qk_done, i * NU + (s + 1))
                            if u["tr"]["bias"]:
                                if not any(x["qb"] == u["qb"] and x["tr"]["bias"] for x in units[:s]):
                                    dve.wait_ge(bias_done, i * QB + (u["qb"] + 1))
                                nc.vector.memset(wait_marks[:, marks:marks + 1], 0.0)
                                marks += 1
                            for p in u["parts"]:
                                lg, mn, n = part_logits(u, p), negmax[:, p["col"]:p["col"] + 1], p["n"]
                                if u["tr"]["bias"]:
                                    if p["kind"] == "win" and u["qb"] >= 4:
                                        nc.vector.tensor_tensor(lg[:, 0:P], lg[:, 0:P], winmask, ALU.add)
                                        dve.drain()
                                    ins = nc.vector.tensor_tensor_reduce(out=lg, in0=lg, in1=u["tr"]["bias"](p), scale=1.0,
                                                                         scalar=3e38, op0=ALU.add, op1=ALU.min, accum_out=mn)
                                    if p["kind"] == "cmp" and u["qb"] == 0:
                                        dve.drain()
                                        ins = nc.vector.tensor_scalar(mn, mn, 1e29, None, ALU.min)
                                else:
                                    if p["kind"] == "mla":
                                        nc.vector.tensor_tensor(lg[:, n - P:n], lg[:, n - P:n], causal, ALU.add)
                                        dve.drain()
                                    ins = nc.vector.tensor_reduce(out=mn, in_=lg, op=ALU.min, axis=AX.X)
                            ins.then_inc(max_done, 1)
                        v = s - LOOK
                        if 0 <= v < NU and units[v]["fin"] is not None:
                            u = units[v]
                            NK = len(u["tr"]["kinds"])
                            rs, cf = rowsum[:, u["c0"]:u["c0"] + NK], coef[:, u["c0"]:u["c0"] + NK]
                            dve.wait_ge(exp_done, i * NU + (v + 1))
                            if "cmp" in u["tr"]["kinds"] and u["qb"] == 0:
                                nc.vector.tensor_scalar(rs, rs, 1e-30, None, ALU.max)
                                dve.drain()
                            nc.vector.reciprocal(cf, rs)
                            if u["tr"].get("gate"):
                                dve.drain()
                                nc.vector.tensor_tensor(cf, cf, u["tr"]["gate"](u["qb"], u["hf"], i), ALU.mult)
                        v = s - LOOK - 2
                        if 0 <= v < NU and units[v]["fin"] is not None:
                            u = units[v]
                            NK, hw = len(u["tr"]["kinds"]), u["tr"]["head_w"]
                            k = next(n for n, t in enumerate(tracks) if t is u["tr"])
                            cf = coef[:, u["c0"]:u["c0"] + NK]
                            o_ps = PS[:, OB + u["f"] % 2, 0:NK * hw]
                            dst = o_sb[:, k, u["qb"] % 2, u["hf"] * hw:(u["hf"] + 1) * hw]
                            if u["hf"] == 0 and u["qb"] >= 2:
                                dve.wait_ge(tr_done, i * NE + (index[("o", u["qb"] - 2, k)] + 1))
                                nc.vector.memset(wait_marks[:, 40:41], 0.0)
                            dve.drain()
                            dve.wait_ge(pv_done, i * NU + (v + 1))
                            if NK > 1:
                                nc.vector.tensor_tensor(pv_scr.rearrange("p (k d) -> p k d", k=NK),
                                                        o_ps.rearrange("p (k d) -> p k d", k=NK),
                                                        cf.unsqueeze(2).to_broadcast([P, NK, hw]), ALU.mult)
                                dve.drain()
                                nc.vector.tensor_reduce(out=dst, in_=pv_scr.rearrange("p (k d) -> p d k", k=NK),
                                                        op=ALU.add, axis=AX.X).then_inc(fin_done, 1)
                            else:
                                nc.vector.tensor_scalar(dst, o_ps, cf, None, ALU.mult).then_inc(fin_done, 1)
                        for n_gate, job in enumerate(j for j in ended.get(s, []) if j < NG):
                            sl = sil[:, job, :]
                            dve.wait_ge(fill_exp, i * NG + (job + 1))
                            nc.vector.tensor_scalar(sl, sl, 1.0, None, ALU.add)
                            dve.drain()
                            nc.vector.reciprocal(sl, sl)
                            dve.drain()
                            nc.vector.tensor_tensor(sl, sl, PS[:, FILL, :], ALU.mult).then_inc(fill_ev, 1)
                        for c in range(2):
                            ready = max(s_ for s_, l in outs_at.items() if any(qb == 4 * c + 3 for qb, _ in l))
                            jobs_end = fill_end_step(last)
                            gate_end = max(s_ for s_, l in jobs_end.items() for j in l if j < NG and gate_jobs[j][1] == c)
                            if s == max(ready, gate_end):
                                for k, tr in enumerate(tracks):
                                    job = c * len(tracks) + k
                                    dve.wait_ge(ev_done, i * NE + (index[("o", 4 * c + 3, k)] + 1))
                                    nc.vector.memset(wait_marks[:, 41:42], 0.0)
                                    o = oT[:, bass.ds(i + tr["o_tile"], 1), c * HALF:(c + 1) * HALF].rearrange("p a n -> p (a n)")
                                    dve.drain()
                                    nc.vector.tensor_tensor(o, o, sil[:, job, :], ALU.mult)
                    dve.drain()

                each_step(dve, step)

    def output_stage(tag, w_out, tiles, row_runs, post_gain, x_src, out_dst, next_gain):
        wo_w, xt_w, y_w, g_w, sq_w, xn_w = carve(tiles * D, 2 * D, 2 * D, D, D, D)
        wo = wo_w.rearrange("p (k n) -> p k n", k=tiles)
        xt = xt_w.rearrange("p (s n) -> p s n", s=2)
        fused = next_gain is not None
        yt = y_w.rearrange("p (s n) -> p s n", s=2)
        stat, stat2 = small[:, 40:40 + QB], small[:, 50:50 + QB]
        wo_in = [sem(f"{tag}wo{k}") for k in range(tiles)]
        x_in = [sem(f"{tag}x{p}") for p in range(2)]
        g_in, out_done = sem(tag + "g"), [sem(f"{tag}out{p}") for p in range(2)]
        y_done, sq_done, var_done, rt_done, scaled, res_done, sq2, var2, rt2, xn_done, tr_done, hev_act, hev_dve = (
            sem(tag + n) for n in ("y", "sq", "var", "rt", "scaled", "res", "sq2", "var2", "rt2", "xn", "tr", "hev_act", "hev_dve"))
        row = lambda t: PS[:, 2 * (t % 2):2 * (t % 2) + 2, :].rearrange("p b n -> p (b n)")
        with nc.Block() as block:
            @block.sync
            def _(sp):
                for k in range(tiles):
                    for r0, r, n in row_runs(k):
                        sp.dma_start(wo[r0:r0 + n, k, :], w_out[r:r + n, :]).then_inc(wo_in[k], 16)
                sp.dma_start(g_w, post_gain.partition_broadcast(P)).then_inc(g_in, 16)
                for t in range(QB):
                    if t >= 2:
                        sp.wait_ge(res_done, t - 1)
                    sp.dma_start(xt[:, t % 2, :], x_src[t * P:(t + 1) * P, :]).then_inc(x_in[t % 2], 16)
                    if t >= 1:
                        sp.wait_ge(res_done, t)
                        sp.dma_start(out_dst[(t - 1) * P:t * P, :], yt[:, (t - 1) % 2, :]).then_inc(out_done[(t - 1) % 2], 16)
                sp.wait_ge(res_done, QB)
                sp.dma_start(out_dst[(QB - 1) * P:QB * P, :], yt[:, (QB - 1) % 2, :]).then_inc(out_done[(QB - 1) % 2], 16)
                for p in range(2):
                    sp.wait_ge(out_done[p], 16 * (QB // 2))

            @block.tensor
            def _(pe):
                def transposes(t):
                    pe.wait_ge(xn_done, t + 1)
                    if t >= 2:
                        pe.wait_ge(hev_act, t - 1)
                        pe.wait_ge(hev_dve, t - 1)
                    for k in range(KT):
                        ins = nc.tensor.transpose(PS[:, 4 + 2 * (t % 2) + k // 4, (k % 4) * P:(k % 4 + 1) * P], xn_w[:, k * P:(k + 1) * P], ident)
                    ins.then_inc(tr_done, 1)

                for t in range(QB):
                    if t >= 2:
                        pe.wait_ge(scaled, t - 1)
                        pe.wait_ge(sq_done, t - 1)
                    for k in range(tiles):
                        if t == 0:
                            pe.wait_ge(wo_in[k], 16 * len(row_runs(k)))
                        for c in range(2):
                            ins = nc.tensor.matmul(PS[:, 2 * (t % 2) + c, :], oT[:, k, t * P:(t + 1) * P], wo[:, k, c * HALF:(c + 1) * HALF],
                                                   start=k == 0, stop=k == tiles - 1)
                    ins.then_inc(y_done, 1)
                    if fused and t >= 1:
                        transposes(t - 1)
                if fused:
                    transposes(QB - 1)

            @block.scalar
            def _(act):
                def copy(t):
                    act.wait_ge(tr_done, t + 1)
                    for k in range(4):
                        ins = nc.scalar.activation(hT[:, k, t * P:(t + 1) * P], PS[:, 4 + 2 * (t % 2), k * P:(k + 1) * P], ACT.Copy,
                                                   scale=next_gain[:, k:k + 1])
                    ins.then_inc(hev_act, 1)

                for t in range(QB):
                    act.wait_ge(y_done, t + 1)
                    act.drain()
                    nc.scalar.activation(sq_w, row(t), ACT.Square, accum_out=stat[:, t:t + 1]).then_inc(sq_done, 1)
                    act.wait_ge(var_done, t + 1)
                    nc.scalar.activation(stat[:, t:t + 1], stat[:, t:t + 1], ACT.Sqrt).then_inc(rt_done, 1)
                    if fused:
                        act.wait_ge(res_done, t + 1)
                        act.drain()
                        nc.scalar.activation(sq_w, yt[:, t % 2, :], ACT.Square, accum_out=stat2[:, t:t + 1]).then_inc(sq2, 1)
                        act.wait_ge(var2, t + 1)
                        nc.scalar.activation(stat2[:, t:t + 1], stat2[:, t:t + 1], ACT.Sqrt).then_inc(rt2, 1)
                        if t >= 1:
                            copy(t - 1)
                if fused:
                    copy(QB - 1)

            @block.vector
            def _(dve):
                def mean_root(st, before, after):
                    nc.vector.tensor_scalar(st, st, 1.0 / D, EPS, ALU.mult, ALU.add)
                    dve.drain()
                    nc.vector.reciprocal(st, st).then_inc(before, 1)

                def copy(t):
                    dve.wait_ge(tr_done, t + 1)
                    nc.vector.tensor_tensor(hT[:, 4:8, t * P:(t + 1) * P], PS[:, 5 + 2 * (t % 2), :].rearrange("p (k n) -> p k n", k=4),
                                            next_gain[:, 4:8].unsqueeze(2).to_broadcast([P, 4, P]), ALU.mult).then_inc(hev_dve, 1)

                dve.wait_ge(g_in, 16)
                for t in range(QB):
                    st, y = stat[:, t:t + 1], yt[:, t % 2, :]
                    dve.wait_ge(sq_done, t + 1)
                    mean_root(st, var_done, rt_done)
                    dve.wait_ge(rt_done, t + 1)
                    if t >= 2:
                        dve.wait_ge(out_done[t % 2], 16 * (t // 2))
                    nc.vector.scalar_tensor_tensor(out=y, in0=row(t), scalar=st, in1=g_w, op0=ALU.mult, op1=ALU.mult).then_inc(scaled, 1)
                    dve.wait_ge(x_in[t % 2], 16 * (t // 2 + 1))
                    dve.drain()
                    nc.vector.tensor_tensor(y, y, xt[:, t % 2, :], ALU.add).then_inc(res_done, 1)
                    if fused:
                        st2 = stat2[:, t:t + 1]
                        dve.wait_ge(sq2, t + 1)
                        mean_root(st2, var2, rt2)
                        dve.wait_ge(rt2, t + 1)
                        if t >= 1:
                            dve.wait_ge(tr_done, t)
                        nc.vector.tensor_scalar(xn_w, y, st2, None, ALU.mult).then_inc(xn_done, 1)
                        if t >= 1:
                            copy(t - 1)
                if fused:
                    copy(QB - 1)

    ln = lambda kind, qb: dict(mla=P * (qb + 1), slc=P * (qb + 1), win=P * min(qb + 1, 5), swa=P * min(qb + 1, 2),
                               mem=MEM, cmp=min(NC, 8 * (qb + 1) - 1))[kind]

    def of_model(w, i, col, width=P):
        return w.rearrange("(k p) n -> p k n", p=P)[:, :, bass.ds(i + col, width)]

    def plain_loads(w, col, slot):
        return lambda i: [(slot, of_model(w, i * P, col))]

    def paired_loads(w, col, slot):
        return lambda i: [(slot[:, :, g * HD:(g + 1) * HD], of_model(w, i * HD, col + g * 4 * HD, HD)) for g in range(2)]

    def query_out(q, width):
        return lambda ps, c: nc.scalar.activation(q[:, c * HALF:(c + 1) * HALF], ps, ACT.Copy, scale=-(width ** -0.5))

    def first_queries(w, q, width, paired, col):
        runs = [(g * HD, col + g * 4 * HD, HD) for g in range(2)] if paired else [(0, col, P)]
        return (cols(w, *runs), "feat", lambda act, ps: nc.scalar.activation(flat2(q), ps, ACT.Copy, scale=-(width ** -0.5)))

    half_rows = lambda u: slice(u["hf"] * HD, (u["hf"] + 1) * HD)

    def memory_track(w, q_col, gate_col, q, kT, v, o_tile):
        return dict(
            kinds=["mem"], halves=1, head_w=P, o_tile=o_tile, bias=None, parts=lambda qb: [[("mem", MEM)]],
            q_ap=lambda qb, hf: q[:, qb * P:(qb + 1) * P],
            k_ap=lambda u, i, c, w_: kT[:, bass.ds(i * MEM, MEM)],
            v_ap=lambda u, t, i, w_: v[:, bass.ds(i * P + t * 512, P)],
            gate_w=wsl[:, 1], gate_loads=plain_loads(w, gate_col, wsl[:, 1]),
            next_w=wsl[:, 3], next_loads=plain_loads(w, q_col, wsl[:, 3]), next_out=query_out(q, P))

    def mem_jobs(w, kT, v):
        jobs = [(cols(w, (0, h * P, P)), "memk",
                 lambda act, ps, h=h: nc.scalar.activation(kT[:, h * MEM:(h + 1) * MEM], ps[:, 0, 0:MEM], ACT.Copy)) for h in range(4)]
        for h in range(4):
            jobs.append((cols(w, (0, 512 + h * P, P)), "memv",
                         lambda act, ps, h=h: nc.scalar.activation(v.rearrange("p (t n) -> p t n", t=2)[:, :, h * P:(h + 1) * P],
                                                                   ps[:, 0, 0:MEM].rearrange("p (t n) -> p t n", t=2), ACT.Copy)))
        return jobs

    pos_col_i = sb("pos_col", QB, I32)

    def load_positions(sp, pos_row_i, done):
        with nc.allow_non_contiguous_dma(reason="positions, one per partition"):
            sp.dma_start(pos_row_i, a["positions"].partition_broadcast(P)).then_inc(done, 16)
            sp.dma_start(pos_col_i[:, :], a["positions"].rearrange("(b p) -> p b", p=P)).then_inc(done, 16)

    we = a["w_in_even"]
    memT = norm_stage()

    top = 24500

    def at_top(width):
        nonlocal top
        top -= width
        return work[:, top:top + width]
    row_hi, row_lo = at_top(SEQ), at_top(SEQ)
    col_hi, col_lo = at_top(QB), at_top(QB)
    swk, swv, mk, mv, q_swa, q_mem = (at_top(SEQ) for _ in range(6))
    even_top = top
    rows = (row_hi, row_lo, col_hi, col_lo)
    cqn = work[:, 0:2 * SEQ].rearrange("p (k t) -> p k t", k=2)
    ckvn, kr = work[:, 2 * SEQ:3 * SEQ], work[:, 3 * SEQ:4 * SEQ]
    cs = work[:, 4 * SEQ:5 * SEQ]
    sinT = work[:, 5 * SEQ:6 * SEQ]
    pos_row_i = work[:, 6 * SEQ:7 * SEQ].bitcast(I32)
    itmp = work[:, 7 * SEQ:8 * SEQ].bitcast(I32)
    scr3 = [work[:, 8 * SEQ + n * 256:8 * SEQ + (n + 1) * 256] for n in range(3)]
    pos_f = work[:, 9 * SEQ:10 * SEQ]
    mbufs = work[:, 7 * SEQ:7 * SEQ + 6672]
    kslot = [work[:, 7 * SEQ + 6672 + s * SEQ:7 * SEQ + 6672 + (s + 1) * SEQ] for s in range(2)]
    assert 9 * SEQ + 6672 <= even_top
    sqs = oT[:, 0:3, :]
    rs_q, rs_kv = oT[:, 3, :], oT[:, 4, :]
    gq, gkv = gains[:, 16:18], gains[:, 18:19]
    nsink, nsink_pair = small[:, 200:208], small[:, 208:210]
    pos_in, latent_gain_in = sem("p0pos"), sem("p0lg")
    angles_done, trig_done, key_done, root_done = sem("p0angle"), sem("p0trig"), sem("p0key"), sem("p0root")
    QSC = -float((NOPE + ROPE) ** -0.5)

    def p0_loads(sp):
        load_positions(sp, pos_row_i, pos_in)
        sp.dma_start(nsink, a["swa_sinks"].partition_broadcast(P)).then_inc(pos_in, 16)
        with nc.allow_non_contiguous_dma(reason="gains, one per partition"):
            sp.dma_start(gq, a["mla_q_norm"].rearrange("(k p) -> p k", p=P)).then_inc(latent_gain_in, 16)
            sp.dma_start(gkv, a["mla_kv_norm"].rearrange("(k p) -> p k", p=P)).then_inc(latent_gain_in, 16)

    def p0_vector(dve):
        dve.wait_ge(pos_in, 48)
        nc.vector.tensor_copy(pos_f, pos_row_i)
        position_rows(dve, pos_row_i, pos_col_i[:, :], row_hi, row_lo, col_hi, col_lo, itmp)
        TWO_PI = [6.28125, 0.0019350051879882812, 2 * math.pi - 6.28125 - 0.0019350051879882812]
        MAGIC = 1.5 * 2 ** 23
        turns = itmp.bitcast(F32)
        nc.vector.tensor_scalar(pos_f, pos_f, consts[:, C_INV:C_INV + 1], None, ALU.mult)
        dve.drain()
        nc.vector.tensor_scalar(turns, pos_f, 1 / (2 * math.pi), MAGIC, ALU.mult, ALU.add)
        dve.drain()
        nc.vector.tensor_scalar(turns, turns, MAGIC, None, ALU.subtract)
        dve.drain()
        for part in TWO_PI:
            nc.vector.scalar_tensor_tensor(out=pos_f, in0=turns, scalar=-float(part), in1=pos_f, op0=ALU.mult, op1=ALU.add)
            dve.drain()
        PI = 3.1415925
        nc.vector.tensor_scalar(sinT, pos_f, PI, -PI, ALU.min, ALU.max)
        nc.vector.tensor_scalar(turns, pos_f, math.pi / 2, None, ALU.is_gt)
        nc.vector.tensor_scalar(cs, pos_f, math.pi / 2, None, ALU.add)
        dve.drain()
        nc.vector.scalar_tensor_tensor(out=cs, in0=turns, scalar=-2 * math.pi, in1=cs, op0=ALU.mult, op1=ALU.add)
        dve.drain()
        nc.vector.tensor_scalar(cs, cs, PI, -PI, ALU.min, ALU.max).then_inc(angles_done, 1)
        d1, d2 = pos_f[:, 0:SEQ - 1], turns[:, 0:SEQ - 1]
        dve.drain()
        nc.vector.tensor_tensor(d1, row_hi[:, 1:SEQ], row_hi[:, 0:SEQ - 1], ALU.subtract)
        nc.vector.tensor_tensor(d2, row_lo[:, 1:SEQ], row_lo[:, 0:SEQ - 1], ALU.subtract)
        dve.drain()
        nc.vector.scalar_tensor_tensor(out=d1, in0=d1, scalar=65536.0, in1=d2, op0=ALU.mult, op1=ALU.add)
        dve.drain()
        nc.vector.tensor_scalar(d1, d1, 1.0, None, ALU.not_equal)
        dve.drain()
        nc.vector.tensor_reduce(out=gen_f, in_=d1, op=ALU.max, axis=AX.X)
        dve.drain()
        nc.vector.tensor_copy(gen_i[:, :], gen_f)
        bias_block(dve, rows, QB - 1, SEQ - 256, 256, [band[:, h * 256:(h + 1) * 256] for h in range(HEADS)],
                   range(HEADS), scr3, False)
        for h in range(HEADS):
            add_to(band[:, h * 256 + P:(h + 1) * 256], causal)
        dve.wait_ge(trig_done, 1)
        nc.vector.tensor_scalar(cs[96:128, :], sinT[96:128, :], consts[96:128, C_SIGN:C_SIGN + 1], None, ALU.mult)
        dve.wait_ge(key_done, 1)
        dve.drain()
        t1 = sinT[64:96, :]
        nc.vector.tensor_tensor(t1, kr[96:128, :], cs[96:128, :], ALU.mult)
        nc.vector.tensor_tensor(kr[64:96, :], kr[64:96, :], cs[64:96, :], ALU.mult)
        dve.drain()
        for s in range(2):
            nc.vector.tensor_tensor(kslot[s][64:96, :], kr[64:96, :], t1, ALU.add)
        nc.vector.tensor_scalar(cs[64:128, :], cs[64:128, :], QSC, None, ALU.mult)
        dve.wait_ge(root_done, 2)
        dve.wait_ge(latent_gain_in, 32)
        for rs in (rs_q, rs_kv):
            nc.vector.reciprocal(rs, rs)
        dve.drain()
        for k in range(2):
            nc.vector.scalar_tensor_tensor(out=cqn[:, k, :], in0=cqn[:, k, :], scalar=gq[:, k:k + 1], in1=rs_q, op0=ALU.mult, op1=ALU.mult)
        nc.vector.scalar_tensor_tensor(out=ckvn, in0=ckvn, scalar=gkv, in1=rs_kv, op0=ALU.mult, op1=ALU.mult)

    def latent_out(dst, k):
        def go(act, ps):
            nc.scalar.activation(flat2(dst), ps, ACT.Copy)
            return nc.scalar.activation(flat2(sqs[:, k, :]), ps, ACT.Square)
        return go

    def square_sums(ks):
        def go(pe, b):
            for c in range(2):
                for k in ks:
                    ins = nc.tensor.matmul(PS[:, b + c, :], ones, sqs[:, k, c * HALF:(c + 1) * HALF], start=k == ks[0], stop=k == ks[-1])
            return ins
        return go

    def root_out(dst, n):
        def go(act, ps):
            nc.scalar.activation(flat2(dst), ps, ACT.Sqrt, scale=1.0 / n, bias=consts[:, C_EPS:C_EPS + 1]).then_inc(root_done, 1)
            return act.drain()
        return go

    def key_out(act, ps):
        nc.scalar.activation(flat2(kr), ps, ACT.Copy).then_inc(key_done, 1)
        return act.drain()

    def swv_out(act, ps):
        ins = nc.scalar.activation(flat2(swv), ps, ACT.Copy)
        act.wait_ge(angles_done, 1)
        nc.scalar.activation(cs, cs, ACT.Sin)
        nc.scalar.activation(sinT, sinT, ACT.Sin).then_inc(trig_done, 1)
        return act.drain()

    even_jobs = [(cols(we, (0, E_CQ + P * i, P)), "feat", latent_out(cqn[:, i, :], i)) for i in range(2)]
    even_jobs.append((cols(we, (0, E_CKV, P)), "feat", latent_out(ckvn, 2)))
    even_jobs.append((cols(we, (0, E_CKV, 64), (64, E_KR, 32), (96, E_KR + 16, 16), (112, E_KR, 16)), "feat", key_out))
    even_jobs.append((None, square_sums([0, 1]), root_out(rs_q, 256)))
    even_jobs.append((None, square_sums([2]), root_out(rs_kv, 128)))
    even_jobs.append((cols(we, (0, E_KSWA, P)), "feat", copy_out(flat2(swk))))
    even_jobs.append((cols(we, (0, E_VSWA, P)), "tok", swv_out))
    even_jobs.append(first_queries(we, q_swa, HD, True, E_QSWA))
    even_jobs.append(first_queries(we, q_mem, P, False, E_QMEM))
    project_stage("p0", even_jobs + mem_jobs(a["w_mem_kv"][0], mk, mv), memT, p0_vector, p0_loads)

    vs = kr
    qslot = [work[:, 5 * SEQ:6 * SEQ], work[:, 6 * SEQ:7 * SEQ]]
    wuq_w, wukv_w = wsl_t[:, 2 * SEQ:2 * SEQ + 512], wsl_t[:, 2 * SEQ + 512:2 * SEQ + 768]
    rtmp = wsl_t[:, 3 * SEQ:3 * SEQ + HALF]
    wuq = wuq_w.rearrange("p (k h n) -> p k h n", k=2, h=2)
    wukv = wukv_w.rearrange("p (h n) -> p h n", h=2)
    uq = a["mla_w_uq"].rearrange("(k p) n -> p k n", p=P)

    def mla_loads(i):
        out = []
        for hf in range(2):
            c0 = i * (2 * 96) + hf * 96
            out.append((wuq[:, :, hf, 0:96], uq[:, :, bass.ds(c0, 96)]))
            out.append((wuq[:, :, hf, 96:112], uq[:, :, bass.ds(c0 + 80, 16)]))
            out.append((wuq[:, :, hf, 112:128], uq[:, :, bass.ds(c0 + 64, 16)]))
        out.append((wukv_w, a["mla_w_ukv"][:, bass.ds(i * 256, 256)]))
        return out

    def mla_q(hf, c):
        sl = slice(c * HALF, (c + 1) * HALF)

        def emit(b, i):
            for k in range(2):
                ins = nc.tensor.matmul(PS[:, b, :], wuq[:, k, hf, :], cqn[:, k, sl], start=k == 0, stop=k == 1)
            return ins

        def on_act(b):
            return nc.scalar.activation(qslot[hf][0:64, sl], PS[0:64, b, :], ACT.Copy, scale=QSC)

        def on_dve(dve, b):
            nc.vector.tensor_tensor(rtmp[64:96, :], PS[96:128, b, :], cs[96:128, sl], ALU.mult)
            nc.vector.tensor_tensor(qslot[hf][64:96, sl], PS[64:96, b, :], cs[64:96, sl], ALU.mult)
            dve.drain()
            ins = nc.vector.tensor_tensor(qslot[hf][64:96, sl], qslot[hf][64:96, sl], rtmp[64:96, :], ALU.add)
            dve.drain()
            return ins
        return emit, on_act, on_dve

    def mla_k(hf, c):
        sl = slice(c * HALF, (c + 1) * HALF)
        return (lambda b, i: nc.tensor.matmul(PS[0:64, b, :], wukv[:, hf, 0:64], ckvn[:, sl], start=True, stop=True),
                lambda b: nc.scalar.activation(kslot[hf][0:64, sl], PS[0:64, b, :], ACT.Copy), None)

    def mla_v(c):
        def emit(b, i):
            for t in range(4):
                ins = nc.tensor.matmul(PS[:, b, t * P:(t + 1) * P], ckvn[:, (4 * c + t) * P:(4 * c + t + 1) * P],
                                       wukv[:, :, 64:128], start=True, stop=True)
            return ins
        return emit, lambda b: nc.scalar.activation(vs[:, c * HALF:(c + 1) * HALF], PS[:, b, :], ACT.Copy), None

    mla_track = dict(
        kinds=["mla"], halves=2, head_w=HD, o_tile=0, bias=None, bufs=mbufs, parts=lambda qb: [[("mla", ln("mla", qb))]],
        q_ap=lambda qb, hf: qslot[hf][0:96, qb * P:(qb + 1) * P],
        k_ap=lambda u, i, c, w: kslot[u["hf"]][0:96, c:c + w],
        v_ap=lambda u, t, i, w: vs[:, t * P + u["hf"] * HD:t * P + (u["hf"] + 1) * HD],
        gate_w=wsl[:, 0], gate_loads=plain_loads(we, E_GMLA, wsl[:, 0]))
    attention_stage(
        "mla", [mla_track], loads=mla_loads,
        proj_jobs=[mla_q(hf, c) for hf in range(2) for c in range(2)] + [mla_k(hf, c) for hf in range(2) for c in range(2)] + [mla_v(c) for c in range(2)])

    BW = 264
    swab, swband, sc1, sc2, sc3 = carve(2 * QB * BW, HEADS * 256, 256, 256, 256)
    used_w = 2 * QB * BW + HEADS * 256 + 768

    def swa_setup(dve):
        nc.vector.tensor_copy(swband, band[:, :])
        dve.drain()
        for h in range(HEADS):
            add_to(swband[:, h * 256:h * 256 + P], winmask)
        nc.vector.memset(swab.rearrange("p (b n) -> p b n", n=BW)[:, :, 256:257], 0.0)
        nc.vector.tensor_scalar(nsink, nsink, -1.0, None, ALU.mult)
        return dve.drain()

    def swa_block(hf, qb):
        w = P if qb == 0 else 256
        o = (hf * QB + qb) * BW + 256
        return swab[:, o - w:o], w

    def swa_bias(u):
        o = (u["hf"] * QB + u["qb"]) * BW + 256
        return swab[:, o - u["n"]:o + 1]

    def swa_sink(i):
        for g in range(2):
            nc.vector.tensor_copy(nsink_pair[:, g:g + 1], nsink[:, bass.ds(i + 4 * g, 1)])
        nc.vector.drain()
        return nsink_pair

    def swa_stage(qb, i):
        for hf in range(2):
            dst, w = swa_block(hf, qb)
            nc.gpsimd.tensor_copy(dst, swband[:, bass.ds(i * 256 + (hf * 1024 + 256 - w), w)])

    def swa_general(dve, gen, i):
        with dve.If(gen == 1):
            for qb in range(QB):
                w, k0 = (P, 0) if qb == 0 else (256, (qb - 1) * P)
                dst = [swa_block(hf, qb)[0] for hf in range(2)]
                bias_block(dve, rows, qb, k0, w, dst, [i, i + 4], (sc1, sc2, sc3), True)
                for d in dst:
                    add_to(d[:, w - P:w], causal)
                    if qb:
                        add_to(d[:, 0:P], winmask)
                dve.drain()
        with dve.Else():
            dve.nop()

    first_key = lambda u: max(0, u["qb"] - 1) * P
    swa_track = dict(
        kinds=["swa"], halves=2, head_w=HD, o_tile=4, bias=swa_bias, sink=swa_sink, bufs=work[:, used_w:even_top],
        parts=lambda qb: [[("swa", ln("swa", qb))]], bank_of=lambda qb, hf: hf,
        q_ap=lambda qb, hf: q_swa[hf * HD:(hf + 1) * HD, qb * P:(qb + 1) * P],
        k_ap=lambda u, i, c, w: swk[half_rows(u), first_key(u):(u["qb"] + 1) * P],
        v_ap=lambda u, t, i, w: swv[:, first_key(u) + t * P + u["hf"] * HD:first_key(u) + t * P + (u["hf"] + 1) * HD],
        gate_w=wsl[:, 0], gate_loads=paired_loads(we, E_GSWA, wsl[:, 0]),
        next_w=wsl[:, 2], next_loads=paired_loads(we, E_QSWA, wsl[:, 2]), next_out=query_out(q_swa, HD))
    mem_track = memory_track(we, E_QMEM, E_GMEM, q_mem, mk, mv, 8)
    mem_track["bank_of"] = lambda qb, hf: 2 + qb % 2
    attention_stage("swa", [swa_track, mem_track], loads=None, setup_dve=swa_setup, head_dve=swa_general, stage_pool=swa_stage)

    def even_rows(k):
        if 4 <= k < 8:
            return [(0, 512 + (k - 4) * HD, HD), (HD, 512 + (k - 4 + 4) * HD, HD)]
        return [(0, k * P, P)]

    output_stage("o0", a["w_out_even"], 12, even_rows, a["norm_post"][0], a["x"], x1_dram, gains[:, 32:40])

    nc.clear_and_free_semaphores(layer_sems)
    nc.all_engine_barrier()
    layer_sems.clear()
    wo_ = a["w_in_odd"]
    extra = oT_t[:, 8 * SEQ:12 * SEQ]
    mk, mv, row_hi, row_lo = (extra[:, n * SEQ:(n + 1) * SEQ] for n in range(4))
    top = 24500
    kslc, kwin, vslc, vwin, q_nsa, q_mem = (at_top(SEQ) for _ in range(6))
    kcT, vc = at_top(64), at_top(P)
    gl = at_top(QB * 24)
    col_hi, col_lo = at_top(QB), at_top(QB)
    rows = (row_hi, row_lo, col_hi, col_lo)
    odd_top = top
    kcmp, vcmp = work[:, 0:SEQ], work[:, SEQ:2 * SEQ]
    at = 2 * SEQ
    w2 = work[:, at:at + 256].rearrange("p (s m d) -> p s m d", s=2, m=2)
    pos2 = work[:, at + 256:at + 288].rearrange("p (s l) -> p s l", s=2)
    hid = work[:, at + 288:at + 800].rearrange("p (s m c) -> p s m c", s=2, m=2)
    hb = work[:, at + 800:at + 804].rearrange("p (s m) -> p s m", s=2)
    w1 = work[:, 3 * SEQ:11 * SEQ].rearrange("p (s l n) -> p s l n", s=2, l=16)
    memT_w = work[:, 11 * SEQ:13 * SEQ]
    memT = memT_w.rearrange("p (k t) -> p k t", k=KT)
    x2 = work[:, 13 * SEQ:17 * SEQ].rearrange("p (s g t) -> p s g t", s=2, g=2)
    assert 17 * SEQ <= odd_top
    pos_row_i, itmp = oT[:, 0, :].bitcast(I32), oT[:, 1, :].bitcast(I32)
    pos_in, mem_in, raw_done, x2_in = sem("p1pos"), sem("p1mem"), sem("p1raw"), sem("p1x2")
    w1_in, w2_in = [sem("p1w1k"), sem("p1w1v")], sem("p1w2")

    def p1_loads(sp):
        load_positions(sp, pos_row_i, pos_in)

    def p1_vector(dve):
        dve.wait_ge(pos_in, 32)
        position_rows(dve, pos_row_i, pos_col_i[:, :], row_hi, row_lo, col_hi, col_lo, itmp)

    def p1_more_loads(pool):
        for s, n in enumerate("kv"):
            pool.dma_start(w2[:, s], a["cmp_w2_" + n].rearrange("(m p) d -> p m d", p=P)).then_inc(w2_in, 16)
            with nc.allow_non_contiguous_dma(reason="position embedding, one per partition"):
                pool.dma_start(pos2[:, s, :], a["cmp_pos_" + n].rearrange("(l a) d -> (a d) l", a=2)).then_inc(w2_in, 16)
        pool.wait_ge(raw_done, 1)
        for s, src in enumerate((kcmp, vcmp)):
            if s:
                pool.wait_ge(raw_done, 2)
            for g in range(2):
                rows_g = src[g * HD:(g + 1) * HD, :]
                pool.dma_start(x2[0:HD, s, g, :], rows_g).then_inc(x2_in, 16)
                pool.dma_start(x2[HD:P, s, g, 0:SEQ - 1], rows_g[:, 1:SEQ]).then_inc(x2_in, 16)
        for s, n in enumerate("kv"):
            pool.dma_start(w1[:, s], a["cmp_w1_" + n].rearrange("(l p) n -> p l n", p=P)).then_inc(w1_in[s], 16)
        pool.dma_start(memT_w, memT1_dram).then_inc(mem_in, 16)

    def raw_out(dst):
        def go(act, ps):
            nc.scalar.activation(flat2(dst), ps, ACT.Copy).then_inc(raw_done, 1)
            return act.drain()
        return go

    def hidden(s, m):
        def go(pe, b):
            if m == 0:
                if s == 0:
                    pe.wait_ge(x2_in, 16 * 8)
                    pe.wait_ge(w2_in, 64)
                pe.wait_ge(w1_in[s], 16)
            wm = lambda l: w1[:, s, l, m * P:(m + 1) * P]
            for l in range(16):
                ins = nc.tensor.matmul(PS[:, b, 128:129], wm(l), pos2[:, s, l:l + 1], start=l == 0, stop=l == 15)
            for g in range(2):
                for l in range(16):
                    ins = nc.tensor.matmul(PS[:, b, g * 64:g * 64 + NC], wm(l),
                                           x2[:, s, g, 2 * l:2 * l + CMP_S * (NC - 1) + 1:CMP_S], start=l == 0, stop=l == 15)
            return ins
        return go

    def hidden_out(s, m):
        def go(act, ps):
            nc.scalar.activation(hb[:, s, m:m + 1], ps[:, 0, 128:129], ACT.Copy)
            act.drain()
            return nc.scalar.activation(hid[:, s, m, :].rearrange("p (g c) -> p g c", g=2)[:, :, 0:NC],
                                        ps[:, 0, 0:P].rearrange("p (g c) -> p g c", g=2)[:, :, 0:NC],
                                        ACT.Silu, bias=hb[:, s, m:m + 1])
        return go

    def compressed(pe, b):
        for g in range(2):
            for m in range(2):
                nc.tensor.matmul(PS[g * HD:(g + 1) * HD, b, 0:NC], w2[:, 0, m, :], hid[:, 0, m, g * 64:g * 64 + NC], start=m == 0, stop=m == 1)
            for m in range(2):
                ins = nc.tensor.matmul(PS[0:NC, b + 1, g * HD:(g + 1) * HD], hid[:, 1, m, g * 64:g * 64 + NC], w2[:, 1, m, :], start=m == 0, stop=m == 1)
        return ins

    def compressed_out(act, ps):
        nc.scalar.activation(kcT[:, 0:NC], ps[:, 0, 0:NC], ACT.Copy)
        return nc.scalar.activation(vc[0:NC, :], ps[0:NC, 1, 0:P], ACT.Copy)

    def gl_out(act, ps):
        return nc.scalar.activation(gl.rearrange("p (c t n) -> p c t n", c=2, t=4),
                                    ps.rearrange("p c (t n) -> p c t n", t=4)[:, :, :, 0:24], ACT.Sigmoid)

    odd_jobs = [
        (cols(wo_, (0, O_KCMP, P)), "feat", raw_out(kcmp)),
        (cols(wo_, (0, O_VCMP, P)), "feat", raw_out(vcmp)),
        (cols(wo_, (0, O_KSLC, P)), "feat", copy_out(flat2(kslc))),
        (cols(wo_, (0, O_KWIN, P)), "feat", copy_out(flat2(kwin))),
        (cols(wo_, (0, O_VSLC, P)), "tok", copy_out(flat2(vslc))),
        (cols(wo_, (0, O_VWIN, P)), "tok", copy_out(flat2(vwin))),
        first_queries(wo_, q_nsa, HD, True, O_Q),
        first_queries(wo_, q_mem, P, False, O_QMEM),
        (cols(wo_, (0, O_GL, 24)), "tok24", gl_out)]
    hidden_jobs = [(None, hidden(s, m), hidden_out(s, m)) for s in range(2) for m in range(2)]
    memory_jobs = mem_jobs(a["w_mem_kv"][1], mk, mv)
    project_stage("p1", odd_jobs + hidden_jobs + memory_jobs[:4] + [(None, compressed, compressed_out)] + memory_jobs[4:], memT,
                  p1_vector, p1_loads, mem_in, p1_more_loads)

    PACK = [64 * qb * (qb + 1) for qb in range(QB + 1)]
    nb_w, nbufs = work[:, 0:2 * PACK[QB]], work[:, 2 * PACK[QB]:odd_top]
    nb16 = nb_w.rearrange("p (n s) -> p n s", s=CMP_S)

    def nsa_stage(qb, i):
        for hf in range(2):
            o = hf * PACK[QB] + PACK[qb]
            n = PACK[qb + 1] - PACK[qb]
            if n > 256:
                nc.gpsimd.tensor_copy(nb_w[:, o:o + n - 256], band[:, bass.ds(i * 256 + hf * 1024, 1)].to_broadcast([P, n - 256]))
            w = min(n, 256)
            nc.gpsimd.tensor_copy(nb_w[:, o + n - w:o + n], band[:, bass.ds(i * 256 + (hf * 1024 + 256 - w), w)])

    def nsa_general(dve, gen, i):
        with dve.If(gen == 1):
            for qb in range(QB):
                n = PACK[qb + 1] - PACK[qb]
                dst = [nb_w[:, hf * PACK[QB] + PACK[qb]:hf * PACK[QB] + PACK[qb + 1]] for hf in range(2)]
                bias_block(dve, rows, qb, 0, n, dst, [i, i + 4], [nbufs[:, s * SEQ:(s + 1) * SEQ] for s in range(3)], True)
                for d in dst:
                    add_to(d[:, n - P:n], causal)
                dve.drain()
        with dve.Else():
            dve.nop()

    def nsa_bias(u):
        qb, o = u["qb"], u["hf"] * PACK[QB] + PACK[u["qb"]]
        if u["kind"] == "cmp":
            return nb16[:, o // CMP_S + 1:o // CMP_S + 1 + u["n"], CMP_S - 1]
        return nb_w[:, o + P * (qb + 1) - u["n"]:o + P * (qb + 1)]

    def nsa_k(u, i, c, w):
        r = half_rows(u)
        if u["kind"] == "cmp":
            return kcT[r, c:c + w]
        if u["kind"] == "slc":
            return kslc[r, c:c + w]
        k0 = P * (u["qb"] + 1) - u["n"]
        return kwin[r, k0 + c:k0 + c + w]

    def nsa_v(u, t, i, w):
        c = u["hf"] * HD
        if u["kind"] == "cmp":
            return vc[0:w, c:c + HD]
        if u["kind"] == "slc":
            return vslc[:, t * P + c:t * P + c + HD]
        t += u["qb"] + 1 - u["n"] // P
        return vwin[:, t * P + c:t * P + c + HD]

    nsa_track = dict(
        kinds=["cmp", "slc", "win"], halves=2, head_w=HD, o_tile=0, bias=nsa_bias, bufs=nbufs,
        parts=lambda qb: [[("slc", ln("slc", qb))], [("win", ln("win", qb)), ("cmp", ln("cmp", qb))]],
        gate=lambda qb, hf, i: gl[:, bass.ds(i * 3 + (qb * 24 + hf * 12), 3)],
        q_ap=lambda qb, hf: q_nsa[hf * HD:(hf + 1) * HD, qb * P:(qb + 1) * P], k_ap=nsa_k, v_ap=nsa_v,
        gate_w=wsl[:, 0], gate_loads=paired_loads(wo_, O_GNSA, wsl[:, 0]),
        next_w=wsl[:, 2], next_loads=paired_loads(wo_, O_Q, wsl[:, 2]), next_out=query_out(q_nsa, HD))
    attention_stage("nsa", [nsa_track, memory_track(wo_, O_QMEM, O_GMEM, q_mem, mk, mv, 4)], loads=None,
                    head_dve=nsa_general, stage_pool=nsa_stage)

    def odd_rows(k):
        return [(0, k * HD, HD), (HD, (k + 4) * HD, HD)] if k < 4 else [(0, k * P, P)]

    output_stage("o1", a["w_out_odd"], 8, odd_rows, a["norm_post"][1], x1_dram, a["out"], None)
    ctx.close()


SQUEEZE = ("x", "mem", "w_in_even", "mla_q_norm", "mla_kv_norm", "swa_sinks", "mla_w_uq", "mla_w_ukv", "w_out_even", "w_in_odd",
           "cmp_pos_k", "cmp_pos_v", "cmp_w1_k", "cmp_w2_k", "cmp_w1_v", "cmp_w2_v", "w_out_odd")


def build(nc, arrays):
    a = {}
    for name, v in arrays.items():
        ap = nc.dram_tensor(name, v.shape, mybir.dt.from_np(v.dtype), kind="ExternalInput").ap()
        a[name] = ap[0] if name in SQUEEZE else ap
    a["out"] = nc.dram_tensor("out", (1, SEQ, D), F32, kind="ExternalOutput").ap()[0]
    trunk(nc, a)


def kernel(**inputs):
    import concourse.bacc as bacc
    from concourse.bass_utils import run_bass_kernel_spmd

    nc = bacc.Bacc("TRN2", target_bir_lowering=False, num_devices=1)
    arrays = {name: np.ascontiguousarray(v) for name, v in inputs.items()}
    arrays["const_tables"] = make_constants()
    build(nc, arrays)
    return run_bass_kernel_spmd(nc, [arrays], core_ids=[0]).results[0]["out"]
```

```python
import math
from contextlib import ExitStack

import numpy as np

import concourse.bass as bass
import concourse.mybir as mybir

F32 = mybir.dt.float32
I32 = mybir.dt.int32
ALU = mybir.AluOpType
ACT = mybir.ActivationFunctionType
AX = mybir.AxisListType

P = 128
SEQ = 1024
D = 1024
MEM = 256
KT = D // P
QB = SEQ // P
HALF = 512
HD = 64
HEADS = 8
PAIRS = HEADS // 2
NB = 32
BIG = 1e30
EPS = 1e-6

C_ID = 0
C_CAUSAL = 128
C_WIN = 256
C_ONES = 384
C_INV = 512
C_SIGN = 513
C_NTHR = 514
C_BKT = C_NTHR + NB
C_EPS = C_BKT + NB
C_HOT = C_EPS + 1
SKEW = 384
N_CONST = C_HOT + SKEW

E_CQ, E_CKV, E_KR, E_GMLA, E_QSWA, E_KSWA, E_VSWA, E_GSWA, E_QMEM, E_GMEM = (
    0, 256, 384, 416, 928, 1440, 1568, 1696, 2208, 2720)
(O_Q, O_KCMP, O_VCMP, O_KSLC, O_VSLC, O_KWIN, O_VWIN, O_GL, O_GNSA, O_QMEM, O_GMEM) = (
    0, 512, 640, 768, 896, 1024, 1152, 1280, 1304, 1816, 2328)
NOPE, ROPE = 64, 32
CMP_L, CMP_S = 32, 16
NC = (SEQ - CMP_L) // CMP_S + 1
OUT_LAG = 2
LAG = 2
LOOK = 2


def make_constants():
    c = np.zeros((P, N_CONST), np.float32)
    q, k = np.arange(P)[:, None], np.arange(P)[None, :]
    c[:, C_ID:C_ID + P] = np.eye(P)
    c[:, C_CAUSAL:C_CAUSAL + P] = np.where(k <= q, 0, BIG)
    c[:, C_WIN:C_WIN + P] = np.where(k > q, 0, BIG)
    c[:, C_ONES:C_ONES + P] = 1
    half = ROPE // 2
    inv = np.float32(10000.0) ** (-np.arange(half, dtype=np.float32) / np.float32(half))
    c[:, C_INV] = inv[np.arange(P) % half]
    c[:, C_SIGN] = np.where(np.arange(P) % ROPE < half, -1, 1)
    d = np.arange(1, 256, dtype=np.float32)
    ratio = np.log(d / np.float32(16)).astype(np.float32) / np.float32(math.log(8))
    bucket = np.where(d < 16, d, np.minimum(16 + (ratio * 16).astype(np.int32), NB - 1)).astype(int)
    for b in range(1, NB):
        c[:, C_NTHR + b] = -d[np.argmax(bucket >= b)]
    c[:, C_BKT:C_BKT + NB] = np.arange(NB)
    c[:, C_EPS] = EPS
    dist = np.maximum(255 - np.arange(SKEW), 0)
    of = np.where(dist == 0, 0, bucket[np.maximum(dist, 1) - 1])
    c[of, C_HOT + np.arange(SKEW)] = -1
    return c


def trunk(nc, a):
    ctx = ExitStack()

    def sb(name, width, dt=F32):
        return ctx.enter_context(nc.sbuf_tensor(name, [P, width], dt))

    layer_sems = []

    def sem(name):
        layer_sems.append(nc.alloc_semaphore(name))
        return layer_sems[-1]

    def kept_sem(name):
        return nc.alloc_semaphore(name)

    consts = sb("consts", N_CONST)
    ident = consts[:, C_ID:C_ID + P]
    causal = consts[:, C_CAUSAL:C_CAUSAL + P]
    winmask = consts[:, C_WIN:C_WIN + P]
    ones = consts[:, C_ONES:C_ONES + P]
    table = sb("table", NB * HEADS)
    hT_t = sb("hT", KT * SEQ)
    hT = hT_t[:, :].rearrange("p (k t) -> p k t", k=KT)
    oT_t = sb("oT", 12 * SEQ)
    oT = oT_t[:, :].rearrange("p (k t) -> p k t", k=12)
    wsl_t = sb("w_slots", 4 * KT * P)
    wsl = wsl_t[:, :].rearrange("p (s k n) -> p s k n", s=4, k=KT)
    gains = sb("gains", 64)
    band = sb("band", HEADS * 256)
    small = sb("small", 256)
    gen_f = small[:, 250:251]
    wait_marks = small[0:1, 60:160]
    gen_i = sb("gen_i", 1, I32)
    work = sb("work", 24500)
    PS = ctx.enter_context(nc.psum_tensor("PS", [P, 8, HALF], F32))

    def carve(*widths):
        at, out = 0, []
        for w in widths:
            out.append(work[:, at:at + w])
            at += w
        assert at <= 24500, at
        return out

    x1_dram = nc.dram_tensor("x1_scratch", (SEQ, D), F32, kind="Internal").ap()
    skew_dram = nc.dram_tensor("skew_scratch", (P * HEADS * SKEW + P,), F32, kind="Internal").ap()
    memT1_dram = nc.dram_tensor("memT1_scratch", (P, KT * MEM), F32, kind="Internal").ap()

    eng_pe, eng_act, eng_dve = nc.tensor, nc.scalar, nc.vector

    def project(kind, w, b, memT):
        if kind == "feat":
            for c in range(2):
                for k in range(KT):
                    ins = nc.tensor.matmul(PS[:, b + c, :], w[:, k, :], hT[:, k, c * HALF:(c + 1) * HALF],
                                           start=k == 0, stop=k == KT - 1)
        elif kind.startswith("tok"):
            width = int(kind[3:] or P)
            for t in range(QB):
                for k in range(KT):
                    ins = nc.tensor.matmul(PS[:, b + t // 4, (t % 4) * P:(t % 4) * P + width],
                                           hT[:, k, t * P:(t + 1) * P], w[:, k, 0:width],
                                           start=k == 0, stop=k == KT - 1)
        elif kind == "memk":
            for k in range(KT):
                ins = nc.tensor.matmul(PS[:, b, 0:MEM], w[:, k, :], memT[:, k, :], start=k == 0, stop=k == KT - 1)
        else:
            for t in range(MEM // P):
                for k in range(KT):
                    ins = nc.tensor.matmul(PS[:, b, t * P:(t + 1) * P], memT[:, k, t * P:(t + 1) * P],
                                           w[:, k, :], start=k == 0, stop=k == KT - 1)
        return ins

    def norm_stage(jobs, m1_out, next_queue):
        MT = MEM // P
        NT = QB + MT
        xs, sq, memT_w, memT1_w = carve(NT * D, D, KT * MEM, KT * MEM)
        xs = xs.rearrange("p (t d) -> p t d", t=NT)
        memT = memT_w.rearrange("p (k t) -> p k t", k=KT)
        memT1 = memT1_w.rearrange("p (k t) -> p k t", k=KT)
        stat, rstd = small[:, 0:NT], small[:, 16:16 + NT]
        names = ("const", "gain", "sq", "var", "rt", "xn", "tr", "ev_act", "ev_dve", "m1", "job", "job_ev")
        (const_in, gain_in, sq_done, var_done, rt_done, xn_done, tr_done, ev_act, ev_dve, m1_done, job_done, job_ev) = (
            sem("n_" + n) for n in names)
        x_in = [sem(f"n_x{t}") for t in range(NT)]
        queue = weight_queue("m0", jobs)
        NJ = len(jobs)
        with nc.Block() as block:
            @block.sync
            def _(sp):
                for t in range(NT):
                    src = a["mem"][t * P:(t + 1) * P, :] if t < MT else a["x"][(t - MT) * P:(t - MT + 1) * P, :]
                    sp.dma_start(xs[:, t, :], src).then_inc(x_in[t], 16)
                    if t == 0:
                        sp.dma_start(consts[:, :], a["const_tables"]).then_inc(const_in, 16)
                        with nc.allow_non_contiguous_dma(reason="gains, one per partition"):
                            for g, src in ((0, a["norm_pre"][0]), (8, a["mem_norm"][0]), (24, a["mem_norm"][1]), (32, a["norm_pre"][1])):
                                sp.dma_start(gains[:, g:g + KT], src.rearrange("(k p) -> p k", p=P)).then_inc(gain_in, 16)
                    if 2 <= t < 6:
                        queue["send"](sp, t - 2)
                sp.dma_start(table[:, :], a["rel_bias_table"].rearrange("b h -> (b h)").partition_broadcast(P)).then_inc(const_in, 16)
                for m in range(4, NJ):
                    sp.wait_ge(job_done, m - 3)
                    queue["send"](sp, m)
                sp.wait_ge(m1_done, 1)
                sp.dma_start(memT1_dram, memT1_w).then_inc(m1_out, 16)
                for m in range(4):
                    sp.wait_ge(job_done, NJ - 3 + m)
                    next_queue["send"](sp, m)
                sp.wait_ge(const_in, 32)

            @block.scalar
            def _(act):
                def root(t):
                    act.wait_ge(var_done, t + 1)
                    nc.scalar.activation(rstd[:, t:t + 1], stat[:, t:t + 1], ACT.Sqrt).then_inc(rt_done, 1)

                def copy(t):
                    if t >= MT:
                        act.wait_ge(tr_done, 2 * t + 1)
                        cut = slice((t - MT) * P, (t - MT + 1) * P)
                        for k in range(4):
                            ins = nc.scalar.activation(hT[:, k, cut], PS[:, 2 * (t % 2), k * P:(k + 1) * P], ACT.Copy, scale=gains[:, k:k + 1])
                        ins.then_inc(ev_act, 1)
                    if t >= MT and t - MT < NJ:
                        j = t - MT
                        act.wait_ge(job_done, j + 1)
                        jobs[j][2](act, PS[:, 4 + 2 * (j % 2):6 + 2 * (j % 2), :]).then_inc(job_ev, 1)

                for t in range(NT):
                    act.wait_ge(x_in[t], 16)
                    if t:
                        act.wait_ge(sq_done, t)
                    nc.scalar.activation(sq, xs[:, t, :], ACT.Square, accum_out=stat[:, t:t + 1]).then_inc(sq_done, 1)
                    if t >= 1:
                        root(t - 1)
                    if t == LAG:
                        act.wait_ge(gain_in, 64)
                    if t >= LAG:
                        copy(t - LAG)
                root(NT - 1)
                for t in range(NT - LAG, NT):
                    copy(t)

            @block.vector
            def _(dve):
                def scale(t):
                    dve.wait_ge(rt_done, t + 1)
                    nc.vector.tensor_scalar(xs[:, t, :], xs[:, t, :], rstd[:, t:t + 1], None, ALU.mult).then_inc(xn_done, 1)

                def copy(t):
                    b = 2 * (t % 2)
                    if t >= MT:
                        dve.wait_ge(tr_done, 2 * t + 2)
                        nc.vector.tensor_tensor(hT[:, 4:8, (t - MT) * P:(t - MT + 1) * P], PS[:, b + 1, :].rearrange("p (k n) -> p k n", k=4),
                                                gains[:, 4:8].unsqueeze(2).to_broadcast([P, 4, P]), ALU.mult).then_inc(ev_dve, 1)
                        return
                    cut = slice(t * P, (t + 1) * P)
                    for h in range(2):
                        dve.wait_ge(tr_done, 2 * t + h + 1)
                        src = PS[:, b + h, :].rearrange("p (k n) -> p k n", k=4)
                        for dst, g in ((memT, 8), (memT1, 24)):
                            ins = nc.vector.tensor_tensor(dst[:, 4 * h:4 * h + 4, cut], src,
                                                          gains[:, g + 4 * h:g + 4 * h + 4].unsqueeze(2).to_broadcast([P, 4, P]), ALU.mult)
                    ins.then_inc(ev_dve, 1)
                    if t == MT - 1:
                        dve.drain().then_inc(m1_done, 1)

                for t in range(NT):
                    st = stat[:, t:t + 1]
                    dve.wait_ge(sq_done, t + 1)
                    nc.vector.tensor_scalar(st, st, 1.0 / D, EPS, ALU.mult, ALU.add)
                    dve.drain()
                    nc.vector.reciprocal(st, st).then_inc(var_done, 1)
                    if t >= 1:
                        scale(t - 1)
                    if t == LAG:
                        dve.wait_ge(gain_in, 64)
                    if t >= LAG:
                        copy(t - LAG)
                scale(NT - 1)
                for t in range(NT - LAG, NT):
                    copy(t)

            @block.tensor
            def _(pe):
                pe.wait_ge(const_in, 16)
                for t in range(NT):
                    pe.wait_ge(xn_done, t + 1)
                    if t >= 2:
                        pe.wait_ge(ev_dve, t - 1)
                        if t - 2 >= MT:
                            pe.wait_ge(ev_act, t - 1 - MT)
                    for k in range(KT):
                        ins = nc.tensor.transpose(PS[:, 2 * (t % 2) + k // 4, (k % 4) * P:(k % 4 + 1) * P],
                                                  xs[:, t, k * P:(k + 1) * P], ident)
                        if k % 4 == 3:
                            ins.then_inc(tr_done, 1)
                    if MT <= t < MT + NJ:
                        j = t - MT
                        pe.wait_ge(ev_dve, MT)
                        pe.wait_ge(queue["w_in"][j % 4], 16 * (j // 4 + 1))
                        if j >= 2:
                            pe.wait_ge(job_ev, j - 1)
                        project(jobs[j][1], wsl[:, j % 4], 4 + 2 * (j % 2), memT).then_inc(job_done, 1)

    def weight_queue(tag, jobs, kept=()):
        w_in = [kept_sem(f"{tag}w_in{s}") for s in range(4)]
        used = [n for n, job in enumerate(jobs) if job[0]]

        def send(sp, m):
            for dst, src in jobs[used[m]][0](wsl[:, m % 4]):
                sp.dma_start(dst, src).then_inc(w_in[m % 4], 16)
        return dict(w_in=w_in, used=used, send=send, first=lambda sp: [send(sp, m) for m in range(4)])

    def project_stage(tag, jobs, queue, memT, dve_side, sp_side, mem_in=None, pool_side=None):
        w_in, used = queue["w_in"], queue["used"]
        pe_done, ev_done = sem(tag + "pe"), sem(tag + "ev")
        with nc.Block() as block:
            @block.sync
            def _(sp):
                sp_side(sp)
                for m in range(4, len(used)):
                    sp.wait_ge(pe_done, used[m - 4] + 1)
                    queue["send"](sp, m)

            @block.tensor
            def _(pe):
                loaded = [0] * 4
                for n, (loads, kind, _) in enumerate(jobs):
                    if n >= 2:
                        pe.wait_ge(ev_done, n - 1)
                    b = 2 * (n % 2)
                    if loads:
                        m = used.index(n) % 4
                        w = wsl[:, m]
                        loaded[m] += 16 * len(loads(w))
                        pe.wait_ge(w_in[m], loaded[m])
                    if mem_in is not None and not callable(kind) and kind[:3] == "mem" and not any(
                            not callable(j[1]) and j[1][:3] == "mem" for j in jobs[:n]):
                        pe.wait_ge(mem_in, 16)
                    if callable(kind):
                        ins = kind(pe, b)
                    else:
                        ins = project(kind, w, b, memT)
                    ins.then_inc(pe_done, 1)

            @block.scalar
            def _(act):
                for n, (_, kind, evac) in enumerate(jobs):
                    act.wait_ge(pe_done, n + 1)
                    evac(act, PS[:, 2 * (n % 2):2 * (n % 2) + 2, :]).then_inc(ev_done, 1)

            @block.vector
            def _(dve):
                dve_side(dve)

            if pool_side:
                @block.gpsimd
                def _(pool):
                    pool_side(pool)

    def cols(w, *runs):
        v = w.rearrange("(k p) n -> p k n", p=P)
        return lambda slot: [(slot[:, :, s:s + n], v[:, :, c:c + n]) for s, c, n in runs]

    def copy_out(dst):
        return lambda act, ps: nc.scalar.activation(dst, ps, ACT.Copy)

    def flat2(view):
        return view.rearrange("p (c n) -> p c n", c=2)

    def position_rows(dve, pos_row, pos_col, row_hi, row_lo, col_hi, col_lo, tmp):
        for src, hi, lo, t in ((pos_row, row_hi, row_lo, tmp), (pos_col, col_hi, col_lo, tmp[:, 0:QB])):
            nc.vector.tensor_scalar(t, src, 16, None, ALU.arith_shift_right)
            dve.drain()
            nc.vector.tensor_copy(hi, t)
            dve.drain()
            nc.vector.tensor_scalar(t, src, 65535, None, ALU.bitwise_and)
            dve.drain()
            nc.vector.tensor_copy(lo, t)
            dve.drain()

    def bias_block(dve, rows, qb, k0, width, dsts, heads, scratch, loop):
        row_hi, row_lo, col_hi, col_lo = rows
        diff, bkt, hot = (s[:, 0:width] for s in scratch)
        ks = slice(k0, k0 + width)
        nc.vector.tensor_scalar(diff, row_hi[:, ks], col_hi[:, qb:qb + 1], 65536.0, ALU.subtract, ALU.mult)
        nc.vector.memset(bkt, 0.0)
        dve.drain()
        nc.vector.scalar_tensor_tensor(out=diff, in0=row_lo[:, ks], scalar=col_lo[:, qb:qb + 1], in1=diff,
                                       op0=ALU.subtract, op1=ALU.add)
        dve.drain()

        def raise_bucket(thr):
            nc.vector.scalar_tensor_tensor(out=bkt, in0=diff, scalar=thr, in1=bkt, op0=ALU.is_le, op1=ALU.add)
            dve.drain()

        def pick(col, entry):
            nc.vector.tensor_scalar(hot, bkt, col, -1.0, ALU.is_equal, ALU.mult)
            dve.drain()
            for d, e in zip(dsts, entry):
                nc.vector.scalar_tensor_tensor(out=d, in0=hot, scalar=e, in1=d, op0=ALU.mult, op1=ALU.add)
            dve.drain()

        for d in dsts:
            nc.vector.memset(d, 0.0)
        dve.drain()
        if loop:
            with dve.Fori(1, NB) as b:
                raise_bucket(consts[:, bass.ds(b + C_NTHR, 1)])
            with dve.Fori(0, NB) as b:
                pick(consts[:, bass.ds(b + C_BKT, 1)], [table[:, bass.ds(b * HEADS + h, 1)] for h in heads])
        else:
            for b in range(1, NB):
                raise_bucket(consts[:, C_NTHR + b:C_NTHR + b + 1])
            for b in range(NB):
                pick(consts[:, C_BKT + b:C_BKT + b + 1], [table[:, b * HEADS + h:b * HEADS + h + 1] for h in heads])

    def add_to(dst, mask):
        nc.vector.tensor_tensor(dst, dst, mask, ALU.add)

    TP, OB, FILL, FILL_GAP, PIECES = (4, 6), 5, 7, 1, 4

    def attention_stage(tag, tracks, loads, proj_jobs=(), setup_dve=None, head_dve=None, stage_pool=None):
        units, at, owner, fins, col = [], 0, [None] * 4, 0, 0
        for qb in range(QB):
            for tr in tracks:
                for hf in range(tr["halves"]):
                    ulist = tr["parts"](qb)
                    f_cols = {}
                    for kind in tr["kinds"]:
                        f_cols[kind] = col
                        col += 1
                    for un, plist in enumerate(ulist):
                        total = sum(n for _, n in plist)
                        banks = 2 if total > HALF else 1
                        if "bank_of" in tr:
                            at = tr["bank_of"](qb, hf)
                        if banks == 2 and at % 2:
                            at = (at + 1) % 4
                        prev = max((owner[b] for b in range(at, at + banks) if owner[b] is not None), default=None)
                        for b in range(at, at + banks):
                            owner[b] = len(units)
                        parts, off = [], 0
                        for kind, n in plist:
                            parts.append(dict(kind=kind, n=n, off=off, qb=qb, hf=hf, col=f_cols[kind],
                                              slot=tr["kinds"].index(kind)))
                            off += n
                        units.append(dict(tr=tr, qb=qb, hf=hf, parts=parts, bank=at, banks=banks, prev=prev, total=total,
                                          fin=fins if un == len(ulist) - 1 else None, f=fins, c0=col - len(tr["kinds"])))
                        at = (at + banks) % 4
                    fins += 1
        NU, NF, NCOL = len(units), fins, col
        g = 0
        for u in units:
            tiles = []
            for p in u["parts"]:
                for t in range(-(-p["n"] // P)):
                    tiles.append((p["off"] + t * P, min(P, p["n"] - t * P), p, t))
            u["tiles"] = tiles
            u["g0"], g = g, g - (-len(tiles) // 4)
            u["g1"] = g
        fin_unit = {u["fin"]: n for n, u in enumerate(units) if u["fin"] is not None}
        steps_n = NU + LOOK + OUT_LAG
        outs_at = {}
        for qb in range(QB):
            for k, tr in enumerate(tracks):
                last = max(n for n, u in enumerate(units) if u["qb"] == qb and u["tr"] is tr)
                outs_at.setdefault(last + LOOK + OUT_LAG, []).append((qb, k))
        order = []
        for s in range(steps_n):
            if 0 <= s - LOOK < NU:
                u = units[s - LOOK]
                order += [("p", s - LOOK, n) for n in range(u["g1"] - u["g0"])]
            order += [("o", qb, k) for qb, k in outs_at.get(s, [])]
        NE = len(order)
        index = {e: n for n, e in enumerate(order)}
        last_t = {v: index[("p", v, units[v]["g1"] - units[v]["g0"] - 1)] for v in range(NU)}
        last_of = [max(n for n, u in enumerate(units) if u["qb"] == qb and u["tr"]["bias"]) if any(t["bias"] for t in tracks) else 0
                   for qb in range(QB)]
        gate_jobs = [(tr["gate_w"], c, k, "gate") for c in range(2) for k, tr in enumerate(tracks)]
        next_jobs = [(tr["next_w"], c, k, "next") for c in range(2) for k, tr in enumerate(tracks) if tr.get("next_w") is not None]
        NJF = len(gate_jobs) + len(next_jobs)
        NG = len(gate_jobs)

        widths = (3 * 1032, 4 * HALF, 2 * len(tracks) * P, 192, NCOL, NCOL, NCOL, 2 * len(tracks) * HALF)
        region, gate_x = tracks[0]["bufs"], tracks[0]["gate_x"]
        assert sum(widths) <= region.shape[1], (tag, widths, region.shape)
        cut, views = 0, []
        for w in widths:
            views.append(region[:, cut:cut + w])
            cut += w
        p_sb, pt_sb, o_sb, pv_scr, negmax, rowsum, coef, sil = views
        p_sb = p_sb.rearrange("p (s n) -> p s n", s=3)
        pt_sb = pt_sb.rearrange("p (s n) -> p s n", s=4)
        o_sb = o_sb.rearrange("p (k s n) -> p k s n", k=len(tracks), s=2)
        sil = sil.rearrange("p (j n) -> p j n", j=NG)

        names = ("w", "proj", "proj_act", "proj_dve", "qk", "max", "exp", "tr", "ev", "pv", "fin", "fill", "fill_exp", "fill_ev", "silu",
                 "setup", "bias", "sink")
        (w_in, proj_done, proj_act, proj_dve, qk_done, max_done, exp_done, tr_done, ev_done, pv_done, fin_done,
         fill_done, fill_exp, fill_ev, silu_done, setup_done, bias_done, sink_set) = (sem(tag + n) for n in names)
        gw_in = [sem(f"{tag}gw{k}") for k in range(len(tracks))]
        nw_in = [sem(f"{tag}nw{k}") for k in range(len(tracks))]
        n_loads = len(loads(0)) if proj_jobs else 0
        NJ = len(proj_jobs)
        act_jobs = [j for j in range(NJ) if proj_jobs[j][1]]
        dve_jobs = [j for j in range(NJ) if proj_jobs[j][2]]
        NA, ND = len(act_jobs), len(dve_jobs)
        sinks = next((tr["sink"] for tr in tracks if tr.get("sink")), None)
        SINK = 2 * P
        STEPS = 4

        def part_logits(u, p):
            n, b = p["n"], u["bank"]
            if u["tr"].get("sink"):
                return PS[:, b, SINK - n:SINK + 1]
            if u["banks"] == 2:
                return PS[:, b:b + 2, :].rearrange("p b n -> p (b n)")[:, p["off"]:p["off"] + n]
            return PS[:, b, p["off"]:p["off"] + n]

        sink_banks = {u["bank"]: u["hf"] for u in units if u["tr"].get("sink")}
        for u in units:
            assert not u["tr"].get("sink") or sink_banks[u["bank"]] == u["hf"]

        def body_jobs(last):
            return gate_jobs + ([] if last else next_jobs)

        def uses_in(s):
            return (units[s - LOOK]["g1"] - units[s - LOOK]["g0"] if 0 <= s - LOOK < NU else 0) + len(outs_at.get(s, []))

        def fill_plan(last):
            jobs = body_jobs(last)
            first_at = {}
            e = 0
            for s in range(steps_n):
                first_at[s] = e
                e += uses_in(s)
            step_of = [n for n in range(steps_n) for _ in range(uses_in(n))]
            total = len(jobs) * KT
            plan_, at_e = [[] for _ in range(NE)], 0
            for x in range(total):
                job, m = divmod(x, KT)
                w, c, k, what = jobs[job]
                at_e = max(at_e, x * NE // total)
                if m == 0 and job:
                    at_e = max(at_e, first_at[step_of[at_last] + FILL_GAP])
                if m == KT - 1 and what == "next":
                    lastq = max(n for n, u in enumerate(units) if u["tr"] is tracks[k] and u["qb"] < 4 * (c + 1))
                    at_e = max(at_e, first_at[lastq])
                plan_[at_e].append((job, m))
                at_last = at_e
            return plan_

        def fill_end_step(last):
            plan_, at_step, e = fill_plan(last), {}, 0
            for s in range(steps_n):
                for _ in range(uses_in(s)):
                    for job, m in plan_[e]:
                        if m == KT - 1:
                            at_step.setdefault(s, []).append(job)
                    e += 1
            return at_step

        def gate_work(last):
            ended = fill_end_step(last)
            end_of = {job: s for s, l in ended.items() for job in l if job < NG}
            todo, stands = {}, {}
            for job in range(NG):
                room = min(end_of[job + 1] - end_of[job] if job + 1 < NG else PIECES, PIECES)
                assert room > 0
                for p in range(PIECES):
                    s = min(end_of[job] + p * room // PIECES, steps_n - 1)
                    todo.setdefault(s, []).append(("piece", job, p))
                stands[job] = s
            for job in range(NG):
                _, c, k, _ = gate_jobs[job]
                ready = next(s for s, l in outs_at.items() if (4 * c + 3, k) in l)
                todo.setdefault(max(ready, stands[job]), []).append(("product", job, k))
            return todo

        def each_step(engine, body):
            with engine.Fori(0, STEPS - 1) as i:
                body(i, False)
            body(STEPS - 1, True)

        with nc.Block() as block:
            @block.sync
            def _(sp):
                def send(what, done):
                    for dst, src in what:
                        sp.dma_start(dst, src).then_inc(done, 16)

                def gates(i):
                    for k, tr in enumerate(tracks):
                        send(tr["gate_loads"](i), gw_in[k])

                def queries(i):
                    for k, tr in enumerate(tracks):
                        if tr.get("next_w") is not None:
                            send(tr["next_loads"](i), nw_in[k])

                def again(i, with_queries):
                    if proj_jobs:
                        sp.wait_ge(proj_done, i * NJ + NJ)
                        send(loads(i + 1), w_in)
                    sp.wait_ge(fill_done, i * NJF + NG)
                    gates(i + 1)
                    if with_queries and next_jobs:
                        sp.wait_ge(fill_done, i * NJF + NJF)
                        queries(i + 2)
                if proj_jobs:
                    send(loads(0), w_in)
                gates(0)
                queries(1)
                with sp.Fori(0, STEPS - 2) as i:
                    again(i, True)
                again(STEPS - 2, False)

            @block.tensor
            def _(pe):
                def step(i, last):
                    plan_ = fill_plan(last)
                    jobs = body_jobs(last)

                    def fill(e):
                        for job, m in plan_[e]:
                            w, c, k, what = jobs[job]
                            if m == 0:
                                tr = tracks[k]
                                if c == 0:
                                    nl = 16 * len(tr[what + "_loads"](0))
                                    pe.wait_ge((gw_in if what == "gate" else nw_in)[k], i * nl + nl)
                                if job:
                                    pe.wait_ge(fill_ev, i * NJF + job)
                            ins = nc.tensor.matmul(PS[:, FILL, :], w[:, m, :], hT[:, m, c * HALF:(c + 1) * HALF], start=m == 0, stop=m == KT - 1)
                            if m == KT - 1:
                                ins.then_inc(fill_done, 1)

                    if proj_jobs:
                        pe.wait_ge(w_in, i * (16 * n_loads) + 16 * n_loads)
                        for j, (emit, _, _) in enumerate(proj_jobs):
                            if j >= 8:
                                pe.wait_ge(proj_act, i * NA + sum(x <= j - 8 for x in act_jobs))
                                if any(x <= j - 8 for x in dve_jobs):
                                    pe.wait_ge(proj_dve, i * ND + sum(x <= j - 8 for x in dve_jobs))
                            emit(j % 8, i).then_inc(proj_done, 1)
                        pe.wait_ge(proj_act, i * NA + NA)
                        if ND:
                            pe.wait_ge(proj_dve, i * ND + ND)
                    if sinks:
                        pe.wait_ge(sink_set, i + 1)
                    e = 0
                    for s in range(steps_n):
                        if s < NU:
                            u = units[s]
                            if u["prev"] is not None:
                                pe.wait_ge(exp_done, i * NU + (u["prev"] + 1))
                            for p in u["parts"]:
                                start = SINK - p["n"] if u["tr"].get("sink") else p["off"]
                                c = 0
                                while c < p["n"]:
                                    b, o = divmod(start + c, HALF)
                                    w = min(HALF - o, p["n"] - c)
                                    ins = nc.tensor.matmul(PS[:, u["bank"] + b, o:o + w], u["tr"]["q_ap"](u["qb"], u["hf"]),
                                                           u["tr"]["k_ap"](p, i, c, w), start=True, stop=True)
                                    c += w
                            ins.then_inc(qk_done, 1)
                        v = s - LOOK - 1
                        if 0 <= v < NU:
                            u = units[v]
                            pe.wait_ge(ev_done, i * NE + (last_t[v] + 1))
                            if u["f"] >= 1:
                                pe.wait_ge(fin_done, i * NF + u["f"])
                            hw = u["tr"]["head_w"]
                            for n, (c, w, p, t) in enumerate(u["tiles"]):
                                o = PS[:, OB, p["slot"] * hw:(p["slot"] + 1) * hw]
                                ins = nc.tensor.matmul(o, pt_sb[0:w, (u["g0"] + n // 4) % 4, (n % 4) * P:(n % 4 + 1) * P],
                                                       u["tr"]["v_ap"](p, t, i, w), start=t == 0, stop=(t + 1) * P >= p["n"])
                            ins.then_inc(pv_done, 1)
                        v = s - LOOK
                        if 0 <= v < NU:
                            u = units[v]
                            pe.wait_ge(exp_done, i * NU + (v + 1))
                            for gg in range(u["g1"] - u["g0"]):
                                if e >= 2:
                                    pe.wait_ge(ev_done, i * NE + (e - 1))
                                for n, (c, w, p, t) in enumerate(u["tiles"][4 * gg:4 * gg + 4]):
                                    ins = nc.tensor.transpose(PS[:, TP[e % 2], n * P:(n + 1) * P], p_sb[:, v % 3, c:c + P], ident)
                                ins.then_inc(tr_done, 1)
                                fill(e)
                                e += 1
                        for qb, k in outs_at.get(s, []):
                            f = max(u["f"] for u in units if u["qb"] == qb and u["tr"] is tracks[k])
                            pe.wait_ge(fin_done, i * NF + (f + 1))
                            pe.wait_ge(ev_done, i * NE + (e - 1))
                            nc.tensor.transpose(PS[:, TP[e % 2], 0:P], o_sb[:, k, qb % 2, :], ident).then_inc(tr_done, 1)
                            fill(e)
                            e += 1
                    pe.wait_ge(ev_done, i * NE + NE)
                    pe.wait_ge(fill_ev, i * NJF + len(jobs))
                each_step(pe, step)

            @block.scalar
            def _(act):
                def step(i, last):
                    jobs, ended = body_jobs(last), fill_end_step(last)
                    for j in act_jobs:
                        act.wait_ge(proj_done, i * NJ + (j + 1))
                        proj_jobs[j][1](j % 8).then_inc(proj_act, 1)
                    e = 0
                    for s in range(steps_n):
                        v = s - LOOK
                        if 0 <= v < NU:
                            u = units[v]
                            for gg in range(u["g1"] - u["g0"]):
                                act.wait_ge(tr_done, i * NE + (e + 1))
                                G = u["g0"] + gg
                                if G >= 4:
                                    old = next(n for n, x in enumerate(units) if x["g0"] <= G - 4 < x["g1"])
                                    act.wait_ge(pv_done, i * NU + (old + 1))
                                tiles = u["tiles"][4 * gg:4 * gg + 4]
                                nc.scalar.activation(pt_sb[:, G % 4, 0:len(tiles) * P], PS[:, TP[e % 2], 0:len(tiles) * P],
                                                     ACT.Copy).then_inc(ev_done, 1)
                                e += 1
                        for qb, k in outs_at.get(s, []):
                            act.wait_ge(tr_done, i * NE + (e + 1))
                            nc.scalar.activation(oT[:, bass.ds(i + tracks[k]["o_tile"], 1), qb * P:(qb + 1) * P].rearrange("p a n -> p (a n)"),
                                                 PS[:, TP[e % 2], 0:P], ACT.Copy).then_inc(ev_done, 1)
                            e += 1
                        if s < NU:
                            u = units[s]
                            act.wait_ge(max_done, i * NU + (s + 1))
                            if s >= 3:
                                act.wait_ge(tr_done, i * NE + (last_t[s - 3] + 1))
                            for p in u["parts"]:
                                w = p["n"] + (1 if u["tr"].get("sink") else 0)
                                ins = nc.scalar.activation(p_sb[:, s % 3, p["off"]:p["off"] + w], part_logits(u, p), ACT.Exp,
                                                           bias=negmax[:, p["col"]:p["col"] + 1], scale=-1.0,
                                                           accum_out=rowsum[:, p["col"]:p["col"] + 1])
                            ins.then_inc(exp_done, 1)
                        for job in ended.get(s, []):
                            w, c, k, what = jobs[job]
                            act.wait_ge(fill_done, i * NJF + (job + 1))
                            if what == "gate":
                                nc.scalar.activation(sil[:, job, :], PS[:, FILL, :], ACT.Exp, scale=-1.0).then_inc(fill_exp, 1)
                                if job:
                                    act.wait_ge(silu_done, i * NG + job)
                                nc.scalar.activation(gate_x, PS[:, FILL, :], ACT.Copy).then_inc(fill_ev, 1)
                            else:
                                tracks[k]["next_out"](PS[:, FILL, :], c).then_inc(fill_ev, 1)
                each_step(act, step)

            if stage_pool:
                @block.gpsimd
                def _(pool):
                    if setup_dve:
                        pool.wait_ge(setup_done, 1)
                    gen = pool.value_load(gen_i[0:1, 0:1], min_val=0, max_val=1)

                    def stage(qb, i):
                        with pool.If(gen == 0):
                            stage_pool(qb, i)
                        with pool.Else():
                            pool.nop()
                        pool.drain().then_inc(bias_done, 1)

                    for qb in range(QB):
                        stage(qb, 0)
                    with pool.Fori(0, STEPS - 1) as i:
                        for qb in range(QB):
                            pool.wait_ge(max_done, i * NU + (last_of[qb] + 1))
                            nc.gpsimd.tensor_tensor(wait_marks[:, 99 - qb:100 - qb], ident[0:1, 0:1], ident[0:1, 0:1], ALU.add)
                            stage(qb, i + 1)

            @block.vector
            def _(dve):
                if any("cmp" in tr["kinds"] for tr in tracks):
                    nc.vector.memset(p_sb[:, :, :], 0.0)
                    dve.drain()
                if setup_dve:
                    setup_dve(dve).then_inc(setup_done, 1)
                gen = dve.value_load(gen_i[0:1, 0:1], min_val=0, max_val=1) if head_dve else None

                def step(i, last):
                    jobs, gate_jobs_at = body_jobs(last), gate_work(last)
                    if head_dve:
                        head_dve(dve, gen, i)
                    for j in dve_jobs:
                        dve.wait_ge(proj_done, i * NJ + (j + 1))
                        proj_jobs[j][2](dve, j % 8).then_inc(proj_dve, 1)
                    if sinks:
                        pair = sinks(i)
                        for b, hf in sink_banks.items():
                            ins = nc.vector.tensor_copy(PS[:, b, SINK:SINK + 1], pair[:, hf:hf + 1])
                        ins.then_inc(sink_set, 1)
                    marks = 0
                    for s in range(steps_n):
                        if s < NU:
                            u = units[s]
                            dve.wait_ge(qk_done, i * NU + (s + 1))
                            if u["tr"]["bias"]:
                                if not any(x["qb"] == u["qb"] and x["tr"]["bias"] for x in units[:s]):
                                    dve.wait_ge(bias_done, i * QB + (u["qb"] + 1))
                                nc.vector.memset(wait_marks[:, marks:marks + 1], 0.0)
                                marks += 1
                            for p in u["parts"]:
                                lg, mn, n = part_logits(u, p), negmax[:, p["col"]:p["col"] + 1], p["n"]
                                if u["tr"]["bias"]:
                                    if p["kind"] == "win" and u["qb"] >= 4:
                                        nc.vector.tensor_tensor(lg[:, 0:P], lg[:, 0:P], winmask, ALU.add)
                                        dve.drain()
                                    ins = nc.vector.tensor_tensor_reduce(out=lg, in0=lg, in1=u["tr"]["bias"](p), scale=1.0,
                                                                         scalar=3e38, op0=ALU.add, op1=ALU.min, accum_out=mn)
                                    if p["kind"] == "cmp" and u["qb"] == 0:
                                        dve.drain()
                                        ins = nc.vector.tensor_scalar(mn, mn, 1e29, None, ALU.min)
                                else:
                                    if p["kind"] == "mla":
                                        nc.vector.tensor_tensor(lg[:, n - P:n], lg[:, n - P:n], causal, ALU.add)
                                        dve.drain()
                                    ins = nc.vector.tensor_reduce(out=mn, in_=lg, op=ALU.min, axis=AX.X)
                            ins.then_inc(max_done, 1)
                        v = s - LOOK
                        if 0 <= v < NU and units[v]["fin"] is not None:
                            u = units[v]
                            NK = len(u["tr"]["kinds"])
                            rs, cf = rowsum[:, u["c0"]:u["c0"] + NK], coef[:, u["c0"]:u["c0"] + NK]
                            dve.wait_ge(exp_done, i * NU + (v + 1))
                            if "cmp" in u["tr"]["kinds"] and u["qb"] == 0:
                                nc.vector.tensor_scalar(rs, rs, 1e-30, None, ALU.max)
                                dve.drain()
                            nc.vector.reciprocal(cf, rs)
                            if u["tr"].get("gate"):
                                dve.drain()
                                nc.vector.tensor_tensor(cf, cf, u["tr"]["gate"](u["qb"], u["hf"], i), ALU.mult)
                        v = s - LOOK - 1
                        if 0 <= v < NU and units[v]["fin"] is not None:
                            u = units[v]
                            NK, hw = len(u["tr"]["kinds"]), u["tr"]["head_w"]
                            k = next(n for n, t in enumerate(tracks) if t is u["tr"])
                            cf = coef[:, u["c0"]:u["c0"] + NK]
                            o_ps = PS[:, OB, 0:NK * hw]
                            dst = o_sb[:, k, u["qb"] % 2, u["hf"] * hw:(u["hf"] + 1) * hw]
                            if u["hf"] == 0 and u["qb"] >= 2:
                                dve.wait_ge(tr_done, i * NE + (index[("o", u["qb"] - 2, k)] + 1))
                                nc.vector.memset(wait_marks[:, 40:41], 0.0)
                            dve.drain()
                            dve.wait_ge(pv_done, i * NU + (v + 1))
                            if NK > 1:
                                nc.vector.tensor_tensor(pv_scr.rearrange("p (k d) -> p k d", k=NK),
                                                        o_ps.rearrange("p (k d) -> p k d", k=NK),
                                                        cf.unsqueeze(2).to_broadcast([P, NK, hw]), ALU.mult)
                                dve.drain()
                                nc.vector.tensor_reduce(out=dst, in_=pv_scr.rearrange("p (k d) -> p d k", k=NK),
                                                        op=ALU.add, axis=AX.X).then_inc(fin_done, 1)
                            else:
                                nc.vector.tensor_scalar(dst, o_ps, cf, None, ALU.mult).then_inc(fin_done, 1)
                        for what, job, p in gate_jobs_at.get(s, []):
                            sl = sil[:, job, :]
                            if what == "product":
                                _, c, k, _ = gate_jobs[job]
                                dve.wait_ge(ev_done, i * NE + (index[("o", 4 * c + 3, k)] + 1))
                                nc.vector.memset(wait_marks[:, 41:42], 0.0)
                                o = oT[:, bass.ds(i + tracks[k]["o_tile"], 1), c * HALF:(c + 1) * HALF].rearrange("p a n -> p (a n)")
                                dve.drain()
                                nc.vector.tensor_tensor(o, o, sl, ALU.mult)
                                continue
                            if p == 0:
                                dve.wait_ge(fill_exp, i * NG + (job + 1))
                                nc.vector.tensor_scalar(sl, sl, 1.0, None, ALU.add)
                                dve.drain()
                            cut = slice(p * (HALF // PIECES), (p + 1) * (HALF // PIECES))
                            nc.vector.reciprocal(sl[:, cut], sl[:, cut])
                            dve.drain()
                            if p == 0:
                                dve.wait_ge(fill_ev, i * NJF + (jobs.index(gate_jobs[job]) + 1))
                            ins = nc.vector.tensor_tensor(sl[:, cut], sl[:, cut], gate_x[:, cut], ALU.mult)
                            if p == PIECES - 1:
                                ins.then_inc(silu_done, 1)
                    dve.drain()

                each_step(dve, step)

    def output_stage(tag, w_out, tiles, row_runs, post_gain, x_src, out_dst, next_gain, also_load=None):
        wo_w, xt_w, y_w, g_w, sq_w, xn_w = carve(tiles * D, 2 * D, 2 * D, D, D, D)
        wo = wo_w.rearrange("p (k n) -> p k n", k=tiles)
        xt = xt_w.rearrange("p (s n) -> p s n", s=2)
        fused = next_gain is not None
        yt = y_w.rearrange("p (s n) -> p s n", s=2)
        stat, stat2 = small[:, 40:40 + QB], small[:, 50:50 + QB]
        wo_in = [sem(f"{tag}wo{k}") for k in range(tiles)]
        x_in = [sem(f"{tag}x{p}") for p in range(2)]
        g_in, out_done = sem(tag + "g"), [sem(f"{tag}out{p}") for p in range(2)]
        y_done, sq_done, var_done, rt_done, scaled, res_done, sq2, var2, rt2, xn_done, tr_done, hev_act, hev_dve = (
            sem(tag + n) for n in ("y", "sq", "var", "rt", "scaled", "res", "sq2", "var2", "rt2", "xn", "tr", "hev_act", "hev_dve"))
        row = lambda t: PS[:, 2 * (t % 2):2 * (t % 2) + 2, :].rearrange("p b n -> p (b n)")
        with nc.Block() as block:
            @block.sync
            def _(sp):
                for k in range(tiles):
                    for r0, r, n in row_runs(k):
                        sp.dma_start(wo[r0:r0 + n, k, :], w_out[r:r + n, :]).then_inc(wo_in[k], 16)
                sp.dma_start(g_w, post_gain.partition_broadcast(P)).then_inc(g_in, 16)
                if also_load:
                    also_load(sp)
                for t in range(QB):
                    if t >= 2:
                        sp.wait_ge(res_done, t - 1)
                    sp.dma_start(xt[:, t % 2, :], x_src[t * P:(t + 1) * P, :]).then_inc(x_in[t % 2], 16)
                    if t >= 1:
                        sp.wait_ge(res_done, t)
                        sp.dma_start(out_dst[(t - 1) * P:t * P, :], yt[:, (t - 1) % 2, :]).then_inc(out_done[(t - 1) % 2], 16)
                sp.wait_ge(res_done, QB)
                sp.dma_start(out_dst[(QB - 1) * P:QB * P, :], yt[:, (QB - 1) % 2, :]).then_inc(out_done[(QB - 1) % 2], 16)
                for p in range(2):
                    sp.wait_ge(out_done[p], 16 * (QB // 2))

            @block.tensor
            def _(pe):
                def transposes(t):
                    pe.wait_ge(xn_done, t + 1)
                    if t >= 2:
                        pe.wait_ge(hev_act, t - 1)
                        pe.wait_ge(hev_dve, t - 1)
                    for k in range(KT):
                        ins = nc.tensor.transpose(PS[:, 4 + 2 * (t % 2) + k // 4, (k % 4) * P:(k % 4 + 1) * P], xn_w[:, k * P:(k + 1) * P], ident)
                    ins.then_inc(tr_done, 1)

                for t in range(QB):
                    if t >= 2:
                        pe.wait_ge(scaled, t - 1)
                        pe.wait_ge(sq_done, t - 1)
                    for k in range(tiles):
                        if t == 0:
                            pe.wait_ge(wo_in[k], 16 * len(row_runs(k)))
                        for c in range(2):
                            ins = nc.tensor.matmul(PS[:, 2 * (t % 2) + c, :], oT[:, k, t * P:(t + 1) * P], wo[:, k, c * HALF:(c + 1) * HALF],
                                                   start=k == 0, stop=k == tiles - 1)
                    ins.then_inc(y_done, 1)
                    if fused and t >= 1:
                        transposes(t - 1)
                if fused:
                    transposes(QB - 1)

            @block.scalar
            def _(act):
                def copy(t):
                    act.wait_ge(tr_done, t + 1)
                    for k in range(4):
                        ins = nc.scalar.activation(hT[:, k, t * P:(t + 1) * P], PS[:, 4 + 2 * (t % 2), k * P:(k + 1) * P], ACT.Copy,
                                                   scale=next_gain[:, k:k + 1])
                    ins.then_inc(hev_act, 1)

                for t in range(QB):
                    act.wait_ge(y_done, t + 1)
                    act.drain()
                    nc.scalar.activation(sq_w, row(t), ACT.Square, accum_out=stat[:, t:t + 1]).then_inc(sq_done, 1)
                    act.wait_ge(var_done, t + 1)
                    nc.scalar.activation(stat[:, t:t + 1], stat[:, t:t + 1], ACT.Sqrt).then_inc(rt_done, 1)
                    if fused:
                        act.wait_ge(res_done, t + 1)
                        act.drain()
                        nc.scalar.activation(sq_w, yt[:, t % 2, :], ACT.Square, accum_out=stat2[:, t:t + 1]).then_inc(sq2, 1)
                        act.wait_ge(var2, t + 1)
                        nc.scalar.activation(stat2[:, t:t + 1], stat2[:, t:t + 1], ACT.Sqrt).then_inc(rt2, 1)
                        if t >= 1:
                            copy(t - 1)
                if fused:
                    copy(QB - 1)

            @block.vector
            def _(dve):
                def mean_root(st, before, after):
                    nc.vector.tensor_scalar(st, st, 1.0 / D, EPS, ALU.mult, ALU.add)
                    dve.drain()
                    nc.vector.reciprocal(st, st).then_inc(before, 1)

                def copy(t):
                    dve.wait_ge(tr_done, t + 1)
                    nc.vector.tensor_tensor(hT[:, 4:8, t * P:(t + 1) * P], PS[:, 5 + 2 * (t % 2), :].rearrange("p (k n) -> p k n", k=4),
                                            next_gain[:, 4:8].unsqueeze(2).to_broadcast([P, 4, P]), ALU.mult).then_inc(hev_dve, 1)

                dve.wait_ge(g_in, 16)
                for t in range(QB):
                    st, y = stat[:, t:t + 1], yt[:, t % 2, :]
                    dve.wait_ge(sq_done, t + 1)
                    mean_root(st, var_done, rt_done)
                    dve.wait_ge(rt_done, t + 1)
                    if t >= 2:
                        dve.wait_ge(out_done[t % 2], 16 * (t // 2))
                    nc.vector.scalar_tensor_tensor(out=y, in0=row(t), scalar=st, in1=g_w, op0=ALU.mult, op1=ALU.mult).then_inc(scaled, 1)
                    dve.wait_ge(x_in[t % 2], 16 * (t // 2 + 1))
                    dve.drain()
                    nc.vector.tensor_tensor(y, y, xt[:, t % 2, :], ALU.add).then_inc(res_done, 1)
                    if fused:
                        st2 = stat2[:, t:t + 1]
                        dve.wait_ge(sq2, t + 1)
                        mean_root(st2, var2, rt2)
                        dve.wait_ge(rt2, t + 1)
                        if t >= 1:
                            dve.wait_ge(tr_done, t)
                        nc.vector.tensor_scalar(xn_w, y, st2, None, ALU.mult).then_inc(xn_done, 1)
                        if t >= 1:
                            copy(t - 1)
                if fused:
                    copy(QB - 1)

    ln = lambda kind, qb: dict(mla=P * (qb + 1), slc=P * (qb + 1), win=P * min(qb + 1, 5), swa=P * min(qb + 1, 2),
                               mem=MEM, cmp=min(NC, 8 * (qb + 1) - 1))[kind]

    def of_model(w, i, col, width=P):
        return w.rearrange("(k p) n -> p k n", p=P)[:, :, bass.ds(i + col, width)]

    def plain_loads(w, col, slot):
        return lambda i: [(slot, of_model(w, i * P, col))]

    def paired_loads(w, col, slot):
        return lambda i: [(slot[:, :, g * HD:(g + 1) * HD], of_model(w, i * HD, col + g * 4 * HD, HD)) for g in range(2)]

    def query_out(q, width):
        return lambda ps, c: nc.scalar.activation(q[:, c * HALF:(c + 1) * HALF], ps, ACT.Copy, scale=-(width ** -0.5))

    def first_queries(w, q, width, paired, col):
        runs = [(g * HD, col + g * 4 * HD, HD) for g in range(2)] if paired else [(0, col, P)]
        return (cols(w, *runs), "feat", lambda act, ps: nc.scalar.activation(flat2(q), ps, ACT.Copy, scale=-(width ** -0.5)))

    half_rows = lambda u: slice(u["hf"] * HD, (u["hf"] + 1) * HD)

    def memory_track(w, q_col, gate_col, q, kT, v, o_tile):
        return dict(
            kinds=["mem"], halves=1, head_w=P, o_tile=o_tile, bias=None, parts=lambda qb: [[("mem", MEM)]],
            q_ap=lambda qb, hf: q[:, qb * P:(qb + 1) * P],
            k_ap=lambda u, i, c, w_: kT[:, bass.ds(i * MEM, MEM)],
            v_ap=lambda u, t, i, w_: v[:, bass.ds(i * P + t * 512, P)],
            gate_w=wsl[:, 1], gate_loads=plain_loads(w, gate_col, wsl[:, 1]),
            next_w=wsl[:, 3], next_loads=plain_loads(w, q_col, wsl[:, 3]), next_out=query_out(q, P))

    def mem_jobs(w, kT, v):
        jobs = [(cols(w, (0, h * P, P)), "memk",
                 lambda act, ps, h=h: nc.scalar.activation(kT[:, h * MEM:(h + 1) * MEM], ps[:, 0, 0:MEM], ACT.Copy)) for h in range(4)]
        for h in range(4):
            jobs.append((cols(w, (0, 512 + h * P, P)), "memv",
                         lambda act, ps, h=h: nc.scalar.activation(v.rearrange("p (t n) -> p t n", t=2)[:, :, h * P:(h + 1) * P],
                                                                   ps[:, 0, 0:MEM].rearrange("p (t n) -> p t n", t=2), ACT.Copy)))
        return jobs

    pos_col_i = sb("pos_col", QB, I32)

    def load_positions(sp, pos_row_i, done):
        with nc.allow_non_contiguous_dma(reason="positions, one per partition"):
            sp.dma_start(pos_row_i, a["positions"].partition_broadcast(P)).then_inc(done, 16)
            sp.dma_start(pos_col_i[:, :], a["positions"].rearrange("(b p) -> p b", p=P)).then_inc(done, 16)

    we = a["w_in_even"]

    top = 24500

    def at_top(width):
        nonlocal top
        top -= width
        return work[:, top:top + width]
    row_hi, row_lo = at_top(SEQ), at_top(SEQ)
    col_hi, col_lo = at_top(QB), at_top(QB)
    swk, swv, mk, mv, q_swa, q_mem = (at_top(SEQ) for _ in range(6))
    even_top = top
    rows = (row_hi, row_lo, col_hi, col_lo)
    cqn = work[:, 0:2 * SEQ].rearrange("p (k t) -> p k t", k=2)
    ckvn, kr = work[:, 2 * SEQ:3 * SEQ], work[:, 3 * SEQ:4 * SEQ]
    cs = work[:, 4 * SEQ:5 * SEQ]
    sinT = work[:, 5 * SEQ:6 * SEQ]
    pos_row_i = work[:, 6 * SEQ:7 * SEQ].bitcast(I32)
    itmp = work[:, 7 * SEQ:8 * SEQ].bitcast(I32)
    pos_f = work[:, 9 * SEQ:10 * SEQ]
    mbufs = work[:, 7 * SEQ:7 * SEQ + 6672]
    gate_x = wsl_t[:, 3 * SEQ + HALF:4 * SEQ]
    kslot = [work[:, 7 * SEQ + 6672 + s * SEQ:7 * SEQ + 6672 + (s + 1) * SEQ] for s in range(2)]
    assert 9 * SEQ + 6672 <= even_top
    sqs = oT[:, 0:3, :]
    rs_q, rs_kv = oT[:, 3, :], oT[:, 4, :]
    gq, gkv = gains[:, 16:18], gains[:, 18:19]
    nsink, nsink_pair = small[:, 200:208], small[:, 208:210]
    by_dist_w = oT_t[:, 5 * SEQ:8 * SEQ]
    by_dist = by_dist_w.rearrange("p (h n) -> p h n", h=HEADS)
    table_h = oT_t[:, 8 * SEQ:8 * SEQ + HEADS]
    table_in, dist_done, band_out, band_in = sem("p0table"), sem("p0dist"), sem("p0bandout"), sem("p0band")
    memT1_out = sem("n_m1_out")
    pos_in, latent_gain_in = sem("p0pos"), sem("p0lg")
    angles_done, trig_done, key_done, root_done = sem("p0angle"), sem("p0trig"), sem("p0key"), sem("p0root")
    QSC = -float((NOPE + ROPE) ** -0.5)

    def p0_loads(sp):
        load_positions(sp, pos_row_i, pos_in)
        sp.dma_start(table_h[0:NB, :], a["rel_bias_table"]).then_inc(table_in, 16)
        sp.dma_start(nsink, a["swa_sinks"].partition_broadcast(P)).then_inc(pos_in, 16)
        with nc.allow_non_contiguous_dma(reason="gains, one per partition"):
            sp.dma_start(gq, a["mla_q_norm"].rearrange("(k p) -> p k", p=P)).then_inc(latent_gain_in, 16)
            sp.dma_start(gkv, a["mla_kv_norm"].rearrange("(k p) -> p k", p=P)).then_inc(latent_gain_in, 16)

    def p0_vector(dve):
        dve.wait_ge(pos_in, 48)
        nc.vector.tensor_copy(pos_f, pos_row_i)
        position_rows(dve, pos_row_i, pos_col_i[:, :], row_hi, row_lo, col_hi, col_lo, itmp)
        TWO_PI = [6.28125, 0.0019350051879882812, 2 * math.pi - 6.28125 - 0.0019350051879882812]
        MAGIC = 1.5 * 2 ** 23
        turns = itmp.bitcast(F32)
        nc.vector.tensor_scalar(pos_f, pos_f, consts[:, C_INV:C_INV + 1], None, ALU.mult)
        dve.drain()
        nc.vector.tensor_scalar(turns, pos_f, 1 / (2 * math.pi), MAGIC, ALU.mult, ALU.add)
        dve.drain()
        nc.vector.tensor_scalar(turns, turns, MAGIC, None, ALU.subtract)
        dve.drain()
        for part in TWO_PI:
            nc.vector.scalar_tensor_tensor(out=pos_f, in0=turns, scalar=-float(part), in1=pos_f, op0=ALU.mult, op1=ALU.add)
            dve.drain()
        PI = 3.1415925
        nc.vector.tensor_scalar(sinT, pos_f, PI, -PI, ALU.min, ALU.max)
        nc.vector.tensor_scalar(turns, pos_f, math.pi / 2, None, ALU.is_gt)
        nc.vector.tensor_scalar(cs, pos_f, math.pi / 2, None, ALU.add)
        dve.drain()
        nc.vector.scalar_tensor_tensor(out=cs, in0=turns, scalar=-2 * math.pi, in1=cs, op0=ALU.mult, op1=ALU.add)
        dve.drain()
        nc.vector.tensor_scalar(cs, cs, PI, -PI, ALU.min, ALU.max).then_inc(angles_done, 1)
        d1, d2 = pos_f[:, 0:SEQ - 1], turns[:, 0:SEQ - 1]
        dve.drain()
        nc.vector.tensor_tensor(d1, row_hi[:, 1:SEQ], row_hi[:, 0:SEQ - 1], ALU.subtract)
        nc.vector.tensor_tensor(d2, row_lo[:, 1:SEQ], row_lo[:, 0:SEQ - 1], ALU.subtract)
        dve.drain()
        nc.vector.scalar_tensor_tensor(out=d1, in0=d1, scalar=65536.0, in1=d2, op0=ALU.mult, op1=ALU.add)
        dve.drain()
        nc.vector.tensor_scalar(d1, d1, 1.0, None, ALU.not_equal)
        dve.drain()
        nc.vector.tensor_reduce(out=gen_f, in_=d1, op=ALU.max, axis=AX.X)
        dve.drain()
        nc.vector.tensor_copy(gen_i[:, :], gen_f)
        dve.wait_ge(trig_done, 1)
        nc.vector.tensor_scalar(cs[96:128, :], sinT[96:128, :], consts[96:128, C_SIGN:C_SIGN + 1], None, ALU.mult)
        dve.wait_ge(key_done, 1)
        dve.drain()
        dve.wait_ge(memT1_out, 16)
        t1 = sinT[64:96, :]
        nc.vector.tensor_tensor(t1, kr[96:128, :], cs[96:128, :], ALU.mult)
        nc.vector.tensor_tensor(kr[64:96, :], kr[64:96, :], cs[64:96, :], ALU.mult)
        dve.drain()
        for s in range(2):
            nc.vector.tensor_tensor(kslot[s][64:96, :], kr[64:96, :], t1, ALU.add)
        nc.vector.tensor_scalar(cs[64:128, :], cs[64:128, :], QSC, None, ALU.mult)
        dve.wait_ge(root_done, 2)
        dve.wait_ge(latent_gain_in, 32)
        for rs in (rs_q, rs_kv):
            nc.vector.reciprocal(rs, rs)
        dve.drain()
        for k in range(2):
            nc.vector.scalar_tensor_tensor(out=cqn[:, k, :], in0=cqn[:, k, :], scalar=gq[:, k:k + 1], in1=rs_q, op0=ALU.mult, op1=ALU.mult)
        nc.vector.scalar_tensor_tensor(out=ckvn, in0=ckvn, scalar=gkv, in1=rs_kv, op0=ALU.mult, op1=ALU.mult)
        dve.wait_ge(band_in, 16 * HEADS)
        own = band[:, :].rearrange("p (h n) -> p h n", h=HEADS)[:, :, P:256]
        nc.vector.tensor_tensor(own, own, causal.unsqueeze(1).to_broadcast([P, HEADS, P]), ALU.add)

    def distance_bias(h):
        def go(pe, b):
            if h == 0:
                pe.wait_ge(table_in, 16)
            for n in range(2):
                ins = nc.tensor.matmul(PS[:, b + n, 0:SKEW], table_h[0:NB, h + n:h + n + 1].to_broadcast([NB, P]),
                                       consts[0:NB, C_HOT:C_HOT + SKEW], start=True, stop=True)
            return ins
        return go

    def distance_out(h):
        def go(act, ps):
            nc.scalar.activation(by_dist[:, h:h + 2, :], ps[:, :, 0:SKEW], ACT.Copy).then_inc(dist_done, 1)
            return act.drain()
        return go

    def p0_band(pool):
        pool.wait_ge(dist_done, 4)
        pool.dma_start(skew_dram[0:P * HEADS * SKEW].rearrange("(q n) -> q n", q=P), by_dist_w).then_inc(band_out, 16)
        pool.wait_ge(band_out, 16)
        skewed = skew_dram[P - 1:P - 1 + P * (HEADS * SKEW - 1)].rearrange("(q n) -> q n", q=P)[:, 0:HEADS * SKEW - P + 1]
        for h in range(HEADS):
            pool.dma_start(band[:, h * 256:(h + 1) * 256], skewed[:, h * SKEW:h * SKEW + 256]).then_inc(band_in, 16)

    def latent_out(dst, k):
        def go(act, ps):
            nc.scalar.activation(flat2(dst), ps, ACT.Copy)
            return nc.scalar.activation(flat2(sqs[:, k, :]), ps, ACT.Square)
        return go

    def square_sums(ks):
        def go(pe, b):
            for c in range(2):
                for k in ks:
                    ins = nc.tensor.matmul(PS[:, b + c, :], ones, sqs[:, k, c * HALF:(c + 1) * HALF], start=k == ks[0], stop=k == ks[-1])
            return ins
        return go

    def root_out(dst, n):
        def go(act, ps):
            nc.scalar.activation(flat2(dst), ps, ACT.Sqrt, scale=1.0 / n, bias=consts[:, C_EPS:C_EPS + 1]).then_inc(root_done, 1)
            return act.drain()
        return go

    def key_out(act, ps):
        nc.scalar.activation(flat2(kr), ps, ACT.Copy).then_inc(key_done, 1)
        return act.drain()

    def swv_out(act, ps):
        ins = nc.scalar.activation(flat2(swv), ps, ACT.Copy)
        act.wait_ge(angles_done, 1)
        nc.scalar.activation(cs, cs, ACT.Sin)
        nc.scalar.activation(sinT, sinT, ACT.Sin).then_inc(trig_done, 1)
        return act.drain()

    even_jobs = [(cols(we, (0, E_CQ + P * i, P)), "feat", latent_out(cqn[:, i, :], i)) for i in range(2)]
    even_jobs.append((cols(we, (0, E_CKV, P)), "feat", latent_out(ckvn, 2)))
    even_jobs.append((cols(we, (0, E_CKV, 64), (64, E_KR, 32), (96, E_KR + 16, 16), (112, E_KR, 16)), "feat", key_out))
    even_jobs.append((None, square_sums([0, 1]), root_out(rs_q, 256)))
    even_jobs.append((None, square_sums([2]), root_out(rs_kv, 128)))
    even_jobs.append((cols(we, (0, E_KSWA, P)), "feat", copy_out(flat2(swk))))
    even_jobs.append((cols(we, (0, E_VSWA, P)), "tok", swv_out))
    even_jobs += [(None, distance_bias(h), distance_out(h)) for h in range(0, HEADS, 2)]
    even_jobs.append(first_queries(we, q_swa, HD, True, E_QSWA))
    even_jobs.append(first_queries(we, q_mem, P, False, E_QMEM))
    queue = weight_queue("p0", even_jobs)
    norm_stage(mem_jobs(a["w_mem_kv"][0], mk, mv), memT1_out, queue)
    project_stage("p0", even_jobs, queue, None, p0_vector, p0_loads, pool_side=p0_band)

    vs = kr
    qslot = [work[:, 5 * SEQ:6 * SEQ], work[:, 6 * SEQ:7 * SEQ]]
    wuq_w, wukv_w = wsl_t[:, 2 * SEQ:2 * SEQ + 512], wsl_t[:, 2 * SEQ + 512:2 * SEQ + 768]
    rtmp = wsl_t[:, 3 * SEQ:3 * SEQ + HALF]
    wuq = wuq_w.rearrange("p (k h n) -> p k h n", k=2, h=2)
    wukv = wukv_w.rearrange("p (h n) -> p h n", h=2)
    uq = a["mla_w_uq"].rearrange("(k p) n -> p k n", p=P)

    def mla_loads(i):
        out = []
        for hf in range(2):
            c0 = i * (2 * 96) + hf * 96
            out.append((wuq[:, :, hf, 0:96], uq[:, :, bass.ds(c0, 96)]))
            out.append((wuq[:, :, hf, 96:112], uq[:, :, bass.ds(c0 + 80, 16)]))
            out.append((wuq[:, :, hf, 112:128], uq[:, :, bass.ds(c0 + 64, 16)]))
        out.append((wukv_w, a["mla_w_ukv"][:, bass.ds(i * 256, 256)]))
        return out

    def mla_q(hf, c):
        sl = slice(c * HALF, (c + 1) * HALF)

        def emit(b, i):
            for k in range(2):
                ins = nc.tensor.matmul(PS[:, b, :], wuq[:, k, hf, :], cqn[:, k, sl], start=k == 0, stop=k == 1)
            return ins

        def on_act(b):
            return nc.scalar.activation(qslot[hf][0:64, sl], PS[0:64, b, :], ACT.Copy, scale=QSC)

        def on_dve(dve, b):
            nc.vector.tensor_tensor(rtmp[64:96, :], PS[96:128, b, :], cs[96:128, sl], ALU.mult)
            nc.vector.tensor_tensor(qslot[hf][64:96, sl], PS[64:96, b, :], cs[64:96, sl], ALU.mult)
            dve.drain()
            ins = nc.vector.tensor_tensor(qslot[hf][64:96, sl], qslot[hf][64:96, sl], rtmp[64:96, :], ALU.add)
            dve.drain()
            return ins
        return emit, on_act, on_dve

    def mla_k(hf, c):
        sl = slice(c * HALF, (c + 1) * HALF)
        return (lambda b, i: nc.tensor.matmul(PS[0:64, b, :], wukv[:, hf, 0:64], ckvn[:, sl], start=True, stop=True),
                lambda b: nc.scalar.activation(kslot[hf][0:64, sl], PS[0:64, b, :], ACT.Copy), None)

    def mla_v(c):
        def emit(b, i):
            for t in range(4):
                ins = nc.tensor.matmul(PS[:, b, t * P:(t + 1) * P], ckvn[:, (4 * c + t) * P:(4 * c + t + 1) * P],
                                       wukv[:, :, 64:128], start=True, stop=True)
            return ins
        return emit, lambda b: nc.scalar.activation(vs[:, c * HALF:(c + 1) * HALF], PS[:, b, :], ACT.Copy), None

    mla_track = dict(
        kinds=["mla"], halves=2, head_w=HD, o_tile=0, bias=None, bufs=mbufs, gate_x=gate_x, parts=lambda qb: [[("mla", ln("mla", qb))]],
        q_ap=lambda qb, hf: qslot[hf][0:96, qb * P:(qb + 1) * P],
        k_ap=lambda u, i, c, w: kslot[u["hf"]][0:96, c:c + w],
        v_ap=lambda u, t, i, w: vs[:, t * P + u["hf"] * HD:t * P + (u["hf"] + 1) * HD],
        gate_w=wsl[:, 0], gate_loads=plain_loads(we, E_GMLA, wsl[:, 0]))
    attention_stage(
        "mla", [mla_track], loads=mla_loads,
        proj_jobs=[mla_q(hf, c) for hf in range(2) for c in range(2)] + [mla_k(hf, c) for hf in range(2) for c in range(2)] + [mla_v(c) for c in range(2)])

    BW = 264
    swab, swband, sc1, sc2, sc3 = carve(2 * QB * BW, HEADS * 256, 256, 256, 256)
    used_w = 2 * QB * BW + HEADS * 256 + 768

    def swa_setup(dve):
        halves = lambda t: t.rearrange("p (h s n) -> p h s n", h=HEADS, s=2)
        nc.vector.tensor_tensor(halves(swband)[:, :, 0], halves(band[:, :])[:, :, 0], winmask.unsqueeze(1).to_broadcast([P, HEADS, P]), ALU.add)
        nc.vector.tensor_copy(halves(swband)[:, :, 1], halves(band[:, :])[:, :, 1])
        nc.vector.memset(swab.rearrange("p (b n) -> p b n", n=BW)[:, :, 256:257], 0.0)
        nc.vector.tensor_scalar(nsink, nsink, -1.0, None, ALU.mult)
        return dve.drain()

    def swa_block(hf, qb):
        w = P if qb == 0 else 256
        o = (hf * QB + qb) * BW + 256
        return swab[:, o - w:o], w

    def swa_bias(u):
        o = (u["hf"] * QB + u["qb"]) * BW + 256
        return swab[:, o - u["n"]:o + 1]

    def swa_sink(i):
        for g in range(2):
            nc.vector.tensor_copy(nsink_pair[:, g:g + 1], nsink[:, bass.ds(i + 4 * g, 1)])
        nc.vector.drain()
        return nsink_pair

    def swa_stage(qb, i):
        for hf in range(2):
            dst, w = swa_block(hf, qb)
            nc.gpsimd.tensor_copy(dst, swband[:, bass.ds(i * 256 + (hf * 1024 + 256 - w), w)])

    def swa_general(dve, gen, i):
        with dve.If(gen == 1):
            for qb in range(QB):
                w, k0 = (P, 0) if qb == 0 else (256, (qb - 1) * P)
                dst = [swa_block(hf, qb)[0] for hf in range(2)]
                bias_block(dve, rows, qb, k0, w, dst, [i, i + 4], (sc1, sc2, sc3), True)
                for d in dst:
                    add_to(d[:, w - P:w], causal)
                    if qb:
                        add_to(d[:, 0:P], winmask)
                dve.drain()
        with dve.Else():
            dve.nop()

    first_key = lambda u: max(0, u["qb"] - 1) * P
    swa_track = dict(
        kinds=["swa"], halves=2, head_w=HD, o_tile=4, bias=swa_bias, sink=swa_sink, bufs=work[:, used_w:even_top - HALF], gate_x=work[:, even_top - HALF:even_top],
        parts=lambda qb: [[("swa", ln("swa", qb))]], bank_of=lambda qb, hf: hf,
        q_ap=lambda qb, hf: q_swa[hf * HD:(hf + 1) * HD, qb * P:(qb + 1) * P],
        k_ap=lambda u, i, c, w: swk[half_rows(u), first_key(u):(u["qb"] + 1) * P],
        v_ap=lambda u, t, i, w: swv[:, first_key(u) + t * P + u["hf"] * HD:first_key(u) + t * P + (u["hf"] + 1) * HD],
        gate_w=wsl[:, 0], gate_loads=paired_loads(we, E_GSWA, wsl[:, 0]),
        next_w=wsl[:, 2], next_loads=paired_loads(we, E_QSWA, wsl[:, 2]), next_out=query_out(q_swa, HD))
    mem_track = memory_track(we, E_QMEM, E_GMEM, q_mem, mk, mv, 8)
    mem_track["bank_of"] = lambda qb, hf: 2 + qb % 2
    attention_stage("swa", [swa_track, mem_track], loads=None, setup_dve=swa_setup, head_dve=swa_general, stage_pool=swa_stage)

    def even_rows(k):
        if 4 <= k < 8:
            return [(0, 512 + (k - 4) * HD, HD), (HD, 512 + (k - 4 + 4) * HD, HD)]
        return [(0, k * P, P)]

    wo_ = a["w_in_odd"]
    extra = oT_t[:, 8 * SEQ:12 * SEQ]
    mk, mv, row_hi, row_lo = (extra[:, n * SEQ:(n + 1) * SEQ] for n in range(4))
    top = 24500
    kslc, kwin, vslc, vwin, q_nsa, q_mem = (at_top(SEQ) for _ in range(6))
    kcT, vc = at_top(64), at_top(P)
    gl = at_top(QB * 24)
    col_hi, col_lo = at_top(QB), at_top(QB)
    rows = (row_hi, row_lo, col_hi, col_lo)
    odd_top = top
    kcmp, vcmp = work[:, 0:SEQ], work[:, SEQ:2 * SEQ]
    at = 2 * SEQ
    w2 = work[:, at:at + 256].rearrange("p (s m d) -> p s m d", s=2, m=2)
    pos2 = work[:, at + 256:at + 288].rearrange("p (s l) -> p s l", s=2)
    hid = work[:, at + 288:at + 800].rearrange("p (s m c) -> p s m c", s=2, m=2)
    w1 = work[:, 3 * SEQ:11 * SEQ].rearrange("p (s l n) -> p s l n", s=2, l=16)
    memT_w = work[:, 11 * SEQ:13 * SEQ]
    memT = memT_w.rearrange("p (k t) -> p k t", k=KT)
    x2 = work[:, 13 * SEQ:17 * SEQ].rearrange("p (s g t) -> p s g t", s=2, g=2)
    assert 17 * SEQ <= odd_top
    pos_row_i, itmp = oT[:, 0, :].bitcast(I32), oT[:, 1, :].bitcast(I32)
    xe = oT_t[:, 2 * SEQ:6 * SEQ].rearrange("p (s l c) -> p s l c", s=2, l=16)
    hb = oT_t[:, 6 * SEQ:6 * SEQ + 512].rearrange("p (s n) -> p s n", s=2)
    pos_in, mem_in, raw_done, x2_in = kept_sem("p1pos"), kept_sem("p1mem"), kept_sem("p1raw"), [kept_sem("p1x2k"), kept_sem("p1x2v")]
    w1_in, w2_in, xe_done = [kept_sem("p1w1k"), kept_sem("p1w1v")], kept_sem("p1w2"), kept_sem("p1xe")

    def p1_loads(sp):
        load_positions(sp, pos_row_i, pos_in)

    def p1_vector(dve):
        dve.wait_ge(pos_in, 32)
        position_rows(dve, pos_row_i, pos_col_i[:, :], row_hi, row_lo, col_hi, col_lo, itmp)
        dve.wait_ge(w2_in, 64)
        for s in range(2):
            dve.wait_ge(x2_in[s], 64)
            for g in range(2):
                for part in range(2):
                    src = x2[:, s, g, part * CMP_S:part * CMP_S + CMP_S * NC].rearrange("p (c l t) -> p l c t", c=NC, t=2)[:, :, :, 0]
                    ins = nc.vector.tensor_tensor(xe[:, s, part * 8:(part + 1) * 8, g * NC:(g + 1) * NC], src,
                                                  pos2[:, s, part * 8:(part + 1) * 8].unsqueeze(2).to_broadcast([P, 8, NC]), ALU.add)
            ins.then_inc(xe_done, 1)

    def p1_more_loads(pool):
        for s, n in enumerate("kv"):
            pool.dma_start(w2[:, s], a["cmp_w2_" + n].rearrange("(m p) d -> p m d", p=P)).then_inc(w2_in, 16)
            with nc.allow_non_contiguous_dma(reason="position embedding, one per partition"):
                pool.dma_start(pos2[:, s, :], a["cmp_pos_" + n].rearrange("(l a) d -> (a d) l", a=2)).then_inc(w2_in, 16)
        pool.wait_ge(raw_done, 1)
        for s, src in enumerate((kcmp, vcmp)):
            if s:
                pool.wait_ge(raw_done, 2)
            for g in range(2):
                rows_g = src[g * HD:(g + 1) * HD, :]
                pool.dma_start(x2[0:HD, s, g, :], rows_g).then_inc(x2_in[s], 16)
                pool.dma_start(x2[HD:P, s, g, 0:SEQ - 1], rows_g[:, 1:SEQ]).then_inc(x2_in[s], 16)
        for s, n in enumerate("kv"):
            pool.dma_start(w1[:, s], a["cmp_w1_" + n].rearrange("(l p) n -> p l n", p=P)).then_inc(w1_in[s], 16)
        pool.dma_start(memT_w, memT1_dram).then_inc(mem_in, 16)

    def raw_out(dst):
        def go(act, ps):
            nc.scalar.activation(flat2(dst), ps, ACT.Copy).then_inc(raw_done, 1)
            return act.drain()
        return go

    def hidden(s):
        def go(pe, b):
            pe.wait_ge(xe_done, s + 1)
            pe.wait_ge(w1_in[s], 16)
            for l in range(16):
                ins = nc.tensor.matmul(PS[0:126, b, 0:256], xe[:, s, l, 0:126], w1[:, s, l, :], start=l == 0, stop=l == 15)
            return ins
        return go

    def hidden_out(s):
        return lambda act, ps: nc.scalar.activation(hb[0:126, s, :], ps[0:126, 0, 0:256], ACT.Silu)

    def hidden_turned(pe, b):
        for s in range(2):
            for m in range(2):
                ins = nc.tensor.transpose(PS[:, b, (2 * s + m) * P:(2 * s + m) * P + 126], hb[0:126, s, m * P:(m + 1) * P], ident[0:126, 0:126])
        return ins

    def turned_out(act, ps):
        return nc.scalar.activation(hid[:, :, :, 0:126], ps[:, 0, :].rearrange("p (s m c) -> p s m c", s=2, m=2)[:, :, :, 0:126], ACT.Copy)

    def compressed(pe, b):
        for g in range(2):
            for m in range(2):
                nc.tensor.matmul(PS[g * HD:(g + 1) * HD, b, 0:NC], w2[:, 0, m, :], hid[:, 0, m, g * NC:(g + 1) * NC], start=m == 0, stop=m == 1)
            for m in range(2):
                ins = nc.tensor.matmul(PS[0:NC, b + 1, g * HD:(g + 1) * HD], hid[:, 1, m, g * NC:(g + 1) * NC], w2[:, 1, m, :], start=m == 0, stop=m == 1)
        return ins

    def compressed_out(act, ps):
        nc.scalar.activation(kcT[:, 0:NC], ps[:, 0, 0:NC], ACT.Copy)
        return nc.scalar.activation(vc[0:NC, :], ps[0:NC, 1, 0:P], ACT.Copy)

    def gl_out(act, ps):
        return nc.scalar.activation(gl.rearrange("p (c t n) -> p c t n", c=2, t=4),
                                    ps.rearrange("p c (t n) -> p c t n", t=4)[:, :, :, 0:24], ACT.Sigmoid)

    odd_jobs = [
        (cols(wo_, (0, O_KCMP, P)), "feat", raw_out(kcmp)),
        (cols(wo_, (0, O_VCMP, P)), "feat", raw_out(vcmp)),
        (cols(wo_, (0, O_KSLC, P)), "feat", copy_out(flat2(kslc))),
        (cols(wo_, (0, O_KWIN, P)), "feat", copy_out(flat2(kwin))),
        (cols(wo_, (0, O_VSLC, P)), "tok", copy_out(flat2(vslc))),
        (cols(wo_, (0, O_VWIN, P)), "tok", copy_out(flat2(vwin))),
        first_queries(wo_, q_nsa, HD, True, O_Q),
        first_queries(wo_, q_mem, P, False, O_QMEM),
        (cols(wo_, (0, O_GL, 24)), "tok24", gl_out)]
    hidden_jobs = [(None, hidden(s), hidden_out(s)) for s in range(2)]
    memory_jobs = mem_jobs(a["w_mem_kv"][1], mk, mv)
    jobs = (odd_jobs + hidden_jobs + memory_jobs[:2] + [(None, hidden_turned, turned_out)] + memory_jobs[2:4]
            + [(None, compressed, compressed_out)] + memory_jobs[4:])
    queue = weight_queue("p1", jobs)
    output_stage("o0", a["w_out_even"], 12, even_rows, a["norm_post"][0], a["x"], x1_dram, gains[:, 32:40], queue["first"])
    nc.clear_and_free_semaphores(layer_sems)
    nc.all_engine_barrier()
    layer_sems.clear()
    project_stage("p1", jobs, queue, memT, p1_vector, p1_loads, mem_in, p1_more_loads)

    PACK = [64 * qb * (qb + 1) for qb in range(QB + 1)]
    nb_w, nbufs = work[:, 0:2 * PACK[QB]], work[:, 2 * PACK[QB]:odd_top - HALF]
    nb16 = nb_w.rearrange("p (n s) -> p n s", s=CMP_S)

    def nsa_stage(qb, i):
        for hf in range(2):
            o = hf * PACK[QB] + PACK[qb]
            n = PACK[qb + 1] - PACK[qb]
            if n > 256:
                nc.gpsimd.tensor_copy(nb_w[:, o:o + n - 256], band[:, bass.ds(i * 256 + hf * 1024, 1)].to_broadcast([P, n - 256]))
            w = min(n, 256)
            nc.gpsimd.tensor_copy(nb_w[:, o + n - w:o + n], band[:, bass.ds(i * 256 + (hf * 1024 + 256 - w), w)])

    def nsa_general(dve, gen, i):
        with dve.If(gen == 1):
            for qb in range(QB):
                n = PACK[qb + 1] - PACK[qb]
                dst = [nb_w[:, hf * PACK[QB] + PACK[qb]:hf * PACK[QB] + PACK[qb + 1]] for hf in range(2)]
                bias_block(dve, rows, qb, 0, n, dst, [i, i + 4], [nbufs[:, s * SEQ:(s + 1) * SEQ] for s in range(3)], True)
                for d in dst:
                    add_to(d[:, n - P:n], causal)
                dve.drain()
        with dve.Else():
            dve.nop()

    def nsa_bias(u):
        qb, o = u["qb"], u["hf"] * PACK[QB] + PACK[u["qb"]]
        if u["kind"] == "cmp":
            return nb16[:, o // CMP_S + 1:o // CMP_S + 1 + u["n"], CMP_S - 1]
        return nb_w[:, o + P * (qb + 1) - u["n"]:o + P * (qb + 1)]

    def nsa_k(u, i, c, w):
        r = half_rows(u)
        if u["kind"] == "cmp":
            return kcT[r, c:c + w]
        if u["kind"] == "slc":
            return kslc[r, c:c + w]
        k0 = P * (u["qb"] + 1) - u["n"]
        return kwin[r, k0 + c:k0 + c + w]

    def nsa_v(u, t, i, w):
        c = u["hf"] * HD
        if u["kind"] == "cmp":
            return vc[0:w, c:c + HD]
        if u["kind"] == "slc":
            return vslc[:, t * P + c:t * P + c + HD]
        t += u["qb"] + 1 - u["n"] // P
        return vwin[:, t * P + c:t * P + c + HD]

    nsa_track = dict(
        kinds=["cmp", "slc", "win"], halves=2, head_w=HD, o_tile=0, bias=nsa_bias, bufs=nbufs, gate_x=work[:, odd_top - HALF:odd_top],
        parts=lambda qb: [[("slc", ln("slc", qb))], [("win", ln("win", qb)), ("cmp", ln("cmp", qb))]],
        gate=lambda qb, hf, i: gl[:, bass.ds(i * 3 + (qb * 24 + hf * 12), 3)],
        q_ap=lambda qb, hf: q_nsa[hf * HD:(hf + 1) * HD, qb * P:(qb + 1) * P], k_ap=nsa_k, v_ap=nsa_v,
        gate_w=wsl[:, 0], gate_loads=paired_loads(wo_, O_GNSA, wsl[:, 0]),
        next_w=wsl[:, 2], next_loads=paired_loads(wo_, O_Q, wsl[:, 2]), next_out=query_out(q_nsa, HD))
    attention_stage("nsa", [nsa_track, memory_track(wo_, O_QMEM, O_GMEM, q_mem, mk, mv, 4)], loads=None,
                    head_dve=nsa_general, stage_pool=nsa_stage)

    def odd_rows(k):
        return [(0, k * HD, HD), (HD, (k + 4) * HD, HD)] if k < 4 else [(0, k * P, P)]

    output_stage("o1", a["w_out_odd"], 8, odd_rows, a["norm_post"][1], x1_dram, a["out"], None)
    ctx.close()


SQUEEZE = ("x", "mem", "w_in_even", "mla_q_norm", "mla_kv_norm", "swa_sinks", "mla_w_uq", "mla_w_ukv", "w_out_even", "w_in_odd",
           "cmp_pos_k", "cmp_pos_v", "cmp_w1_k", "cmp_w2_k", "cmp_w1_v", "cmp_w2_v", "w_out_odd")


def build(nc, arrays):
    a = {}
    for name, v in arrays.items():
        ap = nc.dram_tensor(name, v.shape, mybir.dt.from_np(v.dtype), kind="ExternalInput").ap()
        a[name] = ap[0] if name in SQUEEZE else ap
    a["out"] = nc.dram_tensor("out", (1, SEQ, D), F32, kind="ExternalOutput").ap()[0]
    trunk(nc, a)


def kernel(**inputs):
    import concourse.bacc as bacc
    from concourse.bass_utils import run_bass_kernel_spmd

    nc = bacc.Bacc("TRN2", target_bir_lowering=False, num_devices=1)
    arrays = {name: np.ascontiguousarray(v) for name, v in inputs.items()}
    arrays["const_tables"] = make_constants()
    build(nc, arrays)
    return run_bass_kernel_spmd(nc, [arrays], core_ids=[0]).results[0]["out"]
```

```python
import math
from contextlib import ExitStack

import numpy as np

import concourse.bass as bass
import concourse.mybir as mybir

F32 = mybir.dt.float32
I32 = mybir.dt.int32
F32R = mybir.dt.float32r
ALU = mybir.AluOpType
ACT = mybir.ActivationFunctionType
AX = mybir.AxisListType

P = 128
SEQ = 1024
D = 1024
MEM = 256
KT = D // P
QB = SEQ // P
HALF = 512
HD = 64
HEADS = 8
PAIRS = HEADS // 2
NB = 32
BIG = 1e30
EPS = 1e-6

C_ID = 0
C_CAUSAL = 128
C_WIN = 256
C_ONES = 384
C_INV = 512
C_SIGN = 513
C_NTHR = 514
C_BKT = C_NTHR + NB
C_EPS = C_BKT + NB
C_HOT = C_EPS + 1
SKEW = 384
N_CONST = C_HOT + SKEW

E_CQ, E_CKV, E_KR, E_GMLA, E_QSWA, E_KSWA, E_VSWA, E_GSWA, E_QMEM, E_GMEM = (
    0, 256, 384, 416, 928, 1440, 1568, 1696, 2208, 2720)
(O_Q, O_KCMP, O_VCMP, O_KSLC, O_VSLC, O_KWIN, O_VWIN, O_GL, O_GNSA, O_QMEM, O_GMEM) = (
    0, 512, 640, 768, 896, 1024, 1152, 1280, 1304, 1816, 2328)
NOPE, ROPE = 64, 32
CMP_L, CMP_S = 32, 16
NC = (SEQ - CMP_L) // CMP_S + 1
OUT_LAG = 2
LAG = 2
LOOK = 2


def make_constants():
    c = np.zeros((P, N_CONST), np.float32)
    q, k = np.arange(P)[:, None], np.arange(P)[None, :]
    c[:, C_ID:C_ID + P] = np.eye(P)
    c[:, C_CAUSAL:C_CAUSAL + P] = np.where(k <= q, 0, BIG)
    c[:, C_WIN:C_WIN + P] = np.where(k > q, 0, BIG)
    c[:, C_ONES:C_ONES + P] = 1
    half = ROPE // 2
    inv = np.float32(10000.0) ** (-np.arange(half, dtype=np.float32) / np.float32(half))
    c[:, C_INV] = inv[np.arange(P) % half]
    c[:, C_SIGN] = np.where(np.arange(P) % ROPE < half, -1, 1)
    d = np.arange(1, 256, dtype=np.float32)
    ratio = np.log(d / np.float32(16)).astype(np.float32) / np.float32(math.log(8))
    bucket = np.where(d < 16, d, np.minimum(16 + (ratio * 16).astype(np.int32), NB - 1)).astype(int)
    for b in range(1, NB):
        c[:, C_NTHR + b] = -d[np.argmax(bucket >= b)]
    c[:, C_BKT:C_BKT + NB] = np.arange(NB)
    c[:, C_EPS] = EPS
    dist = np.maximum(255 - np.arange(SKEW), 0)
    of = np.where(dist == 0, 0, bucket[np.maximum(dist, 1) - 1])
    c[of, C_HOT + np.arange(SKEW)] = -1
    return c


def trunk(nc, a):
    ctx = ExitStack()

    def sb(name, width, dt=F32):
        return ctx.enter_context(nc.sbuf_tensor(name, [P, width], dt))

    layer_sems = []

    def sem(name):
        layer_sems.append(nc.alloc_semaphore(name))
        return layer_sems[-1]

    def kept_sem(name):
        return nc.alloc_semaphore(name)

    consts = sb("consts", N_CONST)
    ident = consts[:, C_ID:C_ID + P]
    causal = consts[:, C_CAUSAL:C_CAUSAL + P]
    winmask = consts[:, C_WIN:C_WIN + P]
    ones = consts[:, C_ONES:C_ONES + P]
    table = sb("table", NB * HEADS)
    hT_t = sb("hT", KT * SEQ)
    hT = hT_t[:, :].rearrange("p (k t) -> p k t", k=KT)
    oT_t = sb("oT", 12 * SEQ)
    oT = oT_t[:, :].rearrange("p (k t) -> p k t", k=12)
    wsl_t = sb("w_slots", 4 * KT * P)
    wsl = wsl_t[:, :].rearrange("p (s k n) -> p s k n", s=4, k=KT)
    gains = sb("gains", 64)
    band = sb("band", HEADS * 256)
    small = sb("small", 256)
    gen_f = small[:, 250:251]
    wait_marks = small[0:1, 60:160]
    gen_i = sb("gen_i", 1, I32)
    pos_col_i = sb("pos_col", QB, I32)

    def lasting(name, width, dt=F32):
        held = ExitStack()
        return held.enter_context(nc.sbuf_tensor(name, [P, width], dt)), held
    work, work_held = lasting("work", 24500)
    PS = ctx.enter_context(nc.psum_tensor("PS", [P, 8, HALF], F32))

    def carve(*widths):
        at, out = 0, []
        for w in widths:
            out.append(work[:, at:at + w])
            at += w
        assert at <= 24500, at
        return out

    x1_dram = nc.dram_tensor("x1_scratch", (SEQ, D), F32, kind="Internal").ap()
    skew_dram = nc.dram_tensor("skew_scratch", (P * HEADS * SKEW + P,), F32, kind="Internal").ap()
    memT1_dram = nc.dram_tensor("memT1_scratch", (P, KT * MEM), F32, kind="Internal").ap()

    eng_pe, eng_act, eng_dve = nc.tensor, nc.scalar, nc.vector

    def project(kind, w, b, memT):
        if kind == "feat":
            for c in range(2):
                for k in range(KT):
                    ins = nc.tensor.matmul(PS[:, b + c, :], w[:, k, :], hT[:, k, c * HALF:(c + 1) * HALF],
                                           start=k == 0, stop=k == KT - 1)
        elif kind.startswith("tok"):
            width = int(kind[3:] or P)
            for t in range(QB):
                for k in range(KT):
                    ins = nc.tensor.matmul(PS[:, b + t // 4, (t % 4) * P:(t % 4) * P + width],
                                           hT[:, k, t * P:(t + 1) * P], w[:, k, 0:width],
                                           start=k == 0, stop=k == KT - 1)
        elif kind == "memk":
            for k in range(KT):
                ins = nc.tensor.matmul(PS[:, b, 0:MEM], w[:, k, :], memT[:, k, :], start=k == 0, stop=k == KT - 1)
        else:
            for t in range(MEM // P):
                for k in range(KT):
                    ins = nc.tensor.matmul(PS[:, b, t * P:(t + 1) * P], memT[:, k, t * P:(t + 1) * P],
                                           w[:, k, :], start=k == 0, stop=k == KT - 1)
        return ins

    def norm_stage(jobs, m1_out, next_queue):
        MT = MEM // P
        NT = QB + MT
        xs, sq, memT_w, memT1_w = carve(NT * D, D, KT * MEM, KT * MEM)
        xs = xs.rearrange("p (t d) -> p t d", t=NT)
        memT = memT_w.rearrange("p (k t) -> p k t", k=KT)
        memT1 = memT1_w.rearrange("p (k t) -> p k t", k=KT)
        stat, rstd = small[:, 0:NT], small[:, 16:16 + NT]
        names = ("const", "gain", "sq", "var", "rt", "xn", "tr", "ev_act", "ev_dve", "m1", "job", "job_ev")
        (const_in, gain_in, sq_done, var_done, rt_done, xn_done, tr_done, ev_act, ev_dve, m1_done, job_done, job_ev) = (
            sem("n_" + n) for n in names)
        x_in = [sem(f"n_x{t}") for t in range(NT)]
        queue = weight_queue("m0", jobs)
        NJ = len(jobs)
        with nc.Block() as block:
            @block.sync
            def _(sp):
                for t in range(NT):
                    src = a["mem"][t * P:(t + 1) * P, :] if t < MT else a["x"][(t - MT) * P:(t - MT + 1) * P, :]
                    sp.dma_start(xs[:, t, :], src).then_inc(x_in[t], 16)
                    if t == 0:
                        sp.dma_start(consts[:, :], a["const_tables"]).then_inc(const_in, 16)
                        with nc.allow_non_contiguous_dma(reason="gains, one per partition"):
                            for g, src in ((0, a["norm_pre"][0]), (8, a["mem_norm"][0]), (24, a["mem_norm"][1]), (32, a["norm_pre"][1])):
                                sp.dma_start(gains[:, g:g + KT], src.rearrange("(k p) -> p k", p=P)).then_inc(gain_in, 16)
                    if 2 <= t < 6:
                        queue["send"](sp, t - 2)
                sp.dma_start(table[:, :], a["rel_bias_table"].rearrange("b h -> (b h)").partition_broadcast(P)).then_inc(const_in, 16)
                for m in range(4, NJ):
                    sp.wait_ge(job_done, m - 3)
                    queue["send"](sp, m)
                sp.wait_ge(m1_done, 1)
                sp.dma_start(memT1_dram, memT1_w).then_inc(m1_out, 16)
                for m in range(4):
                    sp.wait_ge(job_done, NJ - 3 + m)
                    next_queue["send"](sp, m)
                sp.wait_ge(const_in, 32)

            @block.scalar
            def _(act):
                def root(t):
                    act.wait_ge(var_done, t + 1)
                    nc.scalar.activation(rstd[:, t:t + 1], stat[:, t:t + 1], ACT.Sqrt).then_inc(rt_done, 1)

                def copy(t):
                    if t >= MT:
                        act.wait_ge(tr_done, 2 * t + 1)
                        cut = slice((t - MT) * P, (t - MT + 1) * P)
                        for k in range(4):
                            ins = nc.scalar.activation(hT[:, k, cut], PS[:, 2 * (t % 2), k * P:(k + 1) * P], ACT.Copy, scale=gains[:, k:k + 1])
                        ins.then_inc(ev_act, 1)
                    if t >= MT and t - MT < NJ:
                        j = t - MT
                        act.wait_ge(job_done, j + 1)
                        jobs[j][2](act, PS[:, 4 + 2 * (j % 2):6 + 2 * (j % 2), :]).then_inc(job_ev, 1)

                for t in range(NT):
                    act.wait_ge(x_in[t], 16)
                    if t:
                        act.wait_ge(sq_done, t)
                    nc.scalar.activation(sq, xs[:, t, :], ACT.Square, accum_out=stat[:, t:t + 1]).then_inc(sq_done, 1)
                    if t >= 1:
                        root(t - 1)
                    if t == LAG:
                        act.wait_ge(gain_in, 64)
                    if t >= LAG:
                        copy(t - LAG)
                root(NT - 1)
                for t in range(NT - LAG, NT):
                    copy(t)

            @block.vector
            def _(dve):
                def scale(t):
                    dve.wait_ge(rt_done, t + 1)
                    nc.vector.tensor_scalar(xs[:, t, :], xs[:, t, :], rstd[:, t:t + 1], None, ALU.mult).then_inc(xn_done, 1)

                def copy(t):
                    b = 2 * (t % 2)
                    if t >= MT:
                        dve.wait_ge(tr_done, 2 * t + 2)
                        nc.vector.tensor_tensor(hT[:, 4:8, (t - MT) * P:(t - MT + 1) * P], PS[:, b + 1, :].rearrange("p (k n) -> p k n", k=4),
                                                gains[:, 4:8].unsqueeze(2).to_broadcast([P, 4, P]), ALU.mult).then_inc(ev_dve, 1)
                        return
                    cut = slice(t * P, (t + 1) * P)
                    for h in range(2):
                        dve.wait_ge(tr_done, 2 * t + h + 1)
                        src = PS[:, b + h, :].rearrange("p (k n) -> p k n", k=4)
                        for dst, g in ((memT, 8), (memT1, 24)):
                            ins = nc.vector.tensor_tensor(dst[:, 4 * h:4 * h + 4, cut], src,
                                                          gains[:, g + 4 * h:g + 4 * h + 4].unsqueeze(2).to_broadcast([P, 4, P]), ALU.mult)
                    ins.then_inc(ev_dve, 1)
                    if t == MT - 1:
                        dve.drain().then_inc(m1_done, 1)

                for t in range(NT):
                    st = stat[:, t:t + 1]
                    dve.wait_ge(sq_done, t + 1)
                    nc.vector.tensor_scalar(st, st, 1.0 / D, EPS, ALU.mult, ALU.add)
                    dve.drain()
                    nc.vector.reciprocal(st, st).then_inc(var_done, 1)
                    if t >= 1:
                        scale(t - 1)
                    if t == LAG:
                        dve.wait_ge(gain_in, 64)
                    if t >= LAG:
                        copy(t - LAG)
                scale(NT - 1)
                for t in range(NT - LAG, NT):
                    copy(t)

            @block.tensor
            def _(pe):
                pe.wait_ge(const_in, 16)
                for t in range(NT):
                    pe.wait_ge(xn_done, t + 1)
                    if t >= 2:
                        pe.wait_ge(ev_dve, t - 1)
                        if t - 2 >= MT:
                            pe.wait_ge(ev_act, t - 1 - MT)
                    for k in range(KT):
                        ins = nc.tensor.transpose(PS[:, 2 * (t % 2) + k // 4, (k % 4) * P:(k % 4 + 1) * P],
                                                  xs[:, t, k * P:(k + 1) * P], ident)
                        if k % 4 == 3:
                            ins.then_inc(tr_done, 1)
                    if MT <= t < MT + NJ:
                        j = t - MT
                        pe.wait_ge(ev_dve, MT)
                        pe.wait_ge(queue["w_in"][j % 4], 16 * (j // 4 + 1))
                        if j >= 2:
                            pe.wait_ge(job_ev, j - 1)
                        project(jobs[j][1], wsl[:, j % 4], 4 + 2 * (j % 2), memT).then_inc(job_done, 1)

    def weight_queue(tag, jobs):
        w_in = [kept_sem(f"{tag}w_in{s}") for s in range(4)]
        used = [n for n, job in enumerate(jobs) if job[0]]

        def send(sp, m):
            for dst, src in jobs[used[m]][0](wsl[:, m % 4]):
                sp.dma_start(dst, src).then_inc(w_in[m % 4], 16)
        return dict(w_in=w_in, used=used, send=send, first=lambda sp: [send(sp, m) for m in range(4)])

    def project_stage(tag, jobs, queue, memT, dve_side, sp_side, mem_in=None, pool_side=None, last_sp=None):
        w_in, used = queue["w_in"], queue["used"]
        pe_done, ev_done = sem(tag + "pe"), sem(tag + "ev")
        with nc.Block() as block:
            @block.sync
            def _(sp):
                sp_side(sp)
                for m in range(4, len(used)):
                    sp.wait_ge(pe_done, used[m - 4] + 1)
                    queue["send"](sp, m)
                if last_sp:
                    last_sp(sp, pe_done, used)

            @block.tensor
            def _(pe):
                loaded = [0] * 4
                for n, (loads, kind, _) in enumerate(jobs):
                    if n >= 2:
                        pe.wait_ge(ev_done, n - 1)
                    b = 2 * (n % 2)
                    if loads:
                        m = used.index(n) % 4
                        w = wsl[:, m]
                        loaded[m] += 16 * len(loads(w))
                        pe.wait_ge(w_in[m], loaded[m])
                    if mem_in is not None and not callable(kind) and kind[:3] == "mem" and not any(
                            not callable(j[1]) and j[1][:3] == "mem" for j in jobs[:n]):
                        pe.wait_ge(mem_in, 16)
                    if callable(kind):
                        ins = kind(pe, b)
                    else:
                        ins = project(kind, w, b, memT)
                    ins.then_inc(pe_done, 1)

            @block.scalar
            def _(act):
                for n, (_, kind, evac) in enumerate(jobs):
                    act.wait_ge(pe_done, n + 1)
                    evac(act, PS[:, 2 * (n % 2):2 * (n % 2) + 2, :]).then_inc(ev_done, 1)

            @block.vector
            def _(dve):
                dve_side(dve)

            if pool_side:
                @block.gpsimd
                def _(pool):
                    pool_side(pool)

    def cols(w, *runs):
        v = w.rearrange("(k p) n -> p k n", p=P)
        return lambda slot: [(slot[:, :, s:s + n], v[:, :, c:c + n]) for s, c, n in runs]

    def copy_out(dst):
        return lambda act, ps: nc.scalar.activation(dst, ps, ACT.Copy)

    def flat2(view):
        return view.rearrange("p (c n) -> p c n", c=2)

    def position_rows(dve, pos_row, pos_col, row_hi, row_lo, col_hi, col_lo, tmp):
        for src, hi, lo, t in ((pos_row, row_hi, row_lo, tmp), (pos_col, col_hi, col_lo, tmp[:, 0:QB])):
            nc.vector.tensor_scalar(t, src, 16, None, ALU.arith_shift_right)
            dve.drain()
            nc.vector.tensor_copy(hi, t)
            dve.drain()
            nc.vector.tensor_scalar(t, src, 65535, None, ALU.bitwise_and)
            dve.drain()
            nc.vector.tensor_copy(lo, t)
            dve.drain()

    def bias_block(dve, rows, qb, k0, width, dsts, heads, scratch, loop):
        row_hi, row_lo, col_hi, col_lo = rows
        diff, bkt, hot = (s[:, 0:width] for s in scratch)
        ks = slice(k0, k0 + width)
        nc.vector.tensor_scalar(diff, row_hi[:, ks], col_hi[:, qb:qb + 1], 65536.0, ALU.subtract, ALU.mult)
        nc.vector.memset(bkt, 0.0)
        dve.drain()
        nc.vector.scalar_tensor_tensor(out=diff, in0=row_lo[:, ks], scalar=col_lo[:, qb:qb + 1], in1=diff,
                                       op0=ALU.subtract, op1=ALU.add)
        dve.drain()

        def raise_bucket(thr):
            nc.vector.scalar_tensor_tensor(out=bkt, in0=diff, scalar=thr, in1=bkt, op0=ALU.is_le, op1=ALU.add)
            dve.drain()

        def pick(col, entry):
            nc.vector.tensor_scalar(hot, bkt, col, -1.0, ALU.is_equal, ALU.mult)
            dve.drain()
            for d, e in zip(dsts, entry):
                nc.vector.scalar_tensor_tensor(out=d, in0=hot, scalar=e, in1=d, op0=ALU.mult, op1=ALU.add)
            dve.drain()

        for d in dsts:
            nc.vector.memset(d, 0.0)
        dve.drain()
        if loop:
            with dve.Fori(1, NB) as b:
                raise_bucket(consts[:, bass.ds(b + C_NTHR, 1)])
            with dve.Fori(0, NB) as b:
                pick(consts[:, bass.ds(b + C_BKT, 1)], [table[:, bass.ds(b * HEADS + h, 1)] for h in heads])
        else:
            for b in range(1, NB):
                raise_bucket(consts[:, C_NTHR + b:C_NTHR + b + 1])
            for b in range(NB):
                pick(consts[:, C_BKT + b:C_BKT + b + 1], [table[:, b * HEADS + h:b * HEADS + h + 1] for h in heads])

    def add_to(dst, mask):
        nc.vector.tensor_tensor(dst, dst, mask, ALU.add)

    TP, OB, FILL, FILL_GAP, PIECES, GATE_SPAN = (4, 6), 5, 7, 1, 4, 0.85

    def attention_queue(tag, tracks, loads=None):
        w_in = sem(tag + "w")
        gw_in = [sem(f"{tag}gw{k}") for k in range(len(tracks))]
        nw_in = [sem(f"{tag}nw{k}") for k in range(len(tracks))]

        def send(sp, what, done):
            for dst, src in what:
                sp.dma_start(dst, src).then_inc(done, 16)

        def projections(sp, i):
            if loads:
                send(sp, loads(i), w_in)

        def gates(sp, i):
            for k, tr in enumerate(tracks):
                send(sp, tr["gate_loads"](i), gw_in[k])

        def queries(sp, i):
            for k, tr in enumerate(tracks):
                if tr.get("next_w") is not None:
                    send(sp, tr["next_loads"](i), nw_in[k])

        def first(sp):
            projections(sp, 0)
            gates(sp, 0)
            queries(sp, 1)
        return dict(w_in=w_in, gw_in=gw_in, nw_in=nw_in, n_loads=len(loads(0)) if loads else 0,
                    projections=projections, gates=gates, queries=queries, first=first)

    def attention_stage(tag, tracks, queue, proj_jobs=(), setup_dve=None, general_dve=None, stage_pool=None, also_load=None):
        units, at, owner, fins, col = [], 0, [None] * 4, 0, 0
        for qb in range(QB):
            for tr in tracks:
                for hf in range(tr["halves"]):
                    ulist = tr["parts"](qb)
                    f_cols = {}
                    for kind in tr["kinds"]:
                        f_cols[kind] = col
                        col += 1
                    for un, plist in enumerate(ulist):
                        total = sum(n for _, n in plist)
                        banks = 2 if total > HALF else 1
                        if "bank_of" in tr:
                            at = tr["bank_of"](qb, hf)
                        if banks == 2 and at % 2:
                            at = (at + 1) % 4
                        prev = max((owner[b] for b in range(at, at + banks) if owner[b] is not None), default=None)
                        for b in range(at, at + banks):
                            owner[b] = len(units)
                        parts, off = [], 0
                        for kind, n in plist:
                            parts.append(dict(kind=kind, n=n, off=off, qb=qb, hf=hf, col=f_cols[kind],
                                              slot=tr["kinds"].index(kind)))
                            off += n
                        units.append(dict(tr=tr, qb=qb, hf=hf, parts=parts, bank=at, banks=banks, prev=prev, total=total,
                                          fin=fins if un == len(ulist) - 1 else None, f=fins, c0=col - len(tr["kinds"])))
                        at = (at + banks) % 4
                    fins += 1
        NU, NF, NCOL = len(units), fins, col
        g = 0
        for u in units:
            tiles = []
            for p in u["parts"]:
                for t in range(-(-p["n"] // P)):
                    tiles.append((p["off"] + t * P, min(P, p["n"] - t * P), p, t))
            u["tiles"] = tiles
            u["g0"], g = g, g - (-len(tiles) // 4)
            u["g1"] = g
        fin_unit = {u["fin"]: n for n, u in enumerate(units) if u["fin"] is not None}
        steps_n = NU + LOOK + OUT_LAG
        outs_at = {}
        for qb in range(QB):
            for k, tr in enumerate(tracks):
                last = max(n for n, u in enumerate(units) if u["qb"] == qb and u["tr"] is tr)
                outs_at.setdefault(last + LOOK + OUT_LAG, []).append((qb, k))
        order = []
        for s in range(steps_n):
            if 0 <= s - LOOK < NU:
                u = units[s - LOOK]
                order += [("p", s - LOOK, n) for n in range(u["g1"] - u["g0"])]
            order += [("o", qb, k) for qb, k in outs_at.get(s, [])]
        NE = len(order)
        index = {e: n for n, e in enumerate(order)}
        last_t = {v: index[("p", v, units[v]["g1"] - units[v]["g0"] - 1)] for v in range(NU)}
        biased = [n for n, u in enumerate(units) if u["tr"]["bias"]]
        last_of = [max([n for n in biased if units[n]["hf"] == hf], default=0) for hf in range(2)]
        gate_jobs = [(tr["gate_w"], c, k, "gate") for c in range(2) for k, tr in enumerate(tracks)]
        next_jobs = [(tr["next_w"], c, k, "next") for c in range(2) for k, tr in enumerate(tracks) if tr.get("next_w") is not None]
        NJF = len(gate_jobs) + len(next_jobs)
        NG = len(gate_jobs)

        slot_w = -(-max(max(u["total"] + (u["tr"].get("sink") is not None), *(c + P for c, _, _, _ in u["tiles"])) for u in units) // 8) * 8
        group_w = P * max(min(4, len(u["tiles"])) for u in units)
        widths = (3 * slot_w, 4 * group_w, 2 * len(tracks) * P, 192, NCOL, NCOL, NCOL, 2 * len(tracks) * HALF)
        region, gate_x = next((tr["bufs"], tr["gate_x"]) for tr in tracks if "bufs" in tr)
        assert sum(widths) <= region.shape[1], (tag, widths, region.shape)
        cut, views = 0, []
        for w in widths:
            views.append(region[:, cut:cut + w])
            cut += w
        p_sb, pt_sb, o_sb, pv_scr, negmax, rowsum, coef, sil = views
        p_sb = p_sb.rearrange("p (s n) -> p s n", s=3)
        pt_sb = pt_sb.rearrange("p (s n) -> p s n", s=4)
        o_sb = o_sb.rearrange("p (k s n) -> p k s n", k=len(tracks), s=2)
        sil = sil.rearrange("p (j n) -> p j n", j=NG)

        names = ("proj", "proj_act", "proj_dve", "qk", "max", "exp", "tr", "ev", "pv", "fin", "fill", "fill_exp", "fill_ev", "silu", "fill_high",
                 "setup", "bias", "sink")
        (proj_done, proj_act, proj_dve, qk_done, max_done, exp_done, tr_done, ev_done, pv_done, fin_done,
         fill_done, fill_exp, fill_ev, silu_done, fill_high, setup_done, bias_done, sink_set) = (sem(tag + n) for n in names)
        w_in, gw_in, nw_in, n_loads, projections, gates, queries = (
            queue[n] for n in ("w_in", "gw_in", "nw_in", "n_loads", "projections", "gates", "queries"))
        NJ = len(proj_jobs)
        act_jobs = [j for j in range(NJ) if proj_jobs[j][1]]
        dve_jobs = [j for j in range(NJ) if proj_jobs[j][2]]
        NA, ND = len(act_jobs), len(dve_jobs)
        sinks = next((tr["sink"] for tr in tracks if tr.get("sink")), None)
        SINK = 2 * P
        STEPS = 4

        def part_logits(u, p):
            n, b = p["n"], u["bank"]
            if u["tr"].get("sink"):
                return PS[:, b, SINK - n:SINK + 1]
            if u["banks"] == 2:
                return PS[:, b:b + 2, :].rearrange("p b n -> p (b n)")[:, p["off"]:p["off"] + n]
            return PS[:, b, p["off"]:p["off"] + n]

        sink_banks = {u["bank"]: u["hf"] for u in units if u["tr"].get("sink")}
        for u in units:
            assert not u["tr"].get("sink") or sink_banks[u["bank"]] == u["hf"]

        split_k = next((k for k, tr in enumerate(tracks) if tr.get("next_split")), None)
        split_highs, split_lows, split_needs = tracks[split_k]["next_split"] if split_k is not None else ([], [], [])
        NSP = len(split_highs)

        def body_jobs(last):
            return gate_jobs + ([] if last else next_jobs)

        LEAD = dict(mla={1: [(0, 0), (0, 1)], 2: [(0, 2)]}, swa={1: [(0, 0), (0, 1)], 2: [(0, 2)]},
                    nsa={0: [(0, 0)], 1: [(0, 1), (0, 2)], 2: [(0, 3)]})

        def uses_in(s):
            return (units[s - LOOK]["g1"] - units[s - LOOK]["g0"] if 0 <= s - LOOK < NU else 0) + len(outs_at.get(s, []))

        def fill_plan(last):
            jobs = body_jobs(last)
            first_at = {}
            e = 0
            for s in range(steps_n):
                first_at[s] = e
                e += uses_in(s)
            step_of = [n for n in range(steps_n) for _ in range(uses_in(n))]
            total = len(jobs) * KT
            plan_, at_e = [[] for _ in range(NE)], 0
            for x in range(sum(map(len, LEAD[tag].values())), total):
                job, m = divmod(x, KT)
                w, c, k, what = jobs[job]
                at_e = max(at_e, int(x * NE * (GATE_SPAN if last else 1)) // total)
                if m == 0 and job:
                    _, _, k, what = jobs[job - 1]
                    gap = NSP + 1 if what == "next" and k == split_k else FILL_GAP
                    at_e = max(at_e, first_at[step_of[at_last] + gap])
                if m == KT - 1 and what == "next":
                    lastq = max(n for n, u in enumerate(units) if u["tr"] is tracks[k] and u["qb"] < 4 * (c + 1))
                    at_e = max(at_e, first_at[lastq])
                plan_[at_e].append((job, m))
                at_last = at_e
            return plan_

        def fill_end_step(last):
            plan_, at_step, e = fill_plan(last), {}, 0
            for s in range(steps_n):
                for _ in range(uses_in(s)):
                    for job, m in plan_[e]:
                        if m == KT - 1:
                            at_step.setdefault(s, []).append(job)
                    e += 1
            return at_step

        def split_work(last):
            highs, lows = {}, {}
            for s, l in fill_end_step(last).items():
                for job in l:
                    _, c, k, what = body_jobs(last)[job]
                    if what == "next" and k == split_k:
                        for n in range(NSP):
                            highs.setdefault(min(s + n // 2, steps_n - 1), []).append((c, n))
                            lows.setdefault(min(s + 1 + n, steps_n - 1), []).append((c, n))
            return highs, lows

        def gate_work(last):
            ended = fill_end_step(last)
            end_of = {job: s for s, l in ended.items() for job in l if job < NG}
            todo, stands = {}, {}
            for job in range(NG):
                room = min(end_of[job + 1] - end_of[job] if job + 1 < NG else PIECES, PIECES)
                assert room > 0
                for p in range(PIECES):
                    s = min(end_of[job] + p * room // PIECES, steps_n - 1)
                    todo.setdefault(s, []).append(("piece", job, p))
                stands[job] = s
            for job in range(NG):
                _, c, k, _ = gate_jobs[job]
                ready = next(s for s, l in outs_at.items() if (4 * c + 3, k) in l)
                todo.setdefault(max(ready, stands[job]), []).append(("product", job, k))
            return todo

        def each_step(engine, body):
            with engine.Fori(0, STEPS - 1) as i:
                body(i, False)
            body(STEPS - 1, True)

        with nc.Block() as block:
            @block.sync
            def _(sp):
                if also_load:
                    also_load(sp)

                def again(i, with_queries):
                    if proj_jobs:
                        sp.wait_ge(proj_done, i * NJ + NJ)
                        projections(sp, i + 1)
                    sp.wait_ge(fill_done, i * NJF + NG)
                    gates(sp, i + 1)
                    if with_queries and next_jobs:
                        sp.wait_ge(fill_done, i * NJF + NJF)
                        queries(sp, i + 2)
                with sp.Fori(0, STEPS - 2) as i:
                    again(i, True)
                again(STEPS - 2, False)

            @block.tensor
            def _(pe):
                def step(i, last):
                    plan_, lead = fill_plan(last), LEAD[tag]
                    jobs = body_jobs(last)

                    def fill(e):
                        products(plan_[e])

                    def products(l):
                        for job, m in l:
                            w, c, k, what = jobs[job]
                            if m == 0:
                                tr = tracks[k]
                                if c == 0:
                                    nl = 16 * len(tr[what + "_loads"](0))
                                    pe.wait_ge((gw_in if what == "gate" else nw_in)[k], i * nl + nl)
                                pe.wait_ge(fill_ev, i * NJF + (job + 1))
                            ins = nc.tensor.matmul(PS[:, FILL, :], w[:, m, :], hT[:, m, c * HALF:(c + 1) * HALF], start=m == 0, stop=m == KT - 1)
                            if m == KT - 1:
                                ins.then_inc(fill_done, 1)

                    if proj_jobs:
                        pe.wait_ge(w_in, i * (16 * n_loads) + 16 * n_loads)
                        for j, (emit, _, _) in enumerate(proj_jobs):
                            if j >= 8:
                                pe.wait_ge(proj_act, i * NA + sum(x <= j - 8 for x in act_jobs))
                                if any(x <= j - 8 for x in dve_jobs):
                                    pe.wait_ge(proj_dve, i * ND + sum(x <= j - 8 for x in dve_jobs))
                            emit(j % 8, i).then_inc(proj_done, 1)
                        pe.wait_ge(proj_act, i * NA + NA)
                        if ND:
                            pe.wait_ge(proj_dve, i * ND + ND)
                    if sinks:
                        pe.wait_ge(sink_set, i + 1)
                    e = 0
                    for s in range(steps_n):
                        if s < NU:
                            u = units[s]
                            if u["prev"] is not None:
                                pe.wait_ge(exp_done, i * NU + (u["prev"] + 1))
                            for p in u["parts"]:
                                start = SINK - p["n"] if u["tr"].get("sink") else p["off"]
                                c = 0
                                while c < p["n"]:
                                    b, o = divmod(start + c, HALF)
                                    w = min(HALF - o, p["n"] - c)
                                    qs = u["tr"]["q_ap"](u["qb"], u["hf"])
                                    width = w + w % 2 if len(qs) > 1 else w
                                    for n, q in enumerate(qs):
                                        ins = nc.tensor.matmul(PS[:, u["bank"] + b, o:o + width], q, u["tr"]["k_ap"](p, i, c, width),
                                                               start=n == 0, stop=n == len(qs) - 1)
                                    c += w
                            ins.then_inc(qk_done, 1)
                        products(lead.get(s, []))
                        v = s - LOOK - 1
                        if 0 <= v < NU:
                            u = units[v]
                            pe.wait_ge(ev_done, i * NE + (last_t[v] + 1))
                            if u["f"] >= 1:
                                pe.wait_ge(fin_done, i * NF + u["f"])
                            hw = u["tr"]["head_w"]
                            for n, (c, w, p, t) in enumerate(u["tiles"]):
                                o = PS[:, OB, p["slot"] * hw:(p["slot"] + 1) * hw]
                                ins = nc.tensor.matmul(o, pt_sb[0:w, (u["g0"] + n // 4) % 4, (n % 4) * P:(n % 4 + 1) * P],
                                                       u["tr"]["v_ap"](p, t, i, w), start=t == 0, stop=(t + 1) * P >= p["n"])
                            ins.then_inc(pv_done, 1)
                        v = s - LOOK
                        if 0 <= v < NU:
                            u = units[v]
                            pe.wait_ge(exp_done, i * NU + (v + 1))
                            for gg in range(u["g1"] - u["g0"]):
                                if e >= 2:
                                    pe.wait_ge(ev_done, i * NE + (e - 1))
                                for n, (c, w, p, t) in enumerate(u["tiles"][4 * gg:4 * gg + 4]):
                                    ins = nc.tensor.transpose(PS[:, TP[e % 2], n * P:(n + 1) * P], p_sb[:, v % 3, c:c + P], ident)
                                ins.then_inc(tr_done, 1)
                                fill(e)
                                e += 1
                        for qb, k in outs_at.get(s, []):
                            f = max(u["f"] for u in units if u["qb"] == qb and u["tr"] is tracks[k])
                            pe.wait_ge(fin_done, i * NF + (f + 1))
                            pe.wait_ge(ev_done, i * NE + (e - 1))
                            nc.tensor.transpose(PS[:, TP[e % 2], 0:P], o_sb[:, k, qb % 2, :], ident).then_inc(tr_done, 1)
                            fill(e)
                            e += 1
                    pe.wait_ge(ev_done, i * NE + NE)
                    if proj_jobs:
                        pe.wait_ge(fill_ev, i * NJF + (len(jobs) + 1))
                each_step(pe, step)

            @block.scalar
            def _(act):
                def step(i, last):
                    jobs, ended, split_at = body_jobs(last), fill_end_step(last), split_work(last)
                    for j in act_jobs:
                        act.wait_ge(proj_done, i * NJ + (j + 1))
                        proj_jobs[j][1](j % 8).then_inc(proj_act, 1)
                    e = 0
                    for s in range(steps_n):
                        v = s - LOOK
                        if 0 <= v < NU:
                            u = units[v]
                            for gg in range(u["g1"] - u["g0"]):
                                act.wait_ge(tr_done, i * NE + (e + 1))
                                G = u["g0"] + gg
                                if G >= 4:
                                    old = next(n for n, x in enumerate(units) if x["g0"] <= G - 4 < x["g1"])
                                    act.wait_ge(pv_done, i * NU + (old + 1))
                                tiles = u["tiles"][4 * gg:4 * gg + 4]
                                nc.scalar.activation(pt_sb[:, G % 4, 0:len(tiles) * P], PS[:, TP[e % 2], 0:len(tiles) * P],
                                                     ACT.Copy).then_inc(ev_done, 1)
                                e += 1
                        for qb, k in outs_at.get(s, []):
                            act.wait_ge(tr_done, i * NE + (e + 1))
                            nc.scalar.activation(oT[:, bass.ds(i + tracks[k]["o_tile"], 1), qb * P:(qb + 1) * P].rearrange("p a n -> p (a n)"),
                                                 PS[:, TP[e % 2], 0:P], ACT.Copy).then_inc(ev_done, 1)
                            e += 1
                        if s < NU:
                            u = units[s]
                            act.wait_ge(max_done, i * NU + (s + 1))
                            if s >= 3:
                                act.wait_ge(tr_done, i * NE + (last_t[s - 3] + 1))
                            for p in u["parts"]:
                                w = p["n"] + (1 if u["tr"].get("sink") else 0)
                                ins = nc.scalar.activation(p_sb[:, s % 3, p["off"]:p["off"] + w], part_logits(u, p), ACT.Exp,
                                                           bias=negmax[:, p["col"]:p["col"] + 1], scale=-1.0,
                                                           accum_out=rowsum[:, p["col"]:p["col"] + 1])
                            ins.then_inc(exp_done, 1)
                        for job in ended.get(s, []):
                            w, c, k, what = jobs[job]
                            act.wait_ge(fill_done, i * NJF + (job + 1))
                            if what == "gate":
                                nc.scalar.activation(sil[:, job, :], PS[:, FILL, :], ACT.Exp, scale=-1.0).then_inc(fill_exp, 1)
                                if job:
                                    act.wait_ge(silu_done, i * NG + job)
                                nc.scalar.activation(gate_x, PS[:, FILL, :], ACT.Copy).then_inc(fill_ev, 1)
                            elif not tracks[k].get("next_split"):
                                tracks[k]["next_out"](PS[:, FILL, :], c).then_inc(fill_ev, 1)
                        for c, n in split_at[0].get(s, []):
                            split_highs[n](PS[:, FILL, :], c).then_inc(fill_high, 1)
                act.drain().then_inc(fill_ev, 1)
                each_step(act, step)

            if stage_pool:
                @block.gpsimd
                def _(pool):
                    if setup_dve:
                        pool.wait_ge(setup_done, 1)
                    gen = pool.value_load(gen_i[0:1, 0:1], min_val=0, max_val=1)

                    def stage(hf, i):
                        with pool.If(gen == 0):
                            stage_pool(hf, i)
                        with pool.Else():
                            pool.nop()
                        pool.drain().then_inc(bias_done, 1)

                    for hf in range(2):
                        pool.drain().then_inc(bias_done, 1)
                    with pool.Fori(0, STEPS - 1) as i:
                        for hf in range(2):
                            pool.wait_ge(max_done, i * NU + (last_of[hf] + 1))
                            nc.gpsimd.tensor_tensor(wait_marks[:, 99 - hf:100 - hf], ident[0:1, 0:1], ident[0:1, 0:1], ALU.add)
                            stage(hf, i + 1)

            @block.vector
            def _(dve):
                written = [0] * 3
                for v, u in enumerate(units):
                    end = max(c + P for c, _, _, _ in u["tiles"])
                    written[v % 3] = max(written[v % 3], u["total"])
                    if end > written[v % 3]:
                        nc.vector.memset(p_sb[:, v % 3, written[v % 3]:end], 0.0)
                        written[v % 3] = end
                if setup_dve:
                    setup_dve(dve).then_inc(setup_done, 1)
                gen = dve.value_load(gen_i[0:1, 0:1], min_val=0, max_val=1) if general_dve else None

                def step(i, last):
                    jobs, split_at, gate_jobs_at = body_jobs(last), split_work(last), gate_work(last)
                    for j in dve_jobs:
                        dve.wait_ge(proj_done, i * NJ + (j + 1))
                        proj_jobs[j][2](dve, j % 8).then_inc(proj_dve, 1)
                    if sinks:
                        pair = sinks(i)
                        for b, hf in sink_banks.items():
                            ins = nc.vector.tensor_copy(PS[:, b, SINK:SINK + 1], pair[:, hf:hf + 1])
                        ins.then_inc(sink_set, 1)
                    marks = 0
                    for s in range(steps_n):
                        if s < NU:
                            u = units[s]
                            if s in biased and not any(units[n]["qb"] == u["qb"] for n in biased if n < s):
                                with dve.If(gen == 1):
                                    general_dve(dve, u["qb"], i)
                                with dve.Else():
                                    dve.nop()
                            dve.wait_ge(qk_done, i * NU + (s + 1))
                            if u["tr"]["bias"]:
                                if not any(units[n]["hf"] == u["hf"] for n in biased if n < s):
                                    dve.wait_ge(bias_done, i * 2 + (u["hf"] + 1))
                                nc.vector.memset(wait_marks[:, marks:marks + 1], 0.0)
                                marks += 1
                            for p in u["parts"]:
                                lg, mn, n = part_logits(u, p), negmax[:, p["col"]:p["col"] + 1], p["n"]
                                if u["tr"]["bias"]:
                                    if p["kind"] == "win" and u["qb"] >= 4:
                                        nc.vector.tensor_tensor(lg[:, 0:P], lg[:, 0:P], winmask, ALU.add)
                                        dve.drain()
                                    ins = nc.vector.tensor_tensor_reduce(out=lg, in0=lg, in1=u["tr"]["bias"](p), scale=1.0,
                                                                         scalar=3e38, op0=ALU.add, op1=ALU.min, accum_out=mn)
                                    if p["kind"] == "cmp" and u["qb"] == 0:
                                        dve.drain()
                                        ins = nc.vector.tensor_scalar(mn, mn, 1e29, None, ALU.min)
                                else:
                                    if p["kind"] == "mla":
                                        nc.vector.tensor_tensor(lg[:, n - P:n], lg[:, n - P:n], causal, ALU.add)
                                        dve.drain()
                                    ins = nc.vector.tensor_reduce(out=mn, in_=lg, op=ALU.min, axis=AX.X)
                            ins.then_inc(max_done, 1)
                        v = s - LOOK
                        if 0 <= v < NU and units[v]["fin"] is not None:
                            u = units[v]
                            NK = len(u["tr"]["kinds"])
                            rs, cf = rowsum[:, u["c0"]:u["c0"] + NK], coef[:, u["c0"]:u["c0"] + NK]
                            dve.wait_ge(exp_done, i * NU + (v + 1))
                            if "cmp" in u["tr"]["kinds"] and u["qb"] == 0:
                                nc.vector.tensor_scalar(rs, rs, 1e-30, None, ALU.max)
                                dve.drain()
                            nc.vector.reciprocal(cf, rs)
                            if u["tr"].get("gate"):
                                dve.drain()
                                nc.vector.tensor_tensor(cf, cf, u["tr"]["gate"](u["qb"], u["hf"], i), ALU.mult)
                        v = s - LOOK - 1
                        if 0 <= v < NU and units[v]["fin"] is not None:
                            u = units[v]
                            NK, hw = len(u["tr"]["kinds"]), u["tr"]["head_w"]
                            k = next(n for n, t in enumerate(tracks) if t is u["tr"])
                            cf = coef[:, u["c0"]:u["c0"] + NK]
                            o_ps = PS[:, OB, 0:NK * hw]
                            dst = o_sb[:, k, u["qb"] % 2, u["hf"] * hw:(u["hf"] + 1) * hw]
                            if u["hf"] == 0 and u["qb"] >= 2:
                                dve.wait_ge(tr_done, i * NE + (index[("o", u["qb"] - 2, k)] + 1))
                                nc.vector.memset(wait_marks[:, 40:41], 0.0)
                            dve.drain()
                            dve.wait_ge(pv_done, i * NU + (v + 1))
                            if NK > 1:
                                nc.vector.tensor_tensor(pv_scr.rearrange("p (k d) -> p k d", k=NK),
                                                        o_ps.rearrange("p (k d) -> p k d", k=NK),
                                                        cf.unsqueeze(2).to_broadcast([P, NK, hw]), ALU.mult)
                                dve.drain()
                                nc.vector.tensor_reduce(out=dst, in_=pv_scr.rearrange("p (k d) -> p d k", k=NK),
                                                        op=ALU.add, axis=AX.X).then_inc(fin_done, 1)
                            else:
                                nc.vector.tensor_scalar(dst, o_ps, cf, None, ALU.mult).then_inc(fin_done, 1)
                        for c, n in split_at[1].get(s, []):
                            dve.wait_ge(fill_high, i * 2 * NSP + (c * NSP + split_needs[n]))
                            nc.vector.memset(wait_marks[:, 42:43], 0.0)
                            dve.drain()
                            ins = split_lows[n](PS[:, FILL, :], c)
                            if n == NSP - 1:
                                ins.then_inc(fill_ev, 1)
                        for what, job, p in gate_jobs_at.get(s, []):
                            sl = sil[:, job, :]
                            if what == "product":
                                _, c, k, _ = gate_jobs[job]
                                dve.wait_ge(ev_done, i * NE + (index[("o", 4 * c + 3, k)] + 1))
                                nc.vector.memset(wait_marks[:, 41:42], 0.0)
                                o = oT[:, bass.ds(i + tracks[k]["o_tile"], 1), c * HALF:(c + 1) * HALF].rearrange("p a n -> p (a n)")
                                dve.drain()
                                nc.vector.tensor_tensor(o, o, sl, ALU.mult)
                                continue
                            if p == 0:
                                dve.wait_ge(fill_exp, i * NG + (job + 1))
                                nc.vector.tensor_scalar(sl, sl, 1.0, None, ALU.add)
                                dve.drain()
                            cut = slice(p * (HALF // PIECES), (p + 1) * (HALF // PIECES))
                            nc.vector.reciprocal(sl[:, cut], sl[:, cut])
                            dve.drain()
                            if p == 0:
                                dve.wait_ge(fill_ev, i * NJF + (jobs.index(gate_jobs[job]) + 2))
                            ins = nc.vector.tensor_tensor(sl[:, cut], sl[:, cut], gate_x[:, cut], ALU.mult)
                            if p == PIECES - 1:
                                ins.then_inc(silu_done, 1)
                    dve.drain()

                each_step(dve, step)

    def output_queue(tag, w_out, tiles, row_runs, wo, n_first):
        wo_in = [sem(f"{tag}wo{k}") for k in range(tiles)]

        def send(sp, ks):
            for k in ks:
                for r0, r, n in row_runs(k):
                    sp.dma_start(wo[r0:r0 + n, k, :], w_out[r:r + n, :]).then_inc(wo_in[k], 16)
        return dict(wo_in=wo_in, first=lambda sp: send(sp, range(n_first)), rest=lambda sp: send(sp, range(n_first, tiles)))

    def output_stage(tag, w_out, tiles, row_runs, post_gain, x_src, out_dst, next_gain, wo, queue, also_load=None):
        xt_w, y_w, g_w, sq_w, xn_w = carve(2 * D, 2 * D, D, D, D)
        xt = xt_w.rearrange("p (s n) -> p s n", s=2)
        fused = next_gain is not None
        yt = y_w.rearrange("p (s n) -> p s n", s=2)
        stat, stat2 = small[:, 40:40 + QB], small[:, 50:50 + QB]
        wo_in = queue["wo_in"]
        x_in = [sem(f"{tag}x{p}") for p in range(2)]
        g_in, out_done = sem(tag + "g"), [sem(f"{tag}out{p}") for p in range(2)]
        y_done, sq_done, var_done, rt_done, scaled, res_done, sq2, var2, rt2, xn_done, tr_done, hev_act, hev_dve = (
            sem(tag + n) for n in ("y", "sq", "var", "rt", "scaled", "res", "sq2", "var2", "rt2", "xn", "tr", "hev_act", "hev_dve"))
        row = lambda t: PS[:, 2 * (t % 2):2 * (t % 2) + 2, :].rearrange("p b n -> p (b n)")
        with nc.Block() as block:
            @block.sync
            def _(sp):
                queue["rest"](sp)
                sp.dma_start(g_w, post_gain.partition_broadcast(P)).then_inc(g_in, 16)
                if also_load:
                    also_load(sp)
                for t in range(QB):
                    if t >= 2:
                        sp.wait_ge(res_done, t - 1)
                    sp.dma_start(xt[:, t % 2, :], x_src[t * P:(t + 1) * P, :]).then_inc(x_in[t % 2], 16)
                    if t >= 1:
                        sp.wait_ge(res_done, t)
                        sp.dma_start(out_dst[(t - 1) * P:t * P, :], yt[:, (t - 1) % 2, :]).then_inc(out_done[(t - 1) % 2], 16)
                sp.wait_ge(res_done, QB)
                sp.dma_start(out_dst[(QB - 1) * P:QB * P, :], yt[:, (QB - 1) % 2, :]).then_inc(out_done[(QB - 1) % 2], 16)
                for p in range(2):
                    sp.wait_ge(out_done[p], 16 * (QB // 2))

            @block.tensor
            def _(pe):
                def transposes(t):
                    pe.wait_ge(xn_done, t + 1)
                    if t >= 2:
                        pe.wait_ge(hev_act, t - 1)
                        pe.wait_ge(hev_dve, t - 1)
                    for k in range(KT):
                        ins = nc.tensor.transpose(PS[:, 4 + 2 * (t % 2) + k // 4, (k % 4) * P:(k % 4 + 1) * P], xn_w[:, k * P:(k + 1) * P], ident)
                    ins.then_inc(tr_done, 1)

                for t in range(QB):
                    if t >= 2:
                        pe.wait_ge(scaled, t - 1)
                        pe.wait_ge(sq_done, t - 1)
                    for k in range(tiles):
                        if t == 0:
                            pe.wait_ge(wo_in[k], 16 * len(row_runs(k)))
                        for c in range(2):
                            ins = nc.tensor.matmul(PS[:, 2 * (t % 2) + c, :], oT[:, k, t * P:(t + 1) * P], wo[:, k, c * HALF:(c + 1) * HALF],
                                                   start=k == 0, stop=k == tiles - 1)
                    ins.then_inc(y_done, 1)
                    if fused and t >= 1:
                        transposes(t - 1)
                if fused:
                    transposes(QB - 1)

            @block.scalar
            def _(act):
                def copy(t):
                    act.wait_ge(tr_done, t + 1)
                    for k in range(4):
                        ins = nc.scalar.activation(hT[:, k, t * P:(t + 1) * P], PS[:, 4 + 2 * (t % 2), k * P:(k + 1) * P], ACT.Copy,
                                                   scale=next_gain[:, k:k + 1])
                    ins.then_inc(hev_act, 1)

                for t in range(QB):
                    act.wait_ge(y_done, t + 1)
                    act.drain()
                    nc.scalar.activation(sq_w, row(t), ACT.Square, accum_out=stat[:, t:t + 1]).then_inc(sq_done, 1)
                    act.wait_ge(var_done, t + 1)
                    nc.scalar.activation(stat[:, t:t + 1], stat[:, t:t + 1], ACT.Sqrt).then_inc(rt_done, 1)
                    if fused:
                        act.wait_ge(res_done, t + 1)
                        act.drain()
                        nc.scalar.activation(sq_w, yt[:, t % 2, :], ACT.Square, accum_out=stat2[:, t:t + 1]).then_inc(sq2, 1)
                        act.wait_ge(var2, t + 1)
                        nc.scalar.activation(stat2[:, t:t + 1], stat2[:, t:t + 1], ACT.Sqrt).then_inc(rt2, 1)
                        if t >= 1:
                            copy(t - 1)
                if fused:
                    copy(QB - 1)

            @block.vector
            def _(dve):
                def mean_root(st, before, after):
                    nc.vector.tensor_scalar(st, st, 1.0 / D, EPS, ALU.mult, ALU.add)
                    dve.drain()
                    nc.vector.reciprocal(st, st).then_inc(before, 1)

                def copy(t):
                    dve.wait_ge(tr_done, t + 1)
                    nc.vector.tensor_tensor(hT[:, 4:8, t * P:(t + 1) * P], PS[:, 5 + 2 * (t % 2), :].rearrange("p (k n) -> p k n", k=4),
                                            next_gain[:, 4:8].unsqueeze(2).to_broadcast([P, 4, P]), ALU.mult).then_inc(hev_dve, 1)

                dve.wait_ge(g_in, 16)
                for t in range(QB):
                    st, y = stat[:, t:t + 1], yt[:, t % 2, :]
                    dve.wait_ge(sq_done, t + 1)
                    mean_root(st, var_done, rt_done)
                    dve.wait_ge(rt_done, t + 1)
                    if t >= 2:
                        dve.wait_ge(out_done[t % 2], 16 * (t // 2))
                    nc.vector.scalar_tensor_tensor(out=y, in0=row(t), scalar=st, in1=g_w, op0=ALU.mult, op1=ALU.mult).then_inc(scaled, 1)
                    dve.wait_ge(x_in[t % 2], 16 * (t // 2 + 1))
                    dve.drain()
                    nc.vector.tensor_tensor(y, y, xt[:, t % 2, :], ALU.add).then_inc(res_done, 1)
                    if fused:
                        st2 = stat2[:, t:t + 1]
                        dve.wait_ge(sq2, t + 1)
                        mean_root(st2, var2, rt2)
                        dve.wait_ge(rt2, t + 1)
                        if t >= 1:
                            dve.wait_ge(tr_done, t)
                        nc.vector.tensor_scalar(xn_w, y, st2, None, ALU.mult).then_inc(xn_done, 1)
                        if t >= 1:
                            copy(t - 1)
                if fused:
                    copy(QB - 1)

    ln = lambda kind, qb: dict(mla=P * (qb + 1), slc=P * (qb + 1), win=P * min(qb + 1, 5), swa=P * min(qb + 1, 2),
                               mem=MEM, cmp=min(NC, 8 * (qb + 1) - 1))[kind]

    def of_model(w, i, col, width=P):
        return w.rearrange("(k p) n -> p k n", p=P)[:, :, bass.ds(i + col, width)]

    def plain_loads(w, col, slot):
        return lambda i: [(slot, of_model(w, i * P, col))]

    def paired_loads(w, col, slot):
        return lambda i: [(slot[:, :, g * HD:(g + 1) * HD], of_model(w, i * HD, col + g * 4 * HD, HD)) for g in range(2)]

    def query_out(q, width):
        return lambda ps, c: nc.scalar.activation(q[:, c * HALF:(c + 1) * HALF], ps, ACT.Copy, scale=-(width ** -0.5))

    def first_queries(w, q, width, paired, col):
        runs = [(g * HD, col + g * 4 * HD, HD) for g in range(2)] if paired else [(0, col, P)]
        return (cols(w, *runs), "feat", lambda act, ps: nc.scalar.activation(flat2(q), ps, ACT.Copy, scale=-(width ** -0.5)))

    half_rows = lambda u: slice(u["hf"] * HD, (u["hf"] + 1) * HD)

    def memory_track(w, q_col, gate_col, q, kT, v, o_tile):
        return dict(
            kinds=["mem"], halves=1, head_w=P, o_tile=o_tile, bias=None, parts=lambda qb: [[("mem", MEM)]],
            q_ap=lambda qb, hf: [q[:, qb * P:(qb + 1) * P]],
            k_ap=lambda u, i, c, w_: kT[:, bass.ds(i * MEM, MEM)],
            v_ap=lambda u, t, i, w_: v[:, bass.ds(i * P + t * 512, P)],
            gate_w=wsl[:, 1], gate_loads=plain_loads(w, gate_col, wsl[:, 1]),
            next_w=wsl[:, 3], next_loads=plain_loads(w, q_col, wsl[:, 3]), next_out=query_out(q, P))

    def mem_jobs(w, kT, v):
        jobs = [(cols(w, (0, h * P, P)), "memk",
                 lambda act, ps, h=h: nc.scalar.activation(kT[:, h * MEM:(h + 1) * MEM], ps[:, 0, 0:MEM], ACT.Copy)) for h in range(4)]
        for h in range(4):
            jobs.append((cols(w, (0, 512 + h * P, P)), "memv",
                         lambda act, ps, h=h: nc.scalar.activation(v.rearrange("p (t n) -> p t n", t=2)[:, :, h * P:(h + 1) * P],
                                                                   ps[:, 0, 0:MEM].rearrange("p (t n) -> p t n", t=2), ACT.Copy)))
        return jobs


    def load_positions(sp, pos_row_i, done):
        with nc.allow_non_contiguous_dma(reason="positions, one per partition"):
            sp.dma_start(pos_row_i, a["positions"].partition_broadcast(P)).then_inc(done, 16)
            sp.dma_start(pos_col_i[:, :], a["positions"].rearrange("(b p) -> p b", p=P)).then_inc(done, 16)

    we = a["w_in_even"]

    top = 24500

    def at_top(width):
        nonlocal top
        top -= width
        return work[:, top:top + width]
    row_hi, row_lo = at_top(SEQ), at_top(SEQ)
    col_hi, col_lo = at_top(QB), at_top(QB)
    swk, swv, mk, mv, q_swa, q_mem = (at_top(SEQ) for _ in range(6))
    even_top = top
    rows = (row_hi, row_lo, col_hi, col_lo)
    cqn = work[:, 0:2 * SEQ].rearrange("p (k t) -> p k t", k=2)
    ckvn, kr = work[:, 2 * SEQ:3 * SEQ], work[:, 3 * SEQ:4 * SEQ]
    cs = work[:, 4 * SEQ:5 * SEQ]
    sinT = work[:, 5 * SEQ:6 * SEQ]
    pos_row_i = work[:, 6 * SEQ:7 * SEQ].bitcast(I32)
    itmp = work[:, 7 * SEQ:8 * SEQ].bitcast(I32)
    pos_f = work[:, 9 * SEQ:10 * SEQ]
    mbufs = work[:, 7 * SEQ:7 * SEQ + 6672]
    kslot = [work[:, 7 * SEQ + 6672 + s * SEQ:7 * SEQ + 6672 + (s + 1) * SEQ] for s in range(2)]
    assert 9 * SEQ + 6672 <= even_top
    sqs = oT[:, 0:3, :]
    rs_q, rs_kv = oT[:, 3, :], oT[:, 4, :]
    gq, gkv = gains[:, 16:18], gains[:, 18:19]
    nsink, nsink_pair = small[:, 200:208], small[:, 208:210]
    by_dist_w = oT_t[:, 5 * SEQ:8 * SEQ]
    by_dist = by_dist_w.rearrange("p (h n) -> p h n", h=HEADS)
    table_h = oT_t[:, 8 * SEQ:8 * SEQ + HEADS]
    table_in, dist_done, band_out, band_in = sem("p0table"), sem("p0dist"), sem("p0bandout"), sem("p0band")
    memT1_out = sem("n_m1_out")
    pos_in, latent_gain_in = sem("p0pos"), sem("p0lg")
    angles_done, trig_done, key_done, root_done = sem("p0angle"), sem("p0trig"), sem("p0key"), sem("p0root")
    QSC = -float((NOPE + ROPE) ** -0.5)

    def p0_loads(sp):
        load_positions(sp, pos_row_i, pos_in)
        sp.dma_start(table_h[0:NB, :], a["rel_bias_table"]).then_inc(table_in, 16)
        mla_queue["first"](sp)
        sp.dma_start(nsink, a["swa_sinks"].partition_broadcast(P)).then_inc(pos_in, 16)
        with nc.allow_non_contiguous_dma(reason="gains, one per partition"):
            sp.dma_start(gq, a["mla_q_norm"].rearrange("(k p) -> p k", p=P)).then_inc(latent_gain_in, 16)
            sp.dma_start(gkv, a["mla_kv_norm"].rearrange("(k p) -> p k", p=P)).then_inc(latent_gain_in, 16)

    def p0_vector(dve):
        dve.wait_ge(pos_in, 48)
        nc.vector.tensor_copy(pos_f, pos_row_i)
        position_rows(dve, pos_row_i, pos_col_i[:, :], row_hi, row_lo, col_hi, col_lo, itmp)
        TWO_PI = [6.28125, 0.0019350051879882812, 2 * math.pi - 6.28125 - 0.0019350051879882812]
        MAGIC = 1.5 * 2 ** 23
        turns = itmp.bitcast(F32)
        nc.vector.tensor_scalar(pos_f, pos_f, consts[:, C_INV:C_INV + 1], None, ALU.mult)
        dve.drain()
        nc.vector.tensor_scalar(turns, pos_f, 1 / (2 * math.pi), MAGIC, ALU.mult, ALU.add)
        dve.drain()
        nc.vector.tensor_scalar(turns, turns, MAGIC, None, ALU.subtract)
        dve.drain()
        for part in TWO_PI:
            nc.vector.scalar_tensor_tensor(out=pos_f, in0=turns, scalar=-float(part), in1=pos_f, op0=ALU.mult, op1=ALU.add)
            dve.drain()
        PI = 3.1415925
        nc.vector.tensor_scalar(sinT, pos_f, PI, -PI, ALU.min, ALU.max)
        nc.vector.tensor_scalar(turns, pos_f, math.pi / 2, None, ALU.is_gt)
        nc.vector.tensor_scalar(cs, pos_f, math.pi / 2, None, ALU.add)
        dve.drain()
        nc.vector.scalar_tensor_tensor(out=cs, in0=turns, scalar=-2 * math.pi, in1=cs, op0=ALU.mult, op1=ALU.add)
        dve.drain()
        nc.vector.tensor_scalar(cs, cs, PI, -PI, ALU.min, ALU.max).then_inc(angles_done, 1)
        d1, d2 = pos_f[:, 0:SEQ - 1], turns[:, 0:SEQ - 1]
        dve.drain()
        nc.vector.tensor_tensor(d1, row_hi[:, 1:SEQ], row_hi[:, 0:SEQ - 1], ALU.subtract)
        nc.vector.tensor_tensor(d2, row_lo[:, 1:SEQ], row_lo[:, 0:SEQ - 1], ALU.subtract)
        dve.drain()
        nc.vector.scalar_tensor_tensor(out=d1, in0=d1, scalar=65536.0, in1=d2, op0=ALU.mult, op1=ALU.add)
        dve.drain()
        nc.vector.tensor_scalar(d1, d1, 1.0, None, ALU.not_equal)
        dve.drain()
        nc.vector.tensor_reduce(out=gen_f, in_=d1, op=ALU.max, axis=AX.X)
        dve.drain()
        nc.vector.tensor_copy(gen_i[:, :], gen_f)
        dve.wait_ge(trig_done, 1)
        nc.vector.tensor_scalar(cs[96:128, :], sinT[96:128, :], consts[96:128, C_SIGN:C_SIGN + 1], None, ALU.mult)
        dve.wait_ge(key_done, 1)
        dve.drain()
        dve.wait_ge(memT1_out, 16)
        t1 = sinT[64:96, :]
        nc.vector.tensor_tensor(t1, kr[96:128, :], cs[96:128, :], ALU.mult)
        nc.vector.tensor_tensor(kr[64:96, :], kr[64:96, :], cs[64:96, :], ALU.mult)
        dve.drain()
        for s in range(2):
            nc.vector.tensor_tensor(kslot[s][64:96, :], kr[64:96, :], t1, ALU.add)
        nc.vector.tensor_scalar(cs[64:128, :], cs[64:128, :], QSC, None, ALU.mult)
        dve.wait_ge(root_done, 2)
        dve.wait_ge(latent_gain_in, 32)
        for rs in (rs_q, rs_kv):
            nc.vector.reciprocal(rs, rs)
        dve.drain()
        for k in range(2):
            nc.vector.scalar_tensor_tensor(out=cqn[:, k, :], in0=cqn[:, k, :], scalar=gq[:, k:k + 1], in1=rs_q, op0=ALU.mult, op1=ALU.mult)
        nc.vector.scalar_tensor_tensor(out=ckvn, in0=ckvn, scalar=gkv, in1=rs_kv, op0=ALU.mult, op1=ALU.mult)
        dve.wait_ge(band_in, 16 * HEADS)
        own = band[:, :].rearrange("p (h n) -> p h n", h=HEADS)[:, :, P:256]
        nc.vector.tensor_tensor(own, own, causal.unsqueeze(1).to_broadcast([P, HEADS, P]), ALU.add)

    def distance_bias(h):
        def go(pe, b):
            if h == 0:
                pe.wait_ge(table_in, 16)
            for n in range(2):
                ins = nc.tensor.matmul(PS[:, b + n, 0:SKEW], table_h[0:NB, h + n:h + n + 1].to_broadcast([NB, P]),
                                       consts[0:NB, C_HOT:C_HOT + SKEW], start=True, stop=True)
            return ins
        return go

    def distance_out(h):
        def go(act, ps):
            nc.scalar.activation(by_dist[:, h:h + 2, :], ps[:, :, 0:SKEW], ACT.Copy).then_inc(dist_done, 1)
            return act.drain()
        return go

    def p0_band(pool):
        pool.wait_ge(dist_done, 4)
        pool.dma_start(skew_dram[0:P * HEADS * SKEW].rearrange("(q n) -> q n", q=P), by_dist_w).then_inc(band_out, 16)
        pool.wait_ge(band_out, 16)
        skewed = skew_dram[P - 1:P - 1 + P * (HEADS * SKEW - 1)].rearrange("(q n) -> q n", q=P)[:, 0:HEADS * SKEW - P + 1]
        for h in range(HEADS):
            pool.dma_start(band[:, h * 256:(h + 1) * 256], skewed[:, h * SKEW:h * SKEW + 256]).then_inc(band_in, 16)

    def latent_out(dst, k):
        def go(act, ps):
            nc.scalar.activation(flat2(dst), ps, ACT.Copy)
            return nc.scalar.activation(flat2(sqs[:, k, :]), ps, ACT.Square)
        return go

    def square_sums(ks):
        def go(pe, b):
            for c in range(2):
                for k in ks:
                    ins = nc.tensor.matmul(PS[:, b + c, :], ones, sqs[:, k, c * HALF:(c + 1) * HALF], start=k == ks[0], stop=k == ks[-1])
            return ins
        return go

    def root_out(dst, n):
        def go(act, ps):
            nc.scalar.activation(flat2(dst), ps, ACT.Sqrt, scale=1.0 / n, bias=consts[:, C_EPS:C_EPS + 1]).then_inc(root_done, 1)
            return act.drain()
        return go

    def key_out(act, ps):
        nc.scalar.activation(flat2(kr), ps, ACT.Copy).then_inc(key_done, 1)
        return act.drain()

    def swv_out(act, ps):
        ins = nc.scalar.activation(flat2(swv), ps, ACT.Copy)
        act.wait_ge(angles_done, 1)
        nc.scalar.activation(cs, cs, ACT.Sin)
        nc.scalar.activation(sinT, sinT, ACT.Sin).then_inc(trig_done, 1)
        return act.drain()

    even_jobs = [(cols(we, (0, E_CQ + P * i, P)), "feat", latent_out(cqn[:, i, :], i)) for i in range(2)]
    even_jobs.append((cols(we, (0, E_CKV, P)), "feat", latent_out(ckvn, 2)))
    even_jobs.append((cols(we, (0, E_CKV, 64), (64, E_KR, 32), (96, E_KR + 16, 16), (112, E_KR, 16)), "feat", key_out))
    even_jobs += [(None, distance_bias(h), distance_out(h)) for h in range(0, HEADS, 2)]
    even_jobs.append((None, square_sums([0, 1]), root_out(rs_q, 256)))
    even_jobs.append((None, square_sums([2]), root_out(rs_kv, 128)))
    even_jobs.append((cols(we, (0, E_KSWA, P)), "feat", copy_out(flat2(swk))))
    even_jobs.append((cols(we, (0, E_VSWA, P)), "tok", swv_out))
    even_jobs.append(first_queries(we, q_swa, HD, True, E_QSWA))
    even_jobs.append(first_queries(we, q_mem, P, False, E_QMEM))
    queue = weight_queue("p0", even_jobs)
    norm_stage(mem_jobs(a["w_mem_kv"][0], mk, mv), memT1_out, queue)
    vs = kr
    qslot = [work[:, 5 * SEQ:6 * SEQ], work[:, 6 * SEQ:7 * SEQ]]
    wuq_w, wukv_w = oT_t[:, 9 * SEQ:9 * SEQ + 512], oT_t[:, 9 * SEQ + 512:9 * SEQ + 768]
    mla_gate_w = oT_t[:, 10 * SEQ:11 * SEQ].rearrange("p (k n) -> p k n", k=KT)
    rtmp, gate_x = oT_t[:, 11 * SEQ:11 * SEQ + HALF], oT_t[:, 11 * SEQ + HALF:12 * SEQ]
    wuq = wuq_w.rearrange("p (k h n) -> p k h n", k=2, h=2)
    wukv = wukv_w.rearrange("p (h n) -> p h n", h=2)
    uq = a["mla_w_uq"].rearrange("(k p) n -> p k n", p=P)

    def mla_loads(i):
        out = []
        for hf in range(2):
            c0 = i * (2 * 96) + hf * 96
            out.append((wuq[:, :, hf, 0:96], uq[:, :, bass.ds(c0, 96)]))
            out.append((wuq[:, :, hf, 96:112], uq[:, :, bass.ds(c0 + 80, 16)]))
            out.append((wuq[:, :, hf, 112:128], uq[:, :, bass.ds(c0 + 64, 16)]))
        out.append((wukv_w, a["mla_w_ukv"][:, bass.ds(i * 256, 256)]))
        return out

    def mla_q(hf, c):
        sl = slice(c * HALF, (c + 1) * HALF)

        def emit(b, i):
            for k in range(2):
                ins = nc.tensor.matmul(PS[:, b, :], wuq[:, k, hf, :], cqn[:, k, sl], start=k == 0, stop=k == 1)
            return ins

        def on_act(b):
            return nc.scalar.activation(qslot[hf][0:64, sl], PS[0:64, b, :], ACT.Copy, scale=QSC)

        def on_dve(dve, b):
            nc.vector.tensor_tensor(rtmp[64:96, :], PS[96:128, b, :], cs[96:128, sl], ALU.mult)
            nc.vector.tensor_tensor(qslot[hf][64:96, sl], PS[64:96, b, :], cs[64:96, sl], ALU.mult)
            dve.drain()
            ins = nc.vector.tensor_tensor(qslot[hf][64:96, sl], qslot[hf][64:96, sl], rtmp[64:96, :], ALU.add)
            dve.drain()
            return ins
        return emit, on_act, on_dve

    def mla_k(hf, c):
        sl = slice(c * HALF, (c + 1) * HALF)
        return (lambda b, i: nc.tensor.matmul(PS[0:64, b, :], wukv[:, hf, 0:64], ckvn[:, sl], start=True, stop=True),
                lambda b: nc.scalar.activation(kslot[hf][0:64, sl], PS[0:64, b, :], ACT.Copy), None)

    def mla_v(c):
        def emit(b, i):
            for t in range(4):
                ins = nc.tensor.matmul(PS[:, b, t * P:(t + 1) * P], ckvn[:, (4 * c + t) * P:(4 * c + t + 1) * P],
                                       wukv[:, :, 64:128], start=True, stop=True)
            return ins
        return emit, lambda b: nc.scalar.activation(vs[:, c * HALF:(c + 1) * HALF], PS[:, b, :], ACT.Copy), None

    mla_track = dict(
        kinds=["mla"], halves=2, head_w=HD, o_tile=0, bias=None, bufs=mbufs, gate_x=gate_x, parts=lambda qb: [[("mla", ln("mla", qb))]],
        q_ap=lambda qb, hf: [qslot[hf][0:96, qb * P:(qb + 1) * P]],
        k_ap=lambda u, i, c, w: kslot[u["hf"]][0:96, c:c + w],
        v_ap=lambda u, t, i, w: vs[:, t * P + u["hf"] * HD:t * P + (u["hf"] + 1) * HD],
        gate_w=mla_gate_w, gate_loads=plain_loads(we, E_GMLA, mla_gate_w))
    mla_queue = attention_queue("mla", [mla_track], mla_loads)
    project_stage("p0", even_jobs, queue, None, p0_vector, p0_loads, pool_side=p0_band)

    BW = 264
    swab, sc1, sc2, sc3 = carve(2 * BW, 256, 256, 256)
    used_w = 2 * BW + 768

    def swa_setup(dve):
        for hf in range(2):
            nc.vector.tensor_tensor(swab[:, hf * BW:hf * BW + P], band[:, hf * 1024:hf * 1024 + P], winmask, ALU.add)
            nc.vector.tensor_copy(swab[:, hf * BW + P:hf * BW + 256], band[:, hf * 1024 + P:hf * 1024 + 256])
            nc.vector.memset(swab[:, hf * BW + 256:hf * BW + 257], 0.0)
        nc.vector.tensor_scalar(nsink, nsink, -1.0, None, ALU.mult)
        return dve.drain()

    def swa_bias(u):
        o = u["hf"] * BW + 256
        return swab[:, o - u["n"]:o + 1]

    def swa_sink(i):
        for g in range(2):
            nc.vector.tensor_copy(nsink_pair[:, g:g + 1], nsink[:, bass.ds(i + 4 * g, 1)])
        nc.vector.drain()
        return nsink_pair

    def swa_stage(hf, i):
        nc.gpsimd.tensor_tensor(swab[:, hf * BW:hf * BW + P], band[:, bass.ds(i * 256 + hf * 1024, P)], winmask, ALU.add)
        nc.gpsimd.tensor_copy(swab[:, hf * BW + P:hf * BW + 256], band[:, bass.ds(i * 256 + (hf * 1024 + P), P)])

    def swa_general(dve, qb, i):
        w, k0 = (P, 0) if qb == 0 else (256, (qb - 1) * P)
        dst = [swab[:, hf * BW + 256 - w:hf * BW + 256] for hf in range(2)]
        bias_block(dve, rows, qb, k0, w, dst, [i, i + 4], (sc1, sc2, sc3), True)
        for d in dst:
            add_to(d[:, w - P:w], causal)
            if qb:
                add_to(d[:, 0:P], winmask)
        dve.drain()

    first_key = lambda u: max(0, u["qb"] - 1) * P
    swa_track = dict(
        kinds=["swa"], halves=2, head_w=HD, o_tile=4, bias=swa_bias, sink=swa_sink, bufs=work[:, used_w + HALF:9 * SEQ], gate_x=work[:, used_w:used_w + HALF],
        parts=lambda qb: [[("swa", ln("swa", qb))]], bank_of=lambda qb, hf: hf,
        q_ap=lambda qb, hf: [q_swa[hf * HD:(hf + 1) * HD, qb * P:(qb + 1) * P]],
        k_ap=lambda u, i, c, w: swk[half_rows(u), first_key(u):(u["qb"] + 1) * P],
        v_ap=lambda u, t, i, w: swv[:, first_key(u) + t * P + u["hf"] * HD:first_key(u) + t * P + (u["hf"] + 1) * HD],
        gate_w=wsl[:, 0], gate_loads=paired_loads(we, E_GSWA, wsl[:, 0]),
        next_w=wsl[:, 2], next_loads=paired_loads(we, E_QSWA, wsl[:, 2]), next_out=query_out(q_swa, HD))
    mem_track = memory_track(we, E_QMEM, E_GMEM, q_mem, mk, mv, 8)
    mem_track["bank_of"] = lambda qb, hf: 2 + qb % 2

    def even_rows(k):
        if 4 <= k < 8:
            return [(0, 512 + (k - 4) * HD, HD), (HD, 512 + (k - 4 + 4) * HD, HD)]
        return [(0, k * P, P)]

    even_wo = work[:, 9 * SEQ:21 * SEQ].rearrange("p (k n) -> p k n", k=12)
    assert 15 * SEQ <= even_top
    even_out = output_queue("o0", a["w_out_even"], 12, even_rows, even_wo, 6)
    swa_queue = attention_queue("swa", [swa_track, mem_track])
    attention_stage(
        "mla", [mla_track], mla_queue, also_load=swa_queue["first"],
        proj_jobs=[mla_q(hf, c) for hf in range(2) for c in range(2)] + [mla_k(hf, c) for hf in range(2) for c in range(2)] + [mla_v(c) for c in range(2)])

    attention_stage("swa", [swa_track, mem_track], swa_queue, setup_dve=swa_setup, general_dve=swa_general, stage_pool=swa_stage,
                    also_load=even_out["first"])

    wo_ = a["w_in_odd"]
    extra = oT_t[:, 8 * SEQ:12 * SEQ]
    mk, mv, row_hi, row_lo = (extra[:, n * SEQ:(n + 1) * SEQ] for n in range(4))
    work_held.close()
    work = sb("work_odd", 24500 - 8 * SEQ - 2 * 64)
    keys = sb("keys", 4 * SEQ + 2 * 64, F32R)
    x2_t, x2_held = lasting("token_pairs", 4 * SEQ)
    x2_held.close()
    q_all = sb("queries", 4 * SEQ, F32R)
    top = 24500 - 8 * SEQ - 2 * 64
    kslc, kwin = ([keys[:, (2 * n + g) * SEQ:(2 * n + g + 1) * SEQ] for g in range(2)] for n in range(2))
    kcT = [keys[:, 4 * SEQ + g * 64:4 * SEQ + (g + 1) * 64] for g in range(2)]
    q_high, q_low = ([q_all[:, (2 * n + hf) * SEQ:(2 * n + hf + 1) * SEQ] for hf in range(2)] for n in range(2))
    vslc, vwin, q_mem = (at_top(SEQ) for _ in range(3))
    vc = at_top(P)
    gl = at_top(QB * 24)
    col_hi, col_lo = at_top(QB), at_top(QB)
    rows = (row_hi, row_lo, col_hi, col_lo)
    odd_top = top
    kcmp, vcmp = work[:, 0:SEQ], work[:, SEQ:2 * SEQ]
    at = 2 * SEQ
    w2 = work[:, at:at + 256].rearrange("p (s m d) -> p s m d", s=2, m=2)
    pos2 = work[:, at + 256:at + 288].rearrange("p (s l) -> p s l", s=2)
    hid = work[:, at + 288:at + 800].rearrange("p (s m c) -> p s m c", s=2, m=2)
    w1 = work[:, 3 * SEQ:11 * SEQ].rearrange("p (s l n) -> p s l n", s=2, l=16)
    memT_w = work[:, 0:2 * SEQ]
    memT = memT_w.rearrange("p (k t) -> p k t", k=KT)
    x2 = x2_t[:, :].rearrange("p (s g t) -> p s g t", s=2, g=2)
    assert 11 * SEQ <= odd_top
    pos_row_i, itmp = oT[:, 0, :].bitcast(I32), oT[:, 1, :].bitcast(I32)
    xe = oT_t[:, 2 * SEQ:6 * SEQ].rearrange("p (s l c) -> p s l c", s=2, l=16)
    hb = oT_t[:, 6 * SEQ:6 * SEQ + 512].rearrange("p (s n) -> p s n", s=2)
    pos_in, mem_in, raw_done, x2_in = kept_sem("p1pos"), kept_sem("p1mem"), kept_sem("p1raw"), [kept_sem("p1x2k"), kept_sem("p1x2v")]
    w1_in, w2_in, xe_done = [kept_sem("p1w1k"), kept_sem("p1w1v")], kept_sem("p1w2"), kept_sem("p1xe")

    def p1_loads(sp):
        load_positions(sp, pos_row_i, pos_in)

    def p1_vector(dve):
        dve.wait_ge(pos_in, 32)
        position_rows(dve, pos_row_i, pos_col_i[:, :], row_hi, row_lo, col_hi, col_lo, itmp)
        dve.wait_ge(w2_in, 64)
        for s in range(2):
            dve.wait_ge(x2_in[s], 64)
            for g in range(2):
                for part in range(2):
                    src = x2[:, s, g, part * CMP_S:part * CMP_S + CMP_S * NC].rearrange("p (c l t) -> p l c t", c=NC, t=2)[:, :, :, 0]
                    ins = nc.vector.tensor_tensor(xe[:, s, part * 8:(part + 1) * 8, g * NC:(g + 1) * NC], src,
                                                  pos2[:, s, part * 8:(part + 1) * 8].unsqueeze(2).to_broadcast([P, 8, NC]), ALU.add)
            ins.then_inc(xe_done, 1)
        for g in range(2):
            nc.vector.tensor_scalar(kcT[g][:, NC:NC + 1], ones[:, 0:1], 0.0, None, ALU.mult)
        split_banks = [2 * (n % 2) for n, job in enumerate(jobs) if job[2] in splits]
        for n, low in enumerate(lows):
            dve.wait_ge(high_done, n + 1)
            low(PS[:, split_banks[n]:split_banks[n] + 2, :]).then_inc(low_done, 1)

    def p1_more_loads(pool):
        for s, n in enumerate("kv"):
            pool.dma_start(w2[:, s], a["cmp_w2_" + n].rearrange("(m p) d -> p m d", p=P)).then_inc(w2_in, 16)
            with nc.allow_non_contiguous_dma(reason="position embedding, one per partition"):
                pool.dma_start(pos2[:, s, :], a["cmp_pos_" + n].rearrange("(l a) d -> (a d) l", a=2)).then_inc(w2_in, 16)
        pool.wait_ge(raw_done, 1)
        for s, src in enumerate((kcmp, vcmp)):
            if s:
                pool.wait_ge(raw_done, 2)
            for g in range(2):
                rows_g = src[g * HD:(g + 1) * HD, :]
                pool.dma_start(x2[0:HD, s, g, :], rows_g).then_inc(x2_in[s], 16)
                pool.dma_start(x2[HD:P, s, g, 0:SEQ - 1], rows_g[:, 1:SEQ]).then_inc(x2_in[s], 16)
        for s, n in enumerate("kv"):
            pool.dma_start(w1[:, s], a["cmp_w1_" + n].rearrange("(l p) n -> p l n", p=P)).then_inc(w1_in[s], 16)
        for s in range(2):
            pool.wait_ge(x2_in[s], 64)
        pool.dma_start(memT_w, memT1_dram).then_inc(mem_in, 16)

    def rows_of(g):
        return slice(g * HD, (g + 1) * HD)

    def high_keys(ps, dst, cut):
        for g in range(2):
            for half in range(g + 1):
                ins = nc.scalar.activation(dst[g][rows_of(half), cut], ps[rows_of(g)], ACT.Copy)
        return ins

    def low_keys(ps, dst, cut):
        for g in range(2):
            ins = nc.vector.tensor_tensor(dst[g][HD:P, cut], ps[rows_of(g)], dst[g].bitcast(F32)[rows_of(g), cut], ALU.subtract)
        return ins

    NSC = -(HD ** -0.5)

    def high_query(ps, cut, n):
        hf, dst = n % 2, q_high[n % 2]
        if n < 2:
            return nc.scalar.activation(dst[rows_of(hf), cut], ps[rows_of(hf)], ACT.Copy, scale=NSC)
        if n == 2:
            nc.scalar.drain()
        return nc.scalar.activation(dst[rows_of(1 - hf), cut], dst[rows_of(hf), cut], ACT.Copy)

    def low_query(ps, cut, n):
        hf, dst = n % 2, q_low[n % 2]
        if n < 2:
            return nc.vector.scalar_tensor_tensor(out=dst[rows_of(hf), cut], in0=ps[rows_of(hf)], scalar=NSC,
                                                  in1=q_high[hf].bitcast(F32)[rows_of(hf), cut], op0=ALU.mult, op1=ALU.subtract)
        if n == 2:
            nc.vector.drain()
        return nc.vector.tensor_copy(dst[rows_of(1 - hf), cut], dst[rows_of(hf), cut])

    def high_queries(ps, cut):
        return [high_query(ps, cut, n) for n in range(4)][-1]

    def low_queries(ps, cut):
        return [low_query(ps, cut, n) for n in range(4)][-1]

    lows = []
    high_done, low_done = kept_sem("p1high"), kept_sem("p1low")

    def split_out(high, low, more=None):
        lows.append(low)
        n = len(lows)

        def go(act, ps):
            high(ps).then_inc(high_done, 1)
            act.wait_ge(low_done, n)
            return more(ps) if more else act.drain()
        return go

    def both(dst, fn):
        def go(ps):
            for c in range(2):
                ins = fn(ps[:, c, :], dst, slice(c * HALF, (c + 1) * HALF)) if dst else fn(ps[:, c, :], slice(c * HALF, (c + 1) * HALF))
            return ins
        return go

    def raw_out(dst):
        def go(act, ps):
            nc.scalar.activation(flat2(dst), ps, ACT.Copy).then_inc(raw_done, 1)
            return act.drain()
        return go

    def hidden(s):
        def go(pe, b):
            pe.wait_ge(xe_done, s + 1)
            pe.wait_ge(w1_in[s], 16)
            for l in range(16):
                ins = nc.tensor.matmul(PS[0:126, b, 0:256], xe[:, s, l, 0:126], w1[:, s, l, :], start=l == 0, stop=l == 15)
            return ins
        return go

    def hidden_out(s):
        return lambda act, ps: nc.scalar.activation(hb[0:126, s, :], ps[0:126, 0, 0:256], ACT.Silu)

    def hidden_turned(pe, b):
        for s in range(2):
            for m in range(2):
                ins = nc.tensor.transpose(PS[:, b, (2 * s + m) * P:(2 * s + m) * P + 126], hb[0:126, s, m * P:(m + 1) * P], ident[0:126, 0:126])
        return ins

    def turned_out(act, ps):
        return nc.scalar.activation(hid[:, :, :, 0:126], ps[:, 0, :].rearrange("p (s m c) -> p s m c", s=2, m=2)[:, :, :, 0:126], ACT.Copy)

    def compressed(pe, b):
        for g in range(2):
            for m in range(2):
                nc.tensor.matmul(PS[g * HD:(g + 1) * HD, b, 0:NC], w2[:, 0, m, :], hid[:, 0, m, g * NC:(g + 1) * NC], start=m == 0, stop=m == 1)
            for m in range(2):
                ins = nc.tensor.matmul(PS[0:NC, b + 1, g * HD:(g + 1) * HD], hid[:, 1, m, g * NC:(g + 1) * NC], w2[:, 1, m, :], start=m == 0, stop=m == 1)
        return ins

    def gl_out(act, ps):
        return nc.scalar.activation(gl.rearrange("p (c t n) -> p c t n", c=2, t=4),
                                    ps.rearrange("p c (t n) -> p c t n", t=4)[:, :, :, 0:24], ACT.Sigmoid)

    slc_out = split_out(both(kslc, high_keys), both(kslc, low_keys))
    win_out = split_out(both(kwin, high_keys), both(kwin, low_keys))
    q_out = split_out(both(None, high_queries), both(None, low_queries))
    kc_cut = slice(0, NC)
    compressed_out = split_out(lambda ps: high_keys(ps[:, 0, kc_cut], kcT, kc_cut), lambda ps: low_keys(ps[:, 0, kc_cut], kcT, kc_cut),
                               lambda ps: nc.scalar.activation(vc[0:NC, :], ps[0:NC, 1, 0:P], ACT.Copy))
    splits = (slc_out, win_out, q_out, compressed_out)
    odd_jobs = [
        (cols(wo_, (0, O_KCMP, P)), "feat", raw_out(kcmp)),
        (cols(wo_, (0, O_VCMP, P)), "feat", raw_out(vcmp)),
        (cols(wo_, (0, O_KSLC, P)), "feat", slc_out),
        (cols(wo_, (0, O_KWIN, P)), "feat", win_out),
        (cols(wo_, (0, O_VSLC, P)), "tok", copy_out(flat2(vslc))),
        (cols(wo_, (0, O_VWIN, P)), "tok", copy_out(flat2(vwin))),
        (cols(wo_, (0, O_GL, 24)), "tok24", gl_out)]
    query_job = (cols(wo_, *[(g * HD, O_Q + g * 4 * HD, HD) for g in range(2)]), "feat", q_out)
    hidden_jobs = [(None, hidden(s), hidden_out(s)) for s in range(2)]
    memory_jobs = mem_jobs(a["w_mem_kv"][1], mk, mv)
    jobs = (odd_jobs + hidden_jobs + [query_job, first_queries(wo_, q_mem, P, False, O_QMEM), (None, hidden_turned, turned_out)]
            + memory_jobs[:2] + [(None, compressed, compressed_out)] + memory_jobs[2:])
    queue = weight_queue("p1", jobs)
    output_stage("o0", a["w_out_even"], 12, even_rows, a["norm_post"][0], a["x"], x1_dram, gains[:, 32:40], even_wo, even_out, queue["first"])
    nc.clear_and_free_semaphores(layer_sems)
    nc.all_engine_barrier()
    layer_sems.clear()
    nb_w, nscr = work[:, 0:2 * SEQ], work[:, 2 * SEQ:2 * SEQ + 768]
    ngate_x, nbufs = work[:, 3 * SEQ:3 * SEQ + HALF], work[:, 3 * SEQ + HALF:11640]
    nb16 = nb_w.rearrange("p (n s) -> p n s", s=CMP_S)

    def nsa_setup(dve):
        for hf in range(2):
            nc.vector.tensor_copy(nb_w[:, hf * SEQ:(hf + 1) * SEQ - 256], band[:, hf * 1024:hf * 1024 + 1].to_broadcast([P, SEQ - 256]))
            nc.vector.tensor_copy(nb_w[:, (hf + 1) * SEQ - 256:(hf + 1) * SEQ], band[:, hf * 1024:hf * 1024 + 256])
        return dve.drain()

    def nsa_stage(hf, i):
        nc.gpsimd.tensor_copy(nb_w[:, hf * SEQ:(hf + 1) * SEQ - 256], band[:, bass.ds(i * 256 + hf * 1024, 1)].to_broadcast([P, SEQ - 256]))
        nc.gpsimd.tensor_copy(nb_w[:, (hf + 1) * SEQ - 256:(hf + 1) * SEQ], band[:, bass.ds(i * 256 + hf * 1024, 256)])

    def nsa_general(dve, qb, i):
        n = P * (qb + 1)
        dst = [nb_w[:, (hf + 1) * SEQ - n:(hf + 1) * SEQ] for hf in range(2)]
        for k0 in range(0, n, 256):
            w = min(256, n - k0)
            bias_block(dve, rows, qb, k0, w, [d[:, k0:k0 + w] for d in dst], [i, i + 4], [nscr[:, s * 256:(s + 1) * 256] for s in range(3)], True)
        for d in dst:
            add_to(d[:, n - P:n], causal)
        dve.drain()

    def nsa_bias(u):
        end = (u["hf"] + 1) * SEQ
        if u["kind"] == "cmp":
            o = (end - P * (u["qb"] + 1)) // CMP_S
            return nb16[:, o + 1:o + 1 + u["n"], CMP_S - 1]
        return nb_w[:, end - u["n"]:end]

    def nsa_k(u, i, c, w):
        c += {"win": P * (u["qb"] + 1) - u["n"]}.get(u["kind"], 0)
        return dict(cmp=kcT, slc=kslc, win=kwin)[u["kind"]][u["hf"]][:, c:c + w]

    def nsa_v(u, t, i, w):
        c = u["hf"] * HD
        if u["kind"] == "cmp":
            return vc[0:w, c:c + HD]
        if u["kind"] == "slc":
            return vslc[:, t * P + c:t * P + c + HD]
        t += u["qb"] + 1 - u["n"] // P
        return vwin[:, t * P + c:t * P + c + HD]

    of_half = lambda c: slice(c * HALF, (c + 1) * HALF)
    nsa_track = dict(
        kinds=["cmp", "slc", "win"], halves=2, head_w=HD, o_tile=0, bias=nsa_bias, bufs=nbufs, gate_x=ngate_x,
        parts=lambda qb: [[("slc", ln("slc", qb))], [("win", ln("win", qb)), ("cmp", ln("cmp", qb))]],
        gate=lambda qb, hf, i: gl[:, bass.ds(i * 3 + (qb * 24 + hf * 12), 3)],
        q_ap=lambda qb, hf: [q[hf][:, qb * P:(qb + 1) * P] for q in (q_high, q_low)], k_ap=nsa_k, v_ap=nsa_v,
        gate_w=wsl[:, 0], gate_loads=paired_loads(wo_, O_GNSA, wsl[:, 0]),
        next_w=wsl[:, 2], next_loads=paired_loads(wo_, O_Q, wsl[:, 2]),
        next_split=([lambda ps, c, n=n: high_query(ps, of_half(c), n) for n in range(4)],
                    [lambda ps, c, n=n: low_query(ps, of_half(c), n) for n in range(4)],
                    [2, 2, 2, 4]))
    nsa_tracks = [memory_track(wo_, O_QMEM, O_GMEM, q_mem, mk, mv, 4), nsa_track]

    def odd_rows(k):
        return [(0, k * HD, HD), (HD, (k + 4) * HD, HD)] if k < 4 else [(0, k * P, P)]

    def nsa_first(sp, done, used):
        sp.wait_ge(done, used[-1] + 1)
        nsa_queue["first"](sp)

    odd_wo = work[:, 7 * D:7 * D + 8 * SEQ].rearrange("p (k n) -> p k n", k=8)
    odd_out = output_queue("o1", a["w_out_odd"], 8, odd_rows, odd_wo, 0)
    nsa_queue = attention_queue("nsa", nsa_tracks)
    project_stage("p1", jobs, queue, memT, p1_vector, p1_loads, mem_in, p1_more_loads, nsa_first)
    attention_stage("nsa", nsa_tracks, nsa_queue, setup_dve=nsa_setup, general_dve=nsa_general, stage_pool=nsa_stage, also_load=odd_out["first"])
    output_stage("o1", a["w_out_odd"], 8, odd_rows, a["norm_post"][1], x1_dram, a["out"], None, odd_wo, odd_out)
    ctx.close()


SQUEEZE = ("x", "mem", "w_in_even", "mla_q_norm", "mla_kv_norm", "swa_sinks", "mla_w_uq", "mla_w_ukv", "w_out_even", "w_in_odd",
           "cmp_pos_k", "cmp_pos_v", "cmp_w1_k", "cmp_w2_k", "cmp_w1_v", "cmp_w2_v", "w_out_odd")


def build(nc, arrays):
    a = {}
    for name, v in arrays.items():
        ap = nc.dram_tensor(name, v.shape, mybir.dt.from_np(v.dtype), kind="ExternalInput").ap()
        a[name] = ap[0] if name in SQUEEZE else ap
    a["out"] = nc.dram_tensor("out", (1, SEQ, D), F32, kind="ExternalOutput").ap()[0]
    trunk(nc, a)


def kernel(**inputs):
    import concourse.bacc as bacc
    from concourse.bass_utils import run_bass_kernel_spmd

    nc = bacc.Bacc("TRN2", target_bir_lowering=False, num_devices=1)
    arrays = {name: np.ascontiguousarray(v) for name, v in inputs.items()}
    arrays["const_tables"] = make_constants()
    build(nc, arrays)
    return run_bass_kernel_spmd(nc, [arrays], core_ids=[0]).results[0]["out"]
```
